# Optimizing a Trainium2 kernel written in Bass

```python
import jax, jax.numpy as jnp
from jax import lax
import numpy as np
import math

D_MODEL = 1024
BATCH = 1
SEQ = 256
DEPTH = 4

N_MIXERS = 3
D_FF = 4 * D_MODEL
Q_BLOCK = 128
ROPE_BASE = 10000.0
EPS = 1e-6
NEG_INF = -1e30

MLA_HEADS = 8
MLA_Q_RANK = 256
MLA_KV_RANK = 128
MLA_NOPE = 128
MLA_ROPE = 64
MLA_V = 128

SB_HEADS = 16
SB_HEAD_DIM = D_MODEL // SB_HEADS

RET_HEADS = 4
RET_KEY_DIM = D_MODEL // RET_HEADS
RET_VAL_DIM = 2 * D_MODEL // RET_HEADS
RET_CHUNK = 128

N_MLA_LAYERS = (DEPTH + 2) // 3
N_SB_LAYERS = (DEPTH + 1) // 3
N_RET_LAYERS = DEPTH // 3


def rms_norm(x, g):
    xf = x.astype(jnp.float32)
    y = xf * lax.rsqrt(jnp.mean(xf * xf, axis=-1, keepdims=True) + EPS)
    return (y * g.astype(jnp.float32)).astype(x.dtype)

def modulate(x, shift, scale):
    return x * (1.0 + scale[:, None, :]) + shift[:, None, :]

def rope_tables(positions, dim):
    inv_freq = ROPE_BASE ** (-jnp.arange(0, dim, 2, dtype=jnp.float32) / dim)
    ang = positions.astype(jnp.float32)[..., None] * inv_freq
    return jnp.cos(ang)[:, :, None, :], jnp.sin(ang)[:, :, None, :]

def apply_rope(t, cos, sin):
    t1, t2 = jnp.split(t, 2, axis=-1)
    cos = cos.astype(t.dtype)
    sin = sin.astype(t.dtype)
    return jnp.concatenate([t1 * cos - t2 * sin, t2 * cos + t1 * sin], axis=-1)

def to_blocks(t, size):
    b, s, h, d = t.shape
    return t.reshape(b, s // size, size, h, d).transpose(1, 0, 2, 3, 4)

def from_blocks(t):
    nb, b, size, h, d = t.shape
    return t.transpose(1, 0, 2, 3, 4).reshape(b, nb * size, h, d)

def blocked_causal_softmax(q, k, v, scale):
    k_pos = jnp.arange(k.shape[1])
    qb = to_blocks(q, Q_BLOCK)

    def one_block(args):
        q_blk, b_idx = args
        q_pos = b_idx * Q_BLOCK + jnp.arange(Q_BLOCK)
        s = jnp.einsum('bqhd,bkhd->bhqk', q_blk, k).astype(jnp.float32) * scale
        s = jnp.where(k_pos[None, :] <= q_pos[:, None], s, NEG_INF)
        p = jax.nn.softmax(s, axis=-1).astype(v.dtype)
        return jnp.einsum('bhqk,bkhd->bqhd', p, v)

    o = lax.map(one_block, (qb, jnp.arange(qb.shape[0])))
    return from_blocks(o)

def mla_mixer(h, positions, w_in, q_norm, kv_norm, w_q_up, w_kv_up, w_out):
    b, s, _ = h.shape
    q_lat, kv_lat, k_pe = jnp.split(h @ w_in, [MLA_Q_RANK, MLA_Q_RANK + MLA_KV_RANK], axis=-1)
    cos, sin = rope_tables(positions, MLA_ROPE)
    q = (rms_norm(q_lat, q_norm) @ w_q_up).reshape(b, s, MLA_HEADS, MLA_NOPE + MLA_ROPE)
    q_nope, q_pe = jnp.split(q, [MLA_NOPE], axis=-1)
    q = jnp.concatenate([q_nope, apply_rope(q_pe, cos, sin)], axis=-1)
    kv = (rms_norm(kv_lat, kv_norm) @ w_kv_up).reshape(b, s, MLA_HEADS, MLA_NOPE + MLA_V)
    k_nope, v = jnp.split(kv, [MLA_NOPE], axis=-1)
    k_pe = apply_rope(k_pe[:, :, None, :], cos, sin)
    k = jnp.concatenate([k_nope, jnp.broadcast_to(k_pe, (b, s, MLA_HEADS, MLA_ROPE))], axis=-1)
    o = blocked_causal_softmax(q, k, v, (MLA_NOPE + MLA_ROPE) ** -0.5)
    return o.reshape(b, s, MLA_HEADS * MLA_V) @ w_out

def stick_breaking_mixer(h, w_in, w_out):
    b, s, _ = h.shape
    q, k, v = jnp.split(h @ w_in, 3, axis=-1)
    q = q.reshape(b, s, SB_HEADS, SB_HEAD_DIM)
    k = k.reshape(b, s, SB_HEADS, SB_HEAD_DIM)
    v = v.reshape(b, s, SB_HEADS, SB_HEAD_DIM)
    scale = SB_HEAD_DIM ** -0.5
    k_pos = jnp.arange(s)
    qb = to_blocks(q, Q_BLOCK)

    def one_block(args):
        q_blk, b_idx = args
        q_pos = b_idx * Q_BLOCK + jnp.arange(Q_BLOCK)
        z = jnp.einsum('bqhd,bkhd->bhqk', q_blk, k).astype(jnp.float32) * scale
        strict = k_pos[None, :] < q_pos[:, None]
        log_1m = jnp.where(strict, jax.nn.log_sigmoid(-z), 0.0)
        suffix = lax.cumsum(log_1m, axis=3, reverse=True) - log_1m
        a = jnp.where(strict, jnp.exp(jax.nn.log_sigmoid(z) + suffix), 0.0).astype(v.dtype)
        return jnp.einsum('bhqk,bkhd->bqhd', a, v)

    o = from_blocks(lax.map(one_block, (qb, jnp.arange(qb.shape[0]))))
    return o.reshape(b, s, SB_HEADS * SB_HEAD_DIM) @ w_out

def retention_mixer(h, positions, w_in, gn_g, w_out):
    b, s, _ = h.shape
    hk = RET_HEADS * RET_KEY_DIM
    hv = RET_HEADS * RET_VAL_DIM
    q, k, v, g = jnp.split(h @ w_in, [hk, 2 * hk, 2 * hk + hv], axis=-1)
    cos, sin = rope_tables(positions, RET_KEY_DIM)
    q = apply_rope(q.reshape(b, s, RET_HEADS, RET_KEY_DIM), cos, sin).astype(jnp.float32)
    k = apply_rope(k.reshape(b, s, RET_HEADS, RET_KEY_DIM), cos, sin).astype(jnp.float32) * (RET_KEY_DIM ** -0.5)
    v = v.reshape(b, s, RET_HEADS, RET_VAL_DIM).astype(jnp.float32)

    log_gamma = jnp.log(1.0 - 2.0 ** (-5.0 - jnp.arange(RET_HEADS, dtype=jnp.float32)))
    idx = jnp.arange(RET_CHUNK, dtype=jnp.float32)
    diff = idx[:, None] - idx[None, :]
    decay = jnp.where(diff[None] >= 0, jnp.exp(jnp.maximum(diff, 0.0)[None] * log_gamma[:, None, None]), 0.0)
    xi = jnp.exp((idx[:, None] + 1.0) * log_gamma[None, :])
    zeta = jnp.exp((RET_CHUNK - 1.0 - idx)[:, None] * log_gamma[None, :])
    g_chunk = jnp.exp(RET_CHUNK * log_gamma)

    def step(state, inp):
        qc, kc, vc = inp
        sc = jnp.einsum('bihd,bjhd->bhij', qc, kc) * decay[None]
        inner = jnp.einsum('bhij,bjhv->bihv', sc, vc)
        cross = jnp.einsum('bihd,bhdv->bihv', qc, state) * xi[None, :, :, None]
        state = state * g_chunk[None, :, None, None] + jnp.einsum('bjhd,bjhv->bhdv', kc * zeta[None, :, :, None], vc)
        return state, inner + cross

    state0 = jnp.zeros((b, RET_HEADS, RET_KEY_DIM, RET_VAL_DIM), jnp.float32)
    _, o = lax.scan(step, state0, (to_blocks(q, RET_CHUNK), to_blocks(k, RET_CHUNK), to_blocks(v, RET_CHUNK)))
    o = from_blocks(o)
    o = o * lax.rsqrt(jnp.mean(o * o, axis=-1, keepdims=True) + EPS)
    o = o.reshape(b, s, hv) * gn_g.astype(jnp.float32)
    o = (jax.nn.silu(g.astype(jnp.float32)) * o).astype(h.dtype)
    return o @ w_out

def first_inputs(seed: int = 0) -> dict:
    key = jax.random.key(seed)
    ks = jax.random.split(key, 24)

    def dense(k, shape, fan_in, gain=1.0):
        return jax.random.normal(k, shape, jnp.float32) * (gain * fan_in ** -0.5)

    def gains(k, shape):
        return 1.0 + 0.05 * jax.random.normal(k, shape, jnp.float32)

    hk = RET_HEADS * RET_KEY_DIM
    hv = RET_HEADS * RET_VAL_DIM
    return {
        "x": jax.random.normal(ks[0], (BATCH, SEQ, D_MODEL), jnp.float32),
        "c": jax.random.normal(ks[1], (BATCH, D_MODEL), jnp.float32),
        "positions": jnp.broadcast_to(jnp.arange(SEQ, dtype=jnp.int32), (BATCH, SEQ)),
        "ada_w": dense(ks[2], (DEPTH, D_MODEL, 6 * D_MODEL), D_MODEL, 0.5),
        "ada_b": 0.01 * jax.random.normal(ks[3], (DEPTH, 6 * D_MODEL), jnp.float32),
        "norm_g": gains(ks[4], (DEPTH, 4, D_MODEL)),
        "ffn_w1": dense(ks[5], (DEPTH, D_MODEL, D_FF), D_MODEL),
        "ffn_w2": dense(ks[6], (DEPTH, D_FF, D_MODEL), D_FF),
        "mla_w_in": dense(ks[7], (N_MLA_LAYERS, D_MODEL, MLA_Q_RANK + MLA_KV_RANK + MLA_ROPE), D_MODEL),
        "mla_q_norm": gains(ks[8], (N_MLA_LAYERS, MLA_Q_RANK)),
        "mla_kv_norm": gains(ks[9], (N_MLA_LAYERS, MLA_KV_RANK)),
        "mla_w_q_up": dense(ks[10], (N_MLA_LAYERS, MLA_Q_RANK, MLA_HEADS * (MLA_NOPE + MLA_ROPE)), MLA_Q_RANK),
        "mla_w_kv_up": dense(ks[11], (N_MLA_LAYERS, MLA_KV_RANK, MLA_HEADS * (MLA_NOPE + MLA_V)), MLA_KV_RANK),
        "mla_w_out": dense(ks[12], (N_MLA_LAYERS, MLA_HEADS * MLA_V, D_MODEL), MLA_HEADS * MLA_V),
        "sb_w_in": dense(ks[13], (N_SB_LAYERS, D_MODEL, 3 * SB_HEADS * SB_HEAD_DIM), D_MODEL),
        "sb_w_out": dense(ks[14], (N_SB_LAYERS, SB_HEADS * SB_HEAD_DIM, D_MODEL), SB_HEADS * SB_HEAD_DIM),
        "ret_w_in": dense(ks[15], (N_RET_LAYERS, D_MODEL, 2 * hk + 2 * hv), D_MODEL),
        "ret_gn_g": gains(ks[16], (N_RET_LAYERS, hv)),
        "ret_w_out": dense(ks[17], (N_RET_LAYERS, hv, D_MODEL), hv),
    }

def first_block(x, c, positions, ada_w, ada_b, norm_g, ffn_w1, ffn_w2,
              mla_w_in, mla_q_norm, mla_kv_norm, mla_w_q_up, mla_w_kv_up, mla_w_out,
              sb_w_in, sb_w_out, ret_w_in, ret_gn_g, ret_w_out):
    cond = jax.nn.silu(c)
    for i in range(DEPTH):
        mod = cond @ ada_w[i] + ada_b[i]
        sh_a, sc_a, g_a, sh_f, sc_f, g_f = jnp.split(mod, 6, axis=-1)

        h = modulate(rms_norm(x, norm_g[i, 0]), sh_a, sc_a)
        kind, j = i % N_MIXERS, i // N_MIXERS
        if kind == 0:
            y = mla_mixer(h, positions, mla_w_in[j], mla_q_norm[j], mla_kv_norm[j],
                          mla_w_q_up[j], mla_w_kv_up[j], mla_w_out[j])
        elif kind == 1:
            y = stick_breaking_mixer(h, sb_w_in[j], sb_w_out[j])
        else:
            y = retention_mixer(h, positions, ret_w_in[j], ret_gn_g[j], ret_w_out[j])
        x = x + g_a[:, None, :] * rms_norm(y, norm_g[i, 1])

        h = modulate(rms_norm(x, norm_g[i, 2]), sh_f, sc_f)
        y = jnp.square(jax.nn.relu(h @ ffn_w1[i])) @ ffn_w2[i]
        x = x + g_f[:, None, :] * rms_norm(y, norm_g[i, 3])
    return x


DEPTH_2 = 2

GRID_W = 64
CTX_LEN = 256
HEAD_DIM = 128
FNET_GROUPS = 4
FNET_GROUP_DIM = 64
FNET_WIDTH = FNET_GROUPS * FNET_GROUP_DIM
GQA_Q_HEADS = 6
GQA_KV_HEADS = 2
GQA_GROUP = GQA_Q_HEADS // GQA_KV_HEADS
AB_IN_WIDTH = FNET_WIDTH + (GQA_Q_HEADS + 2 * GQA_KV_HEADS) * HEAD_DIM
AB_OUT_WIDTH = FNET_WIDTH + GQA_Q_HEADS * HEAD_DIM
ROPE_THETA = 10000.0
NA_HEADS = 8
NA_WIDTH = NA_HEADS * HEAD_DIM
NA_KH = 8
NA_KW = 16
NA_ROWS_PER_BLOCK = Q_BLOCK // GRID_W
NEG_INF_2 = -1e30
N_EXPERTS = 64
TOP_K = 8
EXPERT_DIM = 256
SHARED_DIM = 256
ROUTE_SCALE = 2.5
MOE_BLOCK = 128
DN_ALPHA = (2 * DEPTH_2) ** 0.25
DN_BETA = (8 * DEPTH_2) ** -0.25
N_EVEN = (DEPTH_2 + 1) // 2
N_ODD = DEPTH_2 // 2
LN_EPS = 1e-6
RMS_EPS = 1e-6


def layer_norm(x, g, b):
    xf = x.astype(jnp.float32)
    mu = xf.mean(-1, keepdims=True)
    xc = xf - mu
    var = (xc * xc).mean(-1, keepdims=True)
    return (xc * lax.rsqrt(var + LN_EPS) * g + b).astype(x.dtype)

def rms_norm_2(x, g):
    xf = x.astype(jnp.float32)
    return (xf * lax.rsqrt((xf * xf).mean(-1, keepdims=True) + RMS_EPS) * g).astype(x.dtype)

def axial_rope(x):
    n_tok = x.shape[1]
    t = jnp.arange(n_tok)
    half = HEAD_DIM // 2
    nf = half // 2
    inv = ROPE_THETA ** (-(2.0 / half) * jnp.arange(nf, dtype=jnp.float32))

    def rot(v, pos):
        ang = pos.astype(jnp.float32)[:, None] * inv
        cos = jnp.cos(ang)[:, None, :]
        sin = jnp.sin(ang)[:, None, :]
        v1, v2 = v[..., :nf], v[..., nf:]
        return jnp.concatenate([v1 * cos - v2 * sin, v1 * sin + v2 * cos], axis=-1)

    xf = x.astype(jnp.float32)
    out = jnp.concatenate([rot(xf[..., :half], t // GRID_W), rot(xf[..., half:], t % GRID_W)], axis=-1)
    return out.astype(x.dtype)

def gqa_attend(q, k, v):
    s = jnp.einsum("bqkgd,bnkd->bkgqn", q, k).astype(jnp.float32) * HEAD_DIM ** -0.5
    p = jax.nn.softmax(s, axis=-1).astype(v.dtype)
    return jnp.einsum("bkgqn,bnkd->bqkgd", p, v)

def fourier_mix(f, w_fnet):
    bsz, n_tok, _ = f.shape
    fg = f.reshape(bsz, n_tok, FNET_GROUPS, FNET_GROUP_DIM).astype(jnp.float32)
    fr = jnp.fft.fft2(fg, axes=(1, 3), norm="ortho").real.astype(f.dtype)
    return jnp.einsum("blgc,gcd->blgd", fr, w_fnet).reshape(bsz, n_tok, FNET_WIDTH)

def mixer_ab(h_lat, h_ctx, w_in, w_fnet, q_gain, k_gain, w_out, want_ctx):
    bsz, n_lat, _ = h_lat.shape
    n_ctx = h_ctx.shape[1]
    nq = GQA_Q_HEADS * HEAD_DIM
    nkv = GQA_KV_HEADS * HEAD_DIM
    cuts = [FNET_WIDTH, FNET_WIDTH + nq, FNET_WIDTH + nq + nkv]
    f, q, k, v = jnp.split(h_lat @ w_in, cuts, axis=-1)
    q = axial_rope(rms_norm_2(q.reshape(bsz, n_lat, GQA_Q_HEADS, HEAD_DIM), q_gain))
    k = axial_rope(rms_norm_2(k.reshape(bsz, n_lat, GQA_KV_HEADS, HEAD_DIM), k_gain))
    v = v.reshape(bsz, n_lat, GQA_KV_HEADS, HEAD_DIM)
    if want_ctx:
        fc, qc, kc, vc = jnp.split(h_ctx @ w_in, cuts, axis=-1)
    else:
        kc, vc = jnp.split(h_ctx @ w_in[:, cuts[1]:], [nkv], axis=-1)
    kc = rms_norm_2(kc.reshape(bsz, n_ctx, GQA_KV_HEADS, HEAD_DIM), k_gain)
    vc = vc.reshape(bsz, n_ctx, GQA_KV_HEADS, HEAD_DIM)
    k_all = jnp.concatenate([k, kc], axis=1)
    v_all = jnp.concatenate([v, vc], axis=1)
    nb = n_lat // Q_BLOCK
    qb = q.reshape(bsz, nb, Q_BLOCK, GQA_KV_HEADS, GQA_GROUP, HEAD_DIM).swapaxes(0, 1)
    o = lax.map(lambda qi: gqa_attend(qi, k_all, v_all), qb)
    o = o.swapaxes(0, 1).reshape(bsz, n_lat, nq)
    y_lat = jnp.concatenate([fourier_mix(f, w_fnet), o], axis=-1) @ w_out
    if not want_ctx:
        return y_lat, None
    qc = rms_norm_2(qc.reshape(bsz, n_ctx, GQA_Q_HEADS, HEAD_DIM), q_gain)
    qc = qc.reshape(bsz, n_ctx, GQA_KV_HEADS, GQA_GROUP, HEAD_DIM)
    oc = gqa_attend(qc, kc, vc).reshape(bsz, n_ctx, nq)
    y_ctx = jnp.concatenate([fourier_mix(fc, w_fnet), oc], axis=-1) @ w_out
    return y_lat, y_ctx

def mixer_na(h_lat, h_ctx, w_in, rpb, w_out, want_ctx):
    bsz, n_lat, _ = h_lat.shape
    n_ctx = h_ctx.shape[1]
    rows = n_lat // GRID_W
    kh = min(NA_KH, rows)
    kw = min(NA_KW, GRID_W)
    qr = NA_ROWS_PER_BLOCK
    nbr = min(qr + kh - 1, rows)
    nblk = rows // qr
    scale = HEAD_DIM ** -0.5
    q, k, v = jnp.split(h_lat @ w_in, 3, axis=-1)
    if want_ctx:
        qc, kc, vc = jnp.split(h_ctx @ w_in, 3, axis=-1)
    else:
        kc, vc = jnp.split(h_ctx @ w_in[:, NA_WIDTH:], 2, axis=-1)
    kc = kc.reshape(bsz, n_ctx, NA_HEADS, HEAD_DIM)
    vc = vc.reshape(bsz, n_ctx, NA_HEADS, HEAD_DIM)
    k_grid = k.reshape(bsz, rows, GRID_W, NA_HEADS, HEAD_DIM)
    v_grid = v.reshape(bsz, rows, GRID_W, NA_HEADS, HEAD_DIM)
    q_blocks = q.reshape(bsz, nblk, qr * GRID_W, NA_HEADS, HEAD_DIM).swapaxes(0, 1)
    col = jnp.arange(GRID_W)
    col_start = jnp.clip(col - kw // 2, 0, GRID_W - kw)
    in_col = (col[None, :] >= col_start[:, None]) & (col[None, :] < col_start[:, None] + kw)
    dc = jnp.clip(col[None, :] - col[:, None] + NA_KW - 1, 0, 2 * NA_KW - 2)

    def block(args):
        i, qi = args
        qrow = i * qr + jnp.arange(qr)
        rstart = jnp.clip(qrow - kh // 2, 0, rows - kh)
        bs = jnp.minimum(rstart[0], rows - nbr)
        krow = bs + jnp.arange(nbr)
        kb = lax.dynamic_slice_in_dim(k_grid, bs, nbr, axis=1).reshape(bsz, nbr * GRID_W, NA_HEADS, HEAD_DIM)
        vb = lax.dynamic_slice_in_dim(v_grid, bs, nbr, axis=1).reshape(bsz, nbr * GRID_W, NA_HEADS, HEAD_DIM)
        in_row = (krow[None, :] >= rstart[:, None]) & (krow[None, :] < rstart[:, None] + kh)
        dr = jnp.clip(krow[None, :] - qrow[:, None] + NA_KH - 1, 0, 2 * NA_KH - 2)
        mask = (in_row[:, None, :, None] & in_col[None, :, None, :]).reshape(qr * GRID_W, nbr * GRID_W)
        bias = rpb[:, dr[:, None, :, None], dc[None, :, None, :]].reshape(NA_HEADS, qr * GRID_W, nbr * GRID_W)
        s_loc = jnp.einsum("bqhd,bnhd->bhqn", qi, kb).astype(jnp.float32) * scale + bias.astype(jnp.float32)
        s_loc = jnp.where(mask, s_loc, NEG_INF_2)
        s_ctx = jnp.einsum("bqhd,bnhd->bhqn", qi, kc).astype(jnp.float32) * scale
        p = jax.nn.softmax(jnp.concatenate([s_loc, s_ctx], axis=-1), axis=-1).astype(vb.dtype)
        n_loc = nbr * GRID_W
        return (jnp.einsum("bhqn,bnhd->bqhd", p[..., :n_loc], vb)
                + jnp.einsum("bhqn,bnhd->bqhd", p[..., n_loc:], vc))

    o = lax.map(block, (jnp.arange(nblk), q_blocks))
    y_lat = o.swapaxes(0, 1).reshape(bsz, n_lat, NA_WIDTH) @ w_out
    if not want_ctx:
        return y_lat, None
    qc = qc.reshape(bsz, n_ctx, NA_HEADS, 1, HEAD_DIM)
    oc = gqa_attend(qc, kc, vc).reshape(bsz, n_ctx, NA_WIDTH)
    return y_lat, oc @ w_out

def moe_ffn(h, w_router, e_bias, w_gate, w_up, w_down, s_gate, s_up, s_down):
    n_tok, d = h.shape
    scores = jax.nn.sigmoid((h @ w_router).astype(jnp.float32))
    _, idx = lax.top_k(scores + e_bias.astype(jnp.float32), TOP_K)
    wts = jnp.take_along_axis(scores, idx, axis=-1)
    wts = wts / wts.sum(-1, keepdims=True) * ROUTE_SCALE
    n_pairs = n_tok * TOP_K
    flat_e = idx.reshape(-1)
    order = jnp.argsort(flat_e)
    sorted_e = flat_e[order]
    sorted_tok = (order // TOP_K).astype(jnp.int32)
    sorted_w = wts.reshape(-1)[order]
    counts = jnp.bincount(flat_e, length=N_EXPERTS)
    padded = (counts + MOE_BLOCK - 1) // MOE_BLOCK * MOE_BLOCK
    pad_end = jnp.cumsum(padded)
    pad_start = pad_end - padded
    grp_start = jnp.cumsum(counts) - counts
    dest = pad_start[sorted_e] + jnp.arange(n_pairs) - grp_start[sorted_e]
    n_blocks = (n_pairs + N_EXPERTS * (MOE_BLOCK - 1)) // MOE_BLOCK + 1
    n_slots = n_blocks * MOE_BLOCK
    slot_tok = jnp.full((n_slots,), n_tok, jnp.int32).at[dest].set(sorted_tok)
    slot_w = jnp.zeros((n_slots,), jnp.float32).at[dest].set(sorted_w)
    block_e = jnp.minimum(jnp.searchsorted(pad_end, jnp.arange(n_blocks) * MOE_BLOCK, side="right"),
                          N_EXPERTS - 1)
    h_pad = jnp.concatenate([h, jnp.zeros((1, d), h.dtype)], axis=0)

    def expert_block(args):
        tok, e = args
        xb = h_pad[tok]
        a = jax.nn.silu(xb @ w_gate[e]) * (xb @ w_up[e])
        return a @ w_down[e]

    yb = lax.map(expert_block, (slot_tok.reshape(n_blocks, MOE_BLOCK), block_e))
    y = yb.reshape(n_slots, d) * slot_w[:, None].astype(h.dtype)
    routed = jnp.zeros((n_tok + 1, d), h.dtype).at[slot_tok].add(y)[:n_tok]
    shared = (jax.nn.silu(h @ s_gate) * (h @ s_up)) @ s_down
    return routed + shared

def second_inputs(seed: int = 0) -> dict:
    key = jax.random.key(seed)
    ks = iter(jax.random.split(key, 32))
    D = D_MODEL

    def nrm(shape, scale):
        return jax.random.normal(next(ks), shape, jnp.float32) * scale

    return {
        "x": nrm((BATCH, SEQ, D), 1.0),
        "c": nrm((BATCH, D), 1.0),
        "ctx": nrm((BATCH, CTX_LEN, D), 1.0),
        "c_ctx": nrm((D,), 1.0),
        "w_mod": nrm((DEPTH_2, D, 6 * D), 0.5 * D ** -0.5),
        "b_mod": nrm((DEPTH_2, 6 * D), 0.02),
        "ln1_g": 1.0 + nrm((DEPTH_2, D), 0.05),
        "ln1_b": nrm((DEPTH_2, D), 0.02),
        "ln2_g": 1.0 + nrm((DEPTH_2, D), 0.05),
        "ln2_b": nrm((DEPTH_2, D), 0.02),
        "ab_w_in": nrm((N_EVEN, D, AB_IN_WIDTH), D ** -0.5),
        "ab_w_fnet": nrm((N_EVEN, FNET_GROUPS, FNET_GROUP_DIM, FNET_GROUP_DIM), FNET_GROUP_DIM ** -0.5),
        "ab_q_norm": 1.0 + nrm((N_EVEN, HEAD_DIM), 0.05),
        "ab_k_norm": 1.0 + nrm((N_EVEN, HEAD_DIM), 0.05),
        "ab_w_out": nrm((N_EVEN, AB_OUT_WIDTH, D), AB_OUT_WIDTH ** -0.5 * DN_BETA),
        "na_w_in": nrm((N_ODD, D, 3 * NA_WIDTH), D ** -0.5),
        "na_rpb": nrm((N_ODD, NA_HEADS, 2 * NA_KH - 1, 2 * NA_KW - 1), 0.5),
        "na_w_out": nrm((N_ODD, NA_WIDTH, D), NA_WIDTH ** -0.5 * DN_BETA),
        "moe_w_router": nrm((DEPTH_2, D, N_EXPERTS), D ** -0.5),
        "moe_bias": nrm((DEPTH_2, N_EXPERTS), 0.01),
        "moe_w_gate": nrm((DEPTH_2, N_EXPERTS, D, EXPERT_DIM), D ** -0.5),
        "moe_w_up": nrm((DEPTH_2, N_EXPERTS, D, EXPERT_DIM), D ** -0.5),
        "moe_w_down": nrm((DEPTH_2, N_EXPERTS, EXPERT_DIM, D), EXPERT_DIM ** -0.5 * DN_BETA),
        "sh_w_gate": nrm((DEPTH_2, D, SHARED_DIM), D ** -0.5),
        "sh_w_up": nrm((DEPTH_2, D, SHARED_DIM), D ** -0.5),
        "sh_w_down": nrm((DEPTH_2, SHARED_DIM, D), SHARED_DIM ** -0.5 * DN_BETA),
    }

def second_block(x, c, ctx, c_ctx, w_mod, b_mod, ln1_g, ln1_b, ln2_g, ln2_b,
              ab_w_in, ab_w_fnet, ab_q_norm, ab_k_norm, ab_w_out,
              na_w_in, na_rpb, na_w_out,
              moe_w_router, moe_bias, moe_w_gate, moe_w_up, moe_w_down,
              sh_w_gate, sh_w_up, sh_w_down):
    bsz, n_lat, d = x.shape
    n_ctx = ctx.shape[1]
    for l in range(DEPTH_2):
        want_ctx = l < DEPTH_2 - 1
        j = l // 2
        mod = jax.nn.silu(c) @ w_mod[l] + b_mod[l]
        mod_c = jax.nn.silu(c_ctx) @ w_mod[l] + b_mod[l]
        sh1, sc1, g1, sh2, sc2, g2 = jnp.split(mod[:, None, :], 6, axis=-1)
        csh1, csc1, cg1, csh2, csc2, cg2 = jnp.split(mod_c, 6, axis=-1)
        h = x * (1.0 + sc1) + sh1
        hc = ctx * (1.0 + csc1) + csh1
        if l % 2 == 0:
            y, yc = mixer_ab(h, hc, ab_w_in[j], ab_w_fnet[j], ab_q_norm[j], ab_k_norm[j], ab_w_out[j], want_ctx)
        else:
            y, yc = mixer_na(h, hc, na_w_in[j], na_rpb[j], na_w_out[j], want_ctx)
        x = layer_norm(DN_ALPHA * x + g1 * y, ln1_g[l], ln1_b[l])
        h2 = (x * (1.0 + sc2) + sh2).reshape(bsz * n_lat, d)
        moe_args = (moe_w_router[l], moe_bias[l], moe_w_gate[l], moe_w_up[l], moe_w_down[l],
                    sh_w_gate[l], sh_w_up[l], sh_w_down[l])
        if want_ctx:
            ctx = layer_norm(DN_ALPHA * ctx + cg1 * yc, ln1_g[l], ln1_b[l])
            hc2 = (ctx * (1.0 + csc2) + csh2).reshape(bsz * n_ctx, d)
            ff = moe_ffn(jnp.concatenate([h2, hc2], axis=0), *moe_args)
            ff_lat = ff[:bsz * n_lat].reshape(bsz, n_lat, d)
            ff_ctx = ff[bsz * n_lat:].reshape(bsz, n_ctx, d)
            ctx = layer_norm(DN_ALPHA * ctx + cg2 * ff_ctx, ln2_g[l], ln2_b[l])
        else:
            ff_lat = moe_ffn(h2, *moe_args).reshape(bsz, n_lat, d)
        x = layer_norm(DN_ALPHA * x + g2 * ff_lat, ln2_g[l], ln2_b[l])
    return x


def setup_inputs(seed=0):
    out = dict(first_inputs(seed))
    for name, value in second_inputs(seed + 1).items():
        if name != "x":
            out[name + "_2"] = value
    return out


def reference(
    x, c, positions, ada_w, ada_b, norm_g, ffn_w1, ffn_w2, mla_w_in, mla_q_norm, mla_kv_norm,
    mla_w_q_up, mla_w_kv_up, mla_w_out, sb_w_in, sb_w_out, ret_w_in, ret_gn_g, ret_w_out, c_2,
    ctx_2, c_ctx_2, w_mod_2, b_mod_2, ln1_g_2, ln1_b_2, ln2_g_2, ln2_b_2, ab_w_in_2,
    ab_w_fnet_2, ab_q_norm_2, ab_k_norm_2, ab_w_out_2, na_w_in_2, na_rpb_2, na_w_out_2,
    moe_w_router_2, moe_bias_2, moe_w_gate_2, moe_w_up_2, moe_w_down_2, sh_w_gate_2, sh_w_up_2,
    sh_w_down_2,
):
    x = first_block(
        x, c, positions, ada_w, ada_b, norm_g, ffn_w1, ffn_w2, mla_w_in, mla_q_norm,
        mla_kv_norm, mla_w_q_up, mla_w_kv_up, mla_w_out, sb_w_in, sb_w_out, ret_w_in, ret_gn_g,
        ret_w_out,
    )
    return second_block(
        x, c_2, ctx_2, c_ctx_2, w_mod_2, b_mod_2, ln1_g_2, ln1_b_2, ln2_g_2, ln2_b_2, ab_w_in_2,
        ab_w_fnet_2, ab_q_norm_2, ab_k_norm_2, ab_w_out_2, na_w_in_2, na_rpb_2, na_w_out_2,
        moe_w_router_2, moe_bias_2, moe_w_gate_2, moe_w_up_2, moe_w_down_2, sh_w_gate_2,
        sh_w_up_2, sh_w_down_2,
    )


_drawn_inputs = setup_inputs


def setup_inputs(seed=0):
    import zlib

    import numpy as np

    out = dict(_drawn_inputs(seed))
    spreads = {}
    factors = {'mla_q_norm': 4.48,
     'ret_gn_g': 3.344,
     'ctx_2': 3.941,
     'b_mod_2': 2.79,
     'ab_q_norm_2': 8.0,
     'ab_k_norm_2': 8.0,
     'na_rpb_2': 8.0}
    for name, (base, spread) in spreads.items():
        noise = np.random.default_rng([zlib.crc32(name.encode()), seed]).standard_normal(out[name].shape)
        drawn = base * np.exp(spread * noise) if base else spread * noise
        out[name] = __import__('jax').numpy.asarray(drawn.astype(out[name].dtype))
    for name, factor in factors.items():
        out[name] = (out[name] * factor).astype(out[name].dtype)
    return out
```

```python
from contextlib import ExitStack

import numpy as np
import concourse.bass as bass
import concourse.mybir as mybir

P = 128
D = 1024
DC = D // P
T = 256
TC = 512
FF = 4096
DEPTH, DEPTH_2 = 4, 2
MODS = 6 * DC
EPS = 1e-6
NEG = -1e30
MLA_H, MLA_NOPE, MLA_ROPE, MLA_V = 8, 128, 64, 128
SB_H, SB_D = 16, 64
RET_H, RET_K, RET_V = 4, 256, 512
GQ_H, GKV_H, FN = 6, 2, 256
NA_H, NA_KW, GRID_W = 8, 16, 64
EXPERTS, TOP_K, EXP_D, ROUTE_SCALE = 64, 8, 256, 2.5
DN_ALPHA = (2 * DEPTH_2) ** 0.25
BANKS = 8
SLOTS = 8
PIECE = 2048

F32 = mybir.dt.float32
I32 = mybir.dt.int32
ACT = mybir.ActivationFunctionType
ALU = mybir.AluOpType
AX = mybir.AxisListType

VEC = {}
_at = 0
for _name, _n in (("ada_b", DEPTH * MODS), ("norm_g", DEPTH * 4 * DC), ("b_mod", DEPTH_2 * MODS),
                  ("ln", DEPTH_2 * 4 * DC), ("q_norm", 4), ("kv_norm", 2), ("gn_g", 16), ("qk_gain", 2),
                  ("conds", 3 * DC), ("e_bias", DEPTH_2 * EXPERTS), ("inv_freq", 2), ("parity", 2),
                  ("eps", 1)):
    VEC[_name] = (_at, _at + _n)
    _at += _n
NVEC = _at
TAB_W = 3 * P + 2 * T


class Phase:

    def __init__(self, banks, pieces, turns=1):
        self.banks, self.pieces, self.turns = banks, pieces, turns

    def fill(self, k, turn=0):
        b = self.banks[k]
        return b, self.base[b] + self.banks[:k].count(b) + 1 + self.banks.count(b) * turn

    def piece(self, j, turn=0):
        p = self.first + j
        return p % SLOTS, p // SLOTS + 1 + (self.pieces // SLOTS) * turn, p


def attention_banks(units):
    return [b for u in range(units) for b in (u % 2, 2 + u % 2, 4 + u % 2)]


def plan():
    order = {}
    for l in range(DEPTH):
        order["mod", l] = Phase([0, 1], 8, 3)
        order["norm", 4 * l] = Phase([7], 0)
        if l % 3 == 0:
            order["mla_in", l] = Phase([0, 1, 2, 3], 2)
            order["mla_up", l] = Phase([4, 5, 6, 7, 0, 1, 2, 3, 4, 5, 6, 7, 0, 1, 2, 3, 4], 3)
            order["att", l] = Phase(attention_banks(2 * MLA_H), 0)
            order["mix_out", l] = Phase([0, 1, 2, 3], 4)
        elif l % 3 == 1:
            order["sb_in", l] = Phase([0, 1, 2, 3, 4, 5, 6, 7, 0, 1, 2, 3], 13)
            order["sb", l] = Phase([b for h in range(SB_H) for b in
                                    ([h % 2, 2 + h % 2] + ([4 + h // 2 % 2] if h % 2 else []))], 0)
            order["mix_out", l] = Phase([0, 1, 2, 3], 4)
        else:
            order["ret_in", l] = Phase([0, 1, 2, 3, 4, 5, 6, 7] * 3, 25)
            order["ret", l] = Phase([b for h in range(RET_H) for b in (h % 2, 2, 3)] + [4, 5, 4, 5], 0)
            order["mix_out", l] = Phase([0, 1, 2, 3], 8)
        order["norm", 4 * l + 1] = Phase([7], 0)
        order["norm", 4 * l + 2] = Phase([7], 0)
        order["ffn_up", l] = Phase(list(range(8)), 8, 2)
        order["ffn_down", l] = Phase([0, 1], 8, 2)
        order["norm", 4 * l + 3] = Phase([7], 0)
    for l in range(DEPTH_2):
        order["mod2", l] = Phase([0, 1], 8, 3)
        if l == 0:
            order["ab_in", l] = Phase([0, 1] + [2, 3, 4, 5, 6, 7, 0, 1] + [2, 3] + [4, 5, 6, 7] * 4, 6)
            order["fnet", l] = Phase([0, 1, 2, 3, 4, 5, 6, 7, 0, 1], 1)
            order["att", 4] = Phase(attention_banks(4 * GQ_H), 0)
            order["out2", l] = Phase(list(range(8)), 4)
        else:
            order["na_in", l] = Phase([0, 1, 2, 3] + [4, 5, 6, 7, 0, 1, 2, 3] + [4, 5, 6, 7] * 2, 12)
            order["att", 5] = Phase(attention_banks(2 * NA_H), 3)
            order["out2", l] = Phase(list(range(8)), 4)
        order["ln", 2 * l] = Phase([6, 7], 0)
        order["route", l] = Phase([0], 1)
        if l == 0:
            order["moe_head", l] = Phase([0, 1, 2, 3], 2)
            order["moe", l] = Phase(([0, 1, 2, 3] + [4, 5, 6, 7] * 2) * 8, 24, EXPERTS // 8)
            order["moe_tail", l] = Phase([4, 5, 6, 7] * 2, 1)
        else:
            order["moe_head", l] = Phase([0, 1], 2)
            order["moe", l] = Phase([2, 3, 4, 5, 6, 7, 0, 1, 4, 5, 6, 7] * 4, 24, EXPERTS // 8)
            order["moe_tail", l] = Phase([4, 5, 6, 7], 1)
        order["moe_turn", l] = Phase(list(range(8)), 0)
        order["ln", 2 * l + 1] = Phase([6, 7], 0)
    base, first = [0] * BANKS, 0
    for ph in order.values():
        ph.base, ph.first = list(base), first
        for b in ph.banks:
            base[b] += ph.turns
        first += ph.pieces * ph.turns
        assert ph.turns == 1 or ph.pieces % SLOTS == 0
    return order, first


PLAN, PIECES = plan()
STREAM = -(-PIECES // SLOTS) * SLOTS
UNIT0 = {0: 0, 3: 16, 4: 32, 5: 56}
UNITS = 72


def build(nc, stream, vec_d, tab_d, x_d, ctx_d, pos_d, out_d):
    ctx = ExitStack()
    with ctx:
        def sb(name, shape, dt=F32):
            return ctx.enter_context(nc.sbuf_tensor(name, shape, dt))

        def sem(name):
            return ctx.enter_context(nc.semaphore(name))

        ring = sb("ring", [P, SLOTS, PIECE])
        X = sb("X", [P, DC, TC])
        H = sb("H", [P, DC, TC])
        YS = sb("YS", [P, DC * TC])
        arena = sb("arena", [P, 16384])
        vec = sb("vec", [P, NVEC])
        tab = sb("tab", [P, TAB_W])
        pos = sb("pos", [P, T], I32)
        rope = sb("rope", [P, 4, T])
        zeros = sb("zeros", [P, TC])
        stat = sb("stat", [P, 4, TC])
        mod = sb("mod", [P, DEPTH, MODS])
        gains = sb("gains", [P, DEPTH, 4, DC])
        mod2 = sb("mod2", [P, DEPTH_2, MODS, 2])
        scale2 = sb("scale2", [P, DEPTH_2, 2, DC, 2])
        cond = sb("cond", [P, DC, 3])
        att_stat = sb("att_stat", [P, 3, UNITS])
        route_s = sb("route_s", [P, 32])
        wts = sb("wts", [P, 4, EXPERTS + 1])
        ps = ctx.enter_context(nc.psum_tensor("ps", [P, BANKS, TC], F32))

        def V(name, i=0, n=1):
            a = VEC[name][0] + i
            return vec[:, a:a + n]

        ident, ones_d, rot = tab[:, 0:P], tab[:, P:2 * P], tab[:, 2 * P:3 * P]
        ax_cos, ax_sin = tab[:, 3 * P:3 * P + T], tab[:, 3 * P + T:3 * P + 2 * T]
        Y = YS[:, 0:DC * T].rearrange("p (c t) -> p c t", c=DC)
        SQ = YS[:, DC * T:2 * DC * T].rearrange("p (c t) -> p c t", c=DC)
        SQ2 = YS[:, :].rearrange("p (c t) -> p c t", c=DC)
        MU, STD, RSTD = stat[:, 0, :], stat[:, 1, :], stat[:, 2, :]

        def region(at, *shape):
            n = int(np.prod(shape))
            v = arena[:, at:at + n]
            if len(shape) == 2:
                v = v.rearrange("p (a b) -> p a b", a=shape[0])
            elif len(shape) == 3:
                v = v.rearrange("p (a b c) -> p a b c", a=shape[0], b=shape[1])
            return v

        piece_full = [sem(f"piece_full{s}") for s in range(SLOTS)]
        piece_used = [sem(f"piece_used{s}") for s in range(SLOTS)]
        filled = [sem(f"filled{b}") for b in range(BANKS)]
        drained = [sem(f"drained{b}") for b in range(BANKS)]
        consts_loaded = sem("consts_loaded")
        x_loaded = sem("x_loaded")
        zeros_set = sem("zeros_set")
        cond_ready = sem("cond_ready")
        rope_reduced = sem("rope_reduced")
        rope_ready = sem("rope_ready")
        dve_step = sem("dve_step")
        act_step = sem("act_step")
        pool_step = sem("pool_step")
        mod_ready = sem("mod_ready")
        sq_dve = sem("sq_dve")
        sq_act = sem("sq_act")
        h_scaled = sem("h_scaled")
        h_ready = sem("h_ready")
        y_scaled = sem("y_scaled")
        x_ready = sem("x_ready")
        hidden_ready = sem("hidden_ready")
        mla_sq = sem("mla_sq")
        mla_lat = sem("mla_lat")
        mla_rope = sem("mla_rope")
        kpe_ready = sem("kpe_ready")
        att_exp = sem("att_exp")
        att_rinv = sem("att_rinv")
        att_prob = sem("att_prob")
        sb_ln = sem("sb_ln")
        sb_soft = sem("sb_soft")
        sb_masked = sem("sb_masked")
        sb_guarded = sem("sb_guarded")
        sb_prob = sem("sb_prob")
        ret_part = sem("ret_part")
        ret_roped = sem("ret_roped")
        ret_sq = sem("ret_sq")
        ret_normed = sem("ret_normed")
        ret_gated = sem("ret_gated")
        hm_dve = sem("hm_dve")
        hm_pool = sem("hm_pool")
        x_alpha = sem("x_alpha")
        xc_dve = sem("xc_dve")
        xc_pool = sem("xc_pool")
        ln_sq = sem("ln_sq")
        ln_scaled = sem("ln_scaled")
        ln_ready = sem("ln_ready")
        ab_sq = sem("ab_sq")
        ab_normed = sem("ab_normed")
        ab_roped = sem("ab_roped")
        acc_zeroed = sem("acc_zeroed")
        stored = sem("stored")

        def wait_filled(eng, ph, k, turn=0):
            b, n = ph.fill(k, turn)
            eng.wait_ge(filled[b], n)
            return b

        def wait_drained(eng, ph, k, turn=0):
            b, n = ph.fill(k, turn)
            eng.wait_ge(drained[b], n)

        def chained(eng, done):
            count = [0]

            def link(ins):
                count[0] += 1
                ins.then_inc(done, 1)
                eng.wait_ge(done, count[0])
            return link

        m_qlat, m_klat, m_kpe = region(0, 2, T), region(512, T), region(768, T)
        m_qn, m_qp, m_kn = region(1024, 8, T), region(3072, 4, T), region(4096, 8, T)
        m_v, m_kpm, m_o = region(6144, 2, D), region(8192, 2, T), region(8704, 8, T)
        m_t1, m_t2, m_sq = region(10752, 4, T), region(11776, 4, T), region(10752, 3, T)
        att_s, att_p, att_pt = (region(12800 + 1024 * i, 2, TC) for i in range(3))

        s_q, s_k, s_v, s_o = region(0, 8, T), region(2048, 8, T), region(4096, 2, D), region(6144, 8, T)
        s_e, s_z, s_sp, s_d = (region(8192 + 768 * i, 2, 384) for i in range(4))

        r_q, r_k, r_v = region(0, 8, T), region(2048, 8, T), region(4096, 2, 2 * D)
        r_g, r_o = region(8192, 16, T), region(12288, 16, T)
        r_ta = YS[:, 0:1024].rearrange("p (i c t) -> p i c t", i=2, c=2)
        r_tb = YS[:, 1024:2048].rearrange("p (i c t) -> p i c t", i=2, c=2)
        r_sc = YS[:, 2048:2816].rearrange("p (i t) -> p i t", i=2)
        r_sq = YS[:, 2816:3840].rearrange("p (c t) -> p c t", c=4)

        a_f, a_q, a_k, a_v = region(0, 4, FN), region(1024, 6, TC), region(4096, 2, TC), region(5120, 4, FN)
        a_o, a_t = region(6144, 8, TC), region(10240, 2, T)
        a_ab, a_fr = region(12800, 4, 2 * T), region(14848, 2, TC)

        n_q, n_k, n_v = region(0, 8, T), region(2048, 8, TC), region(6144, 4, D)
        n_o = region(10240, 8, T)
        n_bm = YS[:, 0:2 * TC].rearrange("p (i t) -> p i t", i=2)

        f_h, f_r = region(0, 32, T), region(8192, 2, TC)
        e_acc, e_a, e_sg = region(0, 4, D), region(4096, 2, 2 * TC), region(6144, 2, 2 * TC)
        e_sc, e_sb, e_rep, e_sel, e_w = (region(8192 + 256 * i, 4, EXPERTS) for i in range(5))

        mla_scale = float((MLA_NOPE + MLA_ROPE) ** -0.5)
        head_scale = float(P ** -0.5)

        def slot(ph, j, turn=0):
            return ring[:, ph.piece(j, turn)[0], :]

        def attention_units(l):
            units = []
            if l in (0, 3):
                mask = slot(PLAN["mla_up", l], 2)[:, 1152:1536]
                for h in range(MLA_H):
                    for qb in range(2):
                        nk, at = (P, 0) if qb == 0 else (T, P)
                        qs = slice(qb * P, qb * P + P)
                        units.append(dict(
                            score=[(m_qn[:, h, qs], m_kn[:, h, 0:nk]), (m_qp[:, h // 2, qs], m_kpm[:, h % 2, 0:nk])],
                            mask=mask[:, at:at + nk], nk=nk, bias=None,
                            v=[m_v[:, kb, h * P:(h + 1) * P] for kb in range(nk // P)], o=m_o[:, h, qs]))
            elif l == 4:
                for qb in range(4):
                    for h in range(GQ_H):
                        k0 = 0 if qb < 2 else T
                        g = h // (GQ_H // GKV_H)
                        qs = slice(qb * P, qb * P + P)
                        units.append(dict(
                            score=[(a_q[:, h, qs], a_k[:, g, k0:TC])], mask=zeros[:, k0:TC], nk=TC - k0, bias=None,
                            v=[a_v[:, kb, g * P:(g + 1) * P] for kb in range(k0 // P, 4)], o=a_o[:, 2 + h, qs]))
            else:
                for h in range(NA_H):
                    for qb in range(2):
                        qs = slice(qb * P, qb * P + P)
                        ph = PLAN["att", 5]
                        units.append(dict(
                            score=[(n_q[:, h, qs], n_k[:, h, :])], mask=None, nk=TC,
                            bias=(slot(ph, qb)[:, h * T:(h + 1) * T], slot(ph, 2)[:, qb * T:(qb + 1) * T]),
                            v=[n_v[:, kb, h * P:(h + 1) * P] for kb in range(4)], o=n_o[:, h, qs]))
            return units

        def turns(eng, ph, body, peel):
            if peel:
                body(0)
            with eng.Fori(1 if peel else 0, ph.turns) as turn:
                body(turn)

        def hidden_wait(eng, l, k, turn):
            base = PLAN["moe_head", l].base
            if l == 0:
                for b in (2, 3):
                    eng.wait_ge(drained[b], turn * 8 + (base[b] + k + 1))
            else:
                b = 1 + 2 * (k % 2)
                eng.wait_ge(drained[b], turn * 4 + (base[b] + k // 2 + 1))

        block = ctx.enter_context(nc.Block())

        @block.sync
        def _(sp):
            for s in range(SLOTS):
                sp.dma_start(ring[:, s, :], stream[s]).then_inc(piece_full[s], 16)
            with sp.Fori(1, STREAM // SLOTS) as i:
                for s in range(SLOTS):
                    sp.wait_ge(piece_used[s], i)
                    sp.dma_start(ring[:, s, :], stream[bass.ds(i * SLOTS + s, 1)].rearrange("a p n -> p (a n)"))\
                        .then_inc(piece_full[s], 16)
            sp.wait_ge(ln_ready, 4 * DC)
            sp.dma_start(out_d, X[:, :, 0:T]).then_inc(stored, 16)
            sp.wait_ge(stored, 16)
            for s in range(SLOTS):
                sp.wait_ge(piece_full[s], 16 * (STREAM // SLOTS))

        @block.tensor
        def _(pe):
            mm = nc.tensor.matmul

            def take(ph, j, turn=0):
                s, n, p = ph.piece(j, turn)
                pe.wait_ge(piece_full[s], n * 16)
                return ring[:, s, :], None if p == 0 and isinstance(turn, int) and turn == 0 else piece_used[(p - 1) % SLOTS]

            def bank(ph, k, turn=0):
                b, n = ph.fill(k, turn)
                if not isinstance(n, int) or n > 1:
                    pe.wait_ge(drained[b], n - 1)
                return ps[:, b, :], filled[b]

            def products(out, pairs, filled_sem=None, used=None):
                for i, (lhs, rhs) in enumerate(pairs):
                    m = mm(out, lhs, rhs, start=(i == 0), stop=(i == len(pairs) - 1))
                    if i == 0 and used is not None:
                        m.then_inc(used, 1)
                if filled_sem is not None:
                    m.then_inc(filled_sem, 1)

            def mods(ph, conds):
                def body(turn):
                    for j in range(8):
                        w, used = take(ph, j, turn)
                        if j % 4 == 0:
                            out, full = bank(ph, j // 4, turn)
                        n = conds.shape[2]
                        for i in range(2):
                            col = ((j % 4) * 2 + i) * n
                            products(out[:, col:col + n],
                                     [(w[:, c * 256 + i * P:c * 256 + i * P + P], conds[:, c, :]) for c in range(DC)],
                                     full if j % 4 == 3 and i == 1 else None, used if i == 0 else None)
                turns(pe, ph, body, ph.first == 0)

            def mean_square(n):
                ph = PLAN["norm", n]
                out, full = bank(ph, 0)
                for k in (0, 2, 1, 3):
                    pe.wait_ge(sq_dve if k % 2 == 0 else sq_act, 2 * n + k // 2 + 1)
                    for c in (2 * k, 2 * k + 1):
                        m = mm(out[:, 0:T], ones_d, SQ[:, c, :], start=(c == 0), stop=(c == DC - 1))
                m.then_inc(full, 1)

            def pair(ph, k, j, rhs, off=0, width=256, waits=None):
                w, used = take(ph, j)
                out, full = bank(ph, k)
                for i in range(2):
                    for c, r in enumerate(rhs):
                        if waits and i == 0:
                            waits(c)
                        m = mm(out[:, i * T:(i + 1) * T], w[:, off + c * width + i * P:off + c * width + i * P + P], r,
                               start=(c == 0), stop=(c == len(rhs) - 1))
                        if i == c == 0 and used is not None and off == 0:
                            m.then_inc(used, 1)
                m.then_inc(full, 1)

            def token_major(ph, k, j, blocks):
                w, used = take(ph, j)
                out, full = bank(ph, k)
                for i, tb in enumerate(blocks):
                    products(out[:, i * 256:(i + 1) * 256],
                             [(H[:, c, tb * P:(tb + 1) * P], w[:, c * 256:(c + 1) * 256]) for c in range(DC)],
                             full if i == 1 else None, used if i == 0 and blocks[0] == 0 else None)

            def wait_h(s):
                return lambda c: pe.wait_ge(h_ready, 8 * s + c + 1)

            h_lat = [H[:, c, 0:T] for c in range(DC)]

            def attention(l):
                ph, units, u0 = PLAN["att", l], attention_units(l), UNIT0[l]
                for i in range(len(units) + 2):
                    if i < len(units):
                        out, full = bank(ph, 3 * i)
                        products(out[:, 0:units[i]["nk"]], units[i]["score"], full)
                    if 1 <= i <= len(units):
                        u = i - 1
                        out, full = bank(ph, 3 * u + 1)
                        pe.wait_ge(att_prob, u0 + u + 1)
                        for kb in range(units[u]["nk"] // P):
                            m = nc.tensor.transpose(out[:, kb * P:(kb + 1) * P], att_p[:, u % 2, kb * P:(kb + 1) * P], ident)
                        m.then_inc(full, 1)
                    if i >= 2:
                        u = i - 2
                        out, full = bank(ph, 3 * u + 2)
                        wait_drained(pe, ph, 3 * u + 1)
                        products(out[:, 0:P], [(v, att_pt[:, u % 2, kb * P:(kb + 1) * P])
                                               for kb, v in enumerate(units[u]["v"])], full)

            def mla(l):
                ph = PLAN["mla_in", l]
                for k in range(2):
                    pair(ph, k, k, h_lat, waits=wait_h(2 * l))
                j = l // 3
                out, full = bank(ph, 2)
                pe.wait_ge(mla_sq, 2 * j + 1)
                products(out[:, 0:T], [(ones_d, m_sq[:, c, :]) for c in range(2)], full)
                out, full = bank(ph, 3)
                pe.wait_ge(mla_sq, 2 * j + 2)
                mm(out[:, 0:T], ones_d, m_sq[:, 2, :], start=True, stop=True).then_inc(full, 1)
                ph = PLAN["mla_up", l]
                pe.wait_ge(mla_lat, 3 * j + 2)
                qlat = [m_qlat[:, c, :] for c in range(2)]
                for k in range(4):
                    w, used = take(ph, 0)
                    out, full = bank(ph, k)
                    for i in range(2):
                        n = (2 * k + i) * P
                        products(out[:, i * T:(i + 1) * T], [(w[:, c * D + n:c * D + n + P], qlat[c]) for c in range(2)],
                                 full if i else None, used if k == i == 0 else None)
                w, used = take(ph, 1)
                pe.wait_ge(mla_lat, 3 * j + 3)
                for k in range(4):
                    out, full = bank(ph, 4 + k)
                    for i in range(2):
                        m = mm(out[:, i * T:(i + 1) * T], w[:, (2 * k + i) * P:(2 * k + i + 1) * P], m_klat, start=True, stop=True)
                        if k == i == 0:
                            m.then_inc(used, 1)
                    m.then_inc(full, 1)
                for k in range(4):
                    out, full = bank(ph, 8 + k)
                    tb, half = k // 2, k % 2
                    mm(out, m_klat[:, tb * P:(tb + 1) * P], w[:, D + half * 512:D + (half + 1) * 512], start=True, stop=True)\
                        .then_inc(full, 1)
                w, used = take(ph, 2)
                for k in range(2):
                    out, full = bank(ph, 12 + k)
                    for i in range(2):
                        n = (2 * k + i) * P
                        products(out[:, i * T:(i + 1) * T], [(w[:, c * 512 + n:c * 512 + n + P], qlat[c]) for c in range(2)],
                                 full if i else None, used if k == i == 0 else None)
                for k in range(2):
                    wait_drained(pe, ph, 12 + k)
                    out, full = bank(ph, 14 + k)
                    for i in range(2):
                        m = mm(out[:, i * T:(i + 1) * T], rot, m_qp[:, 2 * k + i, :], start=True, stop=True)
                    m.then_inc(full, 1)
                out, full = bank(ph, 16)
                mm(out[:, 0:T], rot, m_kpe, start=True, stop=True).then_inc(full, 1)
                for k in range(12):
                    wait_drained(pe, ph, k)
                pe.wait_ge(mla_rope, 2 * j + 2)
                pe.wait_ge(kpe_ready, 2 * j + 2)
                attention(l)
                ph = PLAN["mix_out", l]
                for k in range(2 * MLA_H):
                    wait_drained(pe, PLAN["att", l], 3 * k + 2)
                for k in range(4):
                    pair(ph, k, k, [m_o[:, h, :] for h in range(MLA_H)])

            def stick(l):
                ph = PLAN["sb_in", l]
                for k in range(8):
                    pair(ph, k, k, h_lat, waits=wait_h(2 * l))
                for k in range(4):
                    token_major(ph, 8 + k, 8 + k, (0, 1))
                w, used = take(ph, 12)
                tri, ones = w[:, 0:P], w[:, P:2 * P]
                ph = PLAN["sb", l]
                for k in range(12):
                    wait_drained(pe, PLAN["sb_in", l], k)

                def at(h):
                    return 5 * (h // 2) + 2 * (h % 2)

                for i in range(SB_H + 2):
                    if i < SB_H:
                        rows, g = slice((i % 2) * SB_D, (i % 2 + 1) * SB_D), i // 2
                        out, full = bank(ph, at(i))
                        mm(out[:, 0:T], s_k[rows, g, 0:P], s_q[rows, g, :], start=True, stop=True)
                        mm(out[:, T:384], s_k[rows, g, P:T], s_q[rows, g, P:T], start=True, stop=True).then_inc(full, 1)
                    if 1 <= i <= SB_H:
                        u = i - 1
                        out, full = bank(ph, at(u) + 1)
                        pe.wait_ge(sb_masked, u + 1)
                        m = mm(out[:, 0:384], tri, s_sp[:, u % 2, :], start=True, stop=False)
                        if u == 0:
                            m.then_inc(used, 1)
                        mm(out[:, P:T], ones, s_sp[:, u % 2, T:384], start=False, stop=True).then_inc(full, 1)
                    if i >= 2:
                        u = i - 2
                        rows = slice((u % 2) * SB_D, (u % 2 + 1) * SB_D)
                        if u % 2 == 0:
                            o_out, o_full = bank(ph, at(u) + 4)
                        pe.wait_ge(sb_prob, u + 1)
                        hv = slice(u * SB_D, (u + 1) * SB_D)
                        mm(o_out[rows, 0:T], s_v[:, 0, hv], s_d[:, u % 2, 0:T], start=True, stop=False)
                        m = mm(o_out[rows, P:T], s_v[:, 1, hv], s_d[:, u % 2, T:384], start=False, stop=True)
                        if u % 2:
                            m.then_inc(o_full, 1)
                for g in range(8):
                    wait_drained(pe, ph, 5 * g + 4)
                ph = PLAN["mix_out", l]
                for k in range(4):
                    pair(ph, k, k, [s_o[:, c, :] for c in range(8)])

            def retention(l):
                ph = PLAN["ret_in", l]
                for k in range(8):
                    pair(ph, k, k, h_lat, waits=wait_h(2 * l))
                for k in range(8):
                    token_major(ph, 8 + k, 8 + k, (0, 1))
                for k in range(8):
                    pair(ph, 16 + k, 16 + k, h_lat)
                for k in range(8, 16):
                    wait_drained(pe, ph, k)
                ph = PLAN["ret", l]
                for h in range(RET_H):
                    pe.wait_ge(ret_roped, RET_H + h + 1)
                    out, full = bank(ph, 3 * h)
                    products(out[:, 0:T], [(r_k[:, 2 * h + c, 0:P], r_q[:, 2 * h + c, :]) for c in range(2)], None,
                             piece_used[PLAN["ret_in", l].piece(23)[0]] if h == 0 else None)
                    products(out[:, T:384], [(r_k[:, 2 * h + c, P:T], r_q[:, 2 * h + c, P:T]) for c in range(2)], full)
                    wait_drained(pe, ph, 3 * h)
                    for half in range(2):
                        out, full = bank(ph, 3 * h + 1 + half)
                        for i in range(2):
                            n = h * RET_V + (2 * half + i) * P
                            mm(out[:, i * T:(i + 1) * T], r_v[:, 0, n:n + P], r_sc[:, h % 2, 0:T], start=True, stop=False)
                            m = mm(out[:, i * T + P:(i + 1) * T], r_v[:, 1, n:n + P], r_sc[:, h % 2, T:384],
                                   start=False, stop=True)
                        m.then_inc(full, 1)
                    pe.wait_ge(ret_sq, h + 1)
                    out, full = bank(ph, 12 + h)
                    products(out[:, 0:T], [(ones_d, r_sq[:, c, :]) for c in range(4)], full)
                pe.wait_ge(ret_gated, RET_H)
                ph = PLAN["mix_out", l]
                for k in range(4):
                    out, full = bank(ph, k)
                    for i in range(2):
                        w, used = take(ph, 2 * k + i)
                        products(out[:, i * T:(i + 1) * T], [(w[:, c * P:(c + 1) * P], r_o[:, c, :]) for c in range(16)],
                                 full if i else None, used)

            def ffn(l):
                ph = PLAN["ffn_up", l]
                for c in range(DC):
                    pe.wait_ge(h_ready, 8 * (2 * l + 1) + c + 1)
                with pe.Fori(0, ph.turns) as turn:
                    for j in range(8):
                        w, used = take(ph, j, turn)
                        out, full = bank(ph, j, turn)
                        for i in range(2):
                            products(out[:, i * T:(i + 1) * T],
                                     [(w[:, c * 256 + i * P:c * 256 + i * P + P], h_lat[c]) for c in range(DC)],
                                     full if i else None, None if i else used)
                ph = PLAN["ffn_down", l]
                pe.wait_ge(hidden_ready, 16 * (l + 1))
                with pe.Fori(0, ph.turns) as turn:
                    for k in range(2):
                        out, full = bank(ph, k, turn)
                        for i in range(2):
                            for half in range(2):
                                w, used = take(ph, 4 * k + 2 * i + half, turn)
                                for c in range(16):
                                    m = mm(out[:, i * T:(i + 1) * T], w[:, c * P:(c + 1) * P], f_h[:, 16 * half + c, :],
                                           start=(half == c == 0), stop=(half == 1 and c == 15))
                                    if c == 0:
                                        m.then_inc(used, 1)
                        m.then_inc(full, 1)

            def wait_hm(n):
                pe.wait_ge(hm_dve, 8 * n + 8)
                pe.wait_ge(hm_pool, 8 * min(n, 2) + 8)

            h_all = [H[:, c, :] for c in range(DC)]

            def chunks512(ph, k0, j0, pieces, rhs, cols):
                for j in range(pieces):
                    w, used = take(ph, j0 + j)
                    for i in range(2):
                        out, full = bank(ph, k0 + 2 * j + i)
                        products(out[:, 0:cols], [(w[:, c * 256 + i * P:c * 256 + i * P + P], r) for c, r in enumerate(rhs)],
                                 full, None if i else used)

            def fourier_gqa():
                ph = PLAN["ab_in", 0]
                wait_hm(0)
                for k in range(2):
                    token_major(ph, k, 0, (2 * k, 2 * k + 1))
                chunks512(ph, 2, 1, 4, h_all, TC)
                for k in range(2):
                    token_major(ph, 10 + k, 5, (2 * k, 2 * k + 1))
                for c in range(8):
                    out, full = bank(ph, 12 + c)
                    pe.wait_ge(ab_sq, c + 1)
                    mm(out, ones_d, SQ2[:, c, :], start=True, stop=True).then_inc(full, 1)
                for c in range(8):
                    out, full = bank(ph, 20 + c)
                    pe.wait_ge(ab_normed, c + 1)
                    src = a_q[:, c, 0:T] if c < GQ_H else a_k[:, c - GQ_H, 0:T]
                    mm(out[:, 0:T], rot, src, start=True, stop=True).then_inc(full, 1)
                ph2 = PLAN["fnet", 0]
                w, used = take(ph2, 0)
                for k in range(2):
                    wait_drained(pe, ph, k)
                for k in range(4):
                    tb, cc = 2 * (k // 2), k % 2
                    out, full = bank(ph2, k)
                    for i in range(2):
                        products(out[:, i * T:(i + 1) * T],
                                 [(a_f[:, tb + c, cc * P:(cc + 1) * P], w[:, (2 * i + c) * T:(2 * i + c + 1) * T]) for c in range(2)],
                                 full if i else None, used if i == k == 0 else None)
                for k in range(4):
                    wait_drained(pe, ph2, k)
                    out, full = bank(ph2, 4 + k)
                    products(out[:, 0:T], [(w[:, 1024 + i * P:1024 + (i + 1) * P], a_ab[:, k, i * T:(i + 1) * T]) for i in range(2)], full)
                for k in range(4):
                    wait_drained(pe, ph2, 4 + k)
                for cc in range(2):
                    out, full = bank(ph2, 8 + cc)
                    mm(out, w[:, 1280 + cc * P:1280 + (cc + 1) * P], a_fr[:, cc, :], start=True, stop=True).then_inc(full, 1)
                pe.wait_ge(ab_roped, 8)
                for k in range(2):
                    wait_drained(pe, ph, 10 + k)
                attention(4)
                for k in range(2):
                    wait_drained(pe, ph2, 8 + k)
                for k in range(4 * GQ_H):
                    wait_drained(pe, PLAN["att", 4], 3 * k + 2)
                chunks512(PLAN["out2", 0], 0, 0, 4, [a_o[:, c, :] for c in range(8)], TC)

            def neighbours():
                ph = PLAN["na_in", 1]
                wait_hm(2)
                for k in range(4):
                    pair(ph, k, k, h_lat)
                chunks512(ph, 4, 4, 4, h_all, TC)
                for j in range(4):
                    for half in range(2):
                        token_major(ph, 12 + 2 * j + half, 8 + j, (2 * half, 2 * half + 1))
                for k in range(20):
                    wait_drained(pe, ph, k)
                attention(5)
                for k in range(2 * NA_H):
                    wait_drained(pe, PLAN["att", 5], 3 * k + 2)
                ph, po = PLAN["att", 5], PLAN["out2", 1]
                done = [piece_used[ph.piece(j)[0]] for j in (0, 1)] + [piece_used[(ph.piece(0)[2] - 1) % SLOTS]]
                for j in range(4):
                    w, used = take(po, j)
                    for i in range(2):
                        out, full = bank(po, 2 * j + i)
                        for c in range(DC):
                            m = mm(out[:, 0:T], w[:, c * 256 + i * P:c * 256 + i * P + P], n_o[:, c, :], start=(c == 0), stop=(c == DC - 1))
                            if i == 0 and c == 0:
                                m.then_inc(used, 1)
                            elif i == j == 0 and c <= 3:
                                m.then_inc(done[c - 1], 1)
                        m.then_inc(full, 1)

            def layer_norm(m, cols, y, ks):
                ph = PLAN["ln", m]
                out, full = bank(ph, 0)
                for c in range(DC):
                    wait_drained(pe, y, ks[c])
                    i = mm(out[:, 0:cols], ones_d, X[:, c, 0:cols], start=(c == 0), stop=(c == DC - 1))
                i.then_inc(full, 1)
                out, full = bank(ph, 1)
                for c in range(DC):
                    pe.wait_ge(ln_sq, 8 * m + c + 1)
                    i = mm(out[:, 0:cols], ones_d, SQ2[:, c, 0:cols], start=(c == 0), stop=(c == DC - 1))
                i.then_inc(full, 1)

            def moe(l):
                nb = 4 - 2 * l
                cols = nb * P
                n = 2 * l + 1
                wait_hm(n)
                ph = PLAN["route", l]
                w, used = take(ph, 0)
                out, full = bank(ph, 0)
                for tb in range(nb):
                    products(out[:, tb * EXPERTS:(tb + 1) * EXPERTS],
                             [(H[:, c, tb * P:(tb + 1) * P], w[:, c * EXPERTS:(c + 1) * EXPERTS]) for c in range(DC)],
                             full if tb == nb - 1 else None, used if tb == 0 else None)
                rhs = [H[:, c, 0:cols] for c in range(DC)]

                def up(ph, k, j, turn=0):
                    for part in range(2):
                        w, used = take(ph, j + part, turn)
                        for i in range(2):
                            if l == 0:
                                out, full = bank(ph, k + 2 * part + i, turn)
                            elif i == 0:
                                out, full = bank(ph, k + part, turn)
                            products(out[:, 0:cols] if l == 0 else out[:, i * T:(i + 1) * T],
                                     [(w[:, c * 256 + i * P:c * 256 + i * P + P], rhs[c]) for c in range(DC)],
                                     full if l == 0 or i else None, None if i else used)

                def down(ph, k, j, e, turn=0):
                    w, used = take(ph, j, turn)
                    hidden_wait(pe, l, e, turn)
                    parity = e % 2
                    for tb in range(nb):
                        for half in range(2):
                            out, full = bank(ph, k + 2 * tb + half, turn)
                            products(out, [(e_a[:, parity, c * cols + tb * P:c * cols + (tb + 1) * P],
                                            w[:, c * D + half * 512:c * D + (half + 1) * 512]) for c in range(2)],
                                     full, used if tb == half == 0 else None)

                per = 12 if l == 0 else 6
                nu = 4 if l == 0 else 2
                up(PLAN["moe_head", l], 0, 0)
                ph = PLAN["moe", l]
                with pe.Fori(0, ph.turns) as turn:
                    for k in range(8):
                        up(ph, per * k, 3 * k, turn)
                        down(ph, per * k + nu, 3 * k + 2, k, turn)
                down(PLAN["moe_tail", l], 0, 0, EXPERTS)
                ph = PLAN["moe_turn", l]
                tail = PLAN["moe_tail", l]
                for k in range(2 * nb):
                    wait_drained(pe, tail, k)
                for c in range(DC):
                    out, full = bank(ph, c)
                    for tb in range(nb):
                        m = nc.tensor.transpose(out[:, tb * P:(tb + 1) * P], e_acc[:, tb, c * P:(c + 1) * P], ident)
                    m.then_inc(full, 1)

            pe.wait_ge(consts_loaded, 48)
            pe.wait_ge(cond_ready, 2)
            for l in range(DEPTH):
                mods(PLAN["mod", l], cond[:, :, 0:1])
                mean_square(4 * l)
                (mla, stick, retention)[l % 3](l)
                mean_square(4 * l + 1)
                mean_square(4 * l + 2)
                ffn(l)
                mean_square(4 * l + 3)
            for l in range(DEPTH_2):
                mods(PLAN["mod2", l], cond[:, :, 1:3])
                (fourier_gqa, neighbours)[l]()
                layer_norm(2 * l, TC if l == 0 else T, PLAN["out2", l], list(range(8)))
                moe(l)
                layer_norm(2 * l + 1, TC if l == 0 else T, PLAN["moe_turn", l], list(range(8)))

        @block.scalar
        def _(act):
            link = chained(act, act_step)
            fn = nc.scalar.activation
            act.dma_start(vec[:], vec_d).then_inc(consts_loaded, 16)
            act.dma_start(tab[:], tab_d).then_inc(consts_loaded, 16)
            act.dma_start(pos[:], pos_d).then_inc(consts_loaded, 16)
            act.dma_start(X[:, :, 0:T], x_d).then_inc(x_loaded, 16)
            act.dma_start(X[:, :, T:TC], ctx_d).then_inc(x_loaded, 16)
            eps = V("eps")

            def drain(ph, k, out, in_, func=ACT.Copy, turn=0, **kw):
                b, _ = ph.fill(k, turn)
                wait_filled(act, ph, k, turn)
                return fn(out, in_(ps[:, b, :]), func, **kw).then_inc(drained[b], 1)

            def whole(b):
                return b

            def left(b):
                return b[:, 0:T]

            def pairs(b):
                return b.rearrange("p (a t) -> p a t", a=2)

            def pre_norm(s):
                if s:
                    act.wait_ge(x_ready, 8 * s)
                else:
                    act.wait_ge(x_loaded, 32)
                for k in (1, 3):
                    fn(SQ[:, 2 * k:2 * k + 2, :], X[:, 2 * k:2 * k + 2, 0:T], ACT.Square).then_inc(sq_act, 1)
                drain(PLAN["norm", 2 * s], 0, STD[:, 0:T], left, ACT.Sqrt, bias=eps)
                l = s // 2
                act.wait_ge(mod_ready, l + 1)
                for c in range(DC):
                    act.wait_ge(h_scaled, 8 * s + c + 1)
                    shift = (s % 2) * 3 * DC + c
                    fn(H[:, c, 0:T], H[:, c, 0:T], ACT.Identity, bias=mod[:, l, shift:shift + 1]).then_inc(h_ready, 1)

            def post_norm(s, ph):
                def one(k, at, turn):
                    drain(ph, k, Y[:, at, :], pairs, turn=turn)
                    wait_drained(act, ph, k, turn)
                    fn(SQ[:, at, :], Y[:, at, :], ACT.Square).then_inc(sq_act, 1)
                if ph.turns == 1:
                    for k in (1, 3):
                        one(k, slice(2 * k, 2 * k + 2), 0)
                else:
                    with act.Fori(0, ph.turns) as turn:
                        one(1, bass.ds(turn * 4 + 2, 2), turn)
                drain(PLAN["norm", 2 * s + 1], 0, STD[:, 0:T], left, ACT.Sqrt, bias=eps)

            def attention(l):
                ph, units, u0 = PLAN["att", l], attention_units(l), UNIT0[l]
                for i in range(len(units) + 1):
                    if i < len(units):
                        U, nk = u0 + i, units[i]["nk"]
                        wait_drained(act, ph, 3 * i)
                        fn(att_p[:, i % 2, 0:nk], att_s[:, i % 2, 0:nk], ACT.Exp, scale=-1.0, bias=att_stat[:, 0, U:U + 1],
                           accum_out=att_stat[:, 1, U:U + 1]).then_inc(att_exp, 1)
                    if i >= 1:
                        u = i - 1
                        if u >= 2:
                            wait_filled(act, ph, 3 * (u - 2) + 2)
                        nk = units[u]["nk"]
                        drain(ph, 3 * u + 1, att_pt[:, u % 2, 0:nk], lambda b: b[:, 0:nk])

            def mla(l):
                ph, j = PLAN["mla_in", l], l // 3
                wait_drained(act, ph, 0)
                fn(m_sq[:, 0:2, :], m_qlat, ACT.Square).then_inc(mla_sq, 1)
                wait_drained(act, ph, 1)
                fn(m_sq[:, 2, :], m_klat, ACT.Square).then_inc(mla_sq, 1)
                drain(ph, 2, STD[:, 0:T], left, ACT.Sqrt, scale=D / 256.0, bias=eps)
                drain(ph, 3, STD[:, T:TC], left, ACT.Sqrt, scale=D / 128.0, bias=eps)
                ph = PLAN["mla_up", l]
                for k in range(0, 4):
                    drain(ph, k, m_qn[:, 2 * k:2 * k + 2, :], pairs)
                for k in range(8, 12):
                    tb, half = (k - 8) // 2, k % 2
                    drain(ph, k, m_v[:, tb, half * 512:(half + 1) * 512], whole)
                for k in range(12, 14):
                    drain(ph, k, m_qp[:, 2 * (k - 12):2 * (k - 12) + 2, :], pairs)
                attention(l)

            def stick(l):
                ph = PLAN["sb_in", l]
                for k in range(0, 4):
                    drain(ph, k, s_q[:, 2 * k:2 * k + 2, :], pairs)
                for k in range(8, 12):
                    drain(ph, k, s_v[:, :, (k - 8) * 256:(k - 7) * 256], pairs)
                ph = PLAN["sb", l]
                for i in range(SB_H + 1):
                    if i < SB_H:
                        wait_drained(act, ph, 5 * (i // 2) + 2 * (i % 2))
                        if i >= 2:
                            act.wait_ge(sb_soft, i - 1)
                        e = s_e[:, i % 2, :]
                        link(fn(e, s_z[:, i % 2, :], ACT.Abs))
                        link(fn(e, e, ACT.Exp, scale=-1.0))
                        fn(e, e, ACT.Ln, bias=1.0).then_inc(sb_ln, 1)
                    if i >= 1:
                        u = i - 1
                        act.wait_ge(sb_guarded, u + 1)
                        fn(s_d[:, u % 2, :], s_d[:, u % 2, :], ACT.Exp).then_inc(sb_prob, 1)

            def retention(l):
                ph = PLAN["ret_in", l]
                for k in range(8, 16):
                    drain(ph, k, r_v[:, :, (k - 8) * 256:(k - 7) * 256], pairs)
                for k in range(16, 24):
                    drain(ph, k, r_g[:, 2 * (k - 16):2 * (k - 16) + 2, :], pairs, ACT.Silu)
                ph = PLAN["ret", l]
                for h in range(RET_H):
                    for half in range(2):
                        at = slice(4 * h + 2 * half, 4 * h + 2 * half + 2)
                        drain(ph, 3 * h + 1 + half, r_o[:, at, :], pairs)
                    for half in range(2):
                        wait_drained(act, ph, 3 * h + 1 + half)
                    fn(r_sq[:, :, :], r_o[:, 4 * h:4 * h + 4, :], ACT.Square).then_inc(ret_sq, 1)
                    drain(ph, 12 + h, stat[:, h, 0:T], left, ACT.Sqrt, scale=D / float(RET_V), bias=eps)

            def ffn(l):
                ph = PLAN["ffn_up", l]

                def body(turn):
                    for j in range(8):
                        b = wait_filled(act, ph, j, turn)
                        n = turn * 8 + (16 * l + j - 1)
                        if not isinstance(n, int) or n > 0:
                            act.wait_ge(hidden_ready, n)
                        fn(f_r[:, j % 2, :], ps[:, b, :], ACT.Relu).then_inc(drained[b], 1)
                turns(act, ph, body, l == 0)

            def layer_norm(m, cols):
                ph, l = PLAN["ln", m], m // 2
                drain(ph, 0, MU[:, 0:cols], lambda b: b[:, 0:cols])
                for c in range(DC):
                    act.wait_ge(xc_dve if c % 2 == 0 else xc_pool, 4 * m + c // 2 + 1)
                    fn(SQ2[:, c, 0:cols], X[:, c, 0:cols], ACT.Square).then_inc(ln_sq, 1)
                drain(ph, 1, STD[:, 0:cols], lambda b: b[:, 0:cols], ACT.Sqrt, bias=eps)
                for c in range(DC):
                    act.wait_ge(ln_scaled, 8 * m + c + 1)
                    fn(X[:, c, 0:cols], X[:, c, 0:cols], ACT.Identity, bias=V("ln", (4 * l + 2 * (m % 2) + 1) * DC + c))\
                        .then_inc(ln_ready, 1)

            def fourier_gqa():
                ph = PLAN["ab_in", 0]
                for k in range(2):
                    drain(ph, k, a_f[:, 2 * k:2 * k + 2, :], pairs)
                for c in range(8):
                    wait_drained(act, ph, 2 + c)
                    src = a_q[:, c, :] if c < GQ_H else a_k[:, c - GQ_H, :]
                    fn(SQ2[:, c, :], src, ACT.Square).then_inc(ab_sq, 1)
                for k in range(2):
                    drain(ph, 10 + k, a_v[:, 2 * k:2 * k + 2, :], pairs)
                for c in range(8):
                    if c >= 2:
                        act.wait_ge(ab_normed, c - 1)
                    drain(ph, 12 + c, stat[:, c % 2, :], whole, ACT.Sqrt, scale=D / float(P), bias=eps)
                ph = PLAN["fnet", 0]
                for k in range(4):
                    tok, cc = k // 2, k % 2
                    drain(ph, 4 + k, a_fr[:, cc, tok * T:(tok + 1) * T], left)
                attention(4)

            def neighbours():
                ph = PLAN["na_in", 1]
                for k in range(4):
                    drain(ph, k, n_q[:, 2 * k:2 * k + 2, :], pairs)
                for k in range(4, 12, 2):
                    drain(ph, k, n_k[:, k - 4, :], whole)
                for j in range(4):
                    drain(ph, 12 + 2 * j, n_v[:, 0:2, j * 256:(j + 1) * 256], pairs)
                attention(5)

            def moe(l):
                nb = 4 - 2 * l
                cols = nb * P
                b = wait_filled(act, PLAN["route", l], 0)
                fn(e_sc[:, 0:nb, :], ps[:, b, 0:nb * EXPERTS].rearrange("p (a e) -> p a e", a=nb), ACT.Sigmoid)\
                    .then_inc(drained[b], 1)

                def silu(ph, k, e, turn=0):
                    if not isinstance(turn, int) or turn > 0 or e >= 2:
                        hidden_wait(act, l, e - 2, turn)
                    for i in range(2 if l == 0 else 1):
                        b = wait_filled(act, ph, k + i, turn)
                        fn(e_sg[:, e % 2, i * TC:(i + 1) * TC], ps[:, b, :], ACT.Silu).then_inc(drained[b], 1)

                silu(PLAN["moe_head", l], 0, 0)
                ph = PLAN["moe", l]
                per = 12 if l == 0 else 6

                def body(turn):
                    for k in range(8):
                        silu(ph, per * k, k + 1, turn)
                turns(act, ph, body, True)

            act.wait_ge(consts_loaded, 48)
            conds = V("conds", 0, 3 * DC).rearrange("p (c n) -> p c n", n=3)
            fn(cond[:, :, 0:1], conds[:, :, 0:1], ACT.Silu).then_inc(cond_ready, 1)
            fn(cond[:, :, 1:3], conds[:, :, 1:3], ACT.Silu).then_inc(cond_ready, 1)
            act.wait_ge(rope_reduced, 4)
            for n in range(4):
                fn(rope[:, n, :], rope[:, n, :], ACT.Sin).then_inc(rope_ready, 1)
            for l in range(DEPTH):
                pre_norm(2 * l)
                (mla, stick, retention)[l % 3](l)
                post_norm(2 * l, PLAN["mix_out", l])
                pre_norm(2 * l + 1)
                ffn(l)
                post_norm(2 * l + 1, PLAN["ffn_down", l])
            for l in range(DEPTH_2):
                (fourier_gqa, neighbours)[l]()
                layer_norm(2 * l, TC if l == 0 else T)
                moe(l)
                layer_norm(2 * l + 1, TC if l == 0 else T)

        @block.vector
        def _(dve):
            link = chained(dve, dve_step)
            v = nc.vector
            tt, ts, stt = v.tensor_tensor, v.tensor_scalar, v.scalar_tensor_tensor
            MUL, ADD, SUB = ALU.mult, ALU.add, ALU.subtract

            def pairs(b):
                return b.rearrange("p (a t) -> p a t", a=2)

            def drain(ph, k, out, shape=None, turn=0):
                b = wait_filled(dve, ph, k, turn)
                src = ps[:, b, :] if shape is None else shape(ps[:, b, :])
                v.tensor_copy(out, src).then_inc(drained[b], 1)

            def rope_tables():
                f, turns_, ang = region(0, T), region(T, T), region(2 * T, T)
                c1, c2 = 6.28125, 0.0019350051879882812
                c3 = 2 * np.pi - c1 - c2
                big = 1.5 * 2 ** 23
                link(v.tensor_copy(f, pos[:]))
                for w in range(2):
                    link(ts(ang, f, V("inv_freq", w), None, MUL))
                    for i, quarter in enumerate((0.25, 0.0)):
                        r = rope[:, 2 * w + i, :]
                        link(ts(turns_, ang, float(1 / (2 * np.pi)), quarter, MUL, ADD))
                        link(ts(turns_, turns_, big, None, ADD))
                        link(ts(turns_, turns_, big, None, SUB))
                        link(stt(r, turns_, -c1, ang, MUL, ADD))
                        link(stt(r, turns_, -c2, r, MUL, ADD))
                        link(stt(r, turns_, -float(c3), r, MUL, ADD))
                        link(ts(r, r, float(quarter * 2 * np.pi), 3.1415925, ADD, ALU.min))
                        ts(r, r, -3.1415925, None, ALU.max).then_inc(rope_reduced, 1)

            def mods(l):
                ph = PLAN["mod", l]

                def body(turn):
                    for g in range(2):
                        b = wait_filled(dve, ph, g, turn)
                        at = bass.ds(turn * 16 + g * 8, 8) if not isinstance(turn, int) else slice(turn * 16 + g * 8, turn * 16 + g * 8 + 8)
                        tt(mod[:, l, at], ps[:, b, 0:8], V("ada_b", l * MODS, MODS)[:, at], ADD).then_inc(drained[b], 1)
                turns(dve, ph, body, l == 0)
                for g in range(2):
                    wait_drained(dve, ph, g, ph.turns - 1)

                def part(i):
                    return mod[:, l, i * DC:(i + 1) * DC]

                for i in range(2):
                    g = V("norm_g", (4 * l + 2 * i) * DC, 2 * DC)
                    stt(gains[:, l, 2 * i, :], part(3 * i + 1), 1.0, g[:, 0:DC], ADD, MUL)
                    last = tt(gains[:, l, 2 * i + 1, :], part(3 * i + 2), g[:, DC:2 * DC], MUL)
                last.then_inc(mod_ready, 1)
                dve.wait_ge(mod_ready, l + 1)

            def mods2(l):
                ph = PLAN["mod2", l]

                def body(turn):
                    for g in range(2):
                        b = wait_filled(dve, ph, g, turn)
                        at = bass.ds(turn * 16 + g * 8, 8)
                        src = ps[:, b, 0:16].rearrange("p (a n) -> p a n", n=2)
                        for n in range(2):
                            last = tt(mod2[:, l, at, n], src[:, :, n], V("b_mod", l * MODS, MODS)[:, at], ADD)
                        last.then_inc(drained[b], 1)
                turns(dve, ph, body, False)
                for g in range(2):
                    wait_drained(dve, ph, g, ph.turns - 1)
                for i in range(2):
                    last = ts(scale2[:, l, i, :, :], mod2[:, l, (3 * i + 1) * DC:(3 * i + 2) * DC, :], 1.0, None, ADD)
                last.then_inc(mod_ready, 1)
                dve.wait_ge(mod_ready, DEPTH + l + 1)

            def reciprocal_deviation(n):
                wait_drained(dve, PLAN["norm", n], 0)
                link(v.reciprocal(RSTD[:, 0:T], STD[:, 0:T]))

            def pre_norm(s):
                if s:
                    dve.wait_ge(x_ready, 8 * s)
                else:
                    dve.wait_ge(x_loaded, 32)
                for k in (0, 2):
                    x = X[:, 2 * k:2 * k + 2, 0:T]
                    tt(SQ[:, 2 * k:2 * k + 2, :], x, x, MUL).then_inc(sq_dve, 1)
                reciprocal_deviation(2 * s)
                for c in range(DC):
                    stt(H[:, c, 0:T], X[:, c, 0:T], gains[:, s // 2, 2 * (s % 2), c:c + 1], RSTD[:, 0:T], MUL, MUL)\
                        .then_inc(h_scaled, 1)

            def post_norm(s, ph):
                def one(k, at, turn):
                    drain(ph, k, Y[:, at, :], pairs, turn)
                    wait_drained(dve, ph, k, turn)
                    tt(SQ[:, at, :], Y[:, at, :], Y[:, at, :], MUL).then_inc(sq_dve, 1)
                if ph.turns == 1:
                    for k in (0, 2):
                        one(k, slice(2 * k, 2 * k + 2), 0)
                else:
                    with dve.Fori(0, ph.turns) as turn:
                        one(0, bass.ds(turn * 4, 2), turn)
                reciprocal_deviation(2 * s + 1)
                for c in range(DC):
                    stt(Y[:, c, :], Y[:, c, :], gains[:, s // 2, 2 * (s % 2) + 1, c:c + 1], RSTD[:, 0:T], MUL, MUL)\
                        .then_inc(y_scaled, 1)

            def attention(l, scale):
                ph, units, u0 = PLAN["att", l], attention_units(l), UNIT0[l]
                for i in range(len(units) + 2):
                    if i < len(units):
                        unit, U = units[i], u0 + i
                        nk, mask = unit["nk"], unit["mask"]
                        if unit["bias"] is not None:
                            bias, window = unit["bias"]
                            mask = n_bm[:, i % 2, :]
                            link(stt(mask[:, 0:T], bias, 1.0 / scale, window, MUL, ADD))
                        b = wait_filled(dve, ph, 3 * i)
                        if i >= 2:
                            dve.wait_ge(att_exp, U - 1)
                        v.tensor_tensor_reduce(out=att_s[:, i % 2, 0:nk], in0=ps[:, b, 0:nk], in1=mask, scale=-scale,
                                               scalar=3e38, op0=ADD, op1=ALU.min,
                                               accum_out=att_stat[:, 0, U:U + 1]).then_inc(drained[b], 1)
                        dve.wait_ge(att_exp, U + 1)
                        v.reciprocal(att_stat[:, 2, U:U + 1], att_stat[:, 1, U:U + 1]).then_inc(att_rinv, 1)
                    if i >= 2:
                        drain(ph, 3 * (i - 2) + 2, units[i - 2]["o"], lambda b: b[:, 0:P])

            def mla(l):
                ph, j = PLAN["mla_in", l], l // 3
                drain(ph, 0, m_qlat, pairs)
                drain(ph, 1, region(512, 2, T), pairs)
                wait_drained(dve, ph, 2)
                link(v.reciprocal(RSTD[:, 0:T], STD[:, 0:T]))
                for c in range(2):
                    stt(m_qlat[:, c, :], m_qlat[:, c, :], V("q_norm", 2 * j + c), RSTD[:, 0:T], MUL, MUL).then_inc(mla_lat, 1)
                wait_drained(dve, ph, 3)
                link(v.reciprocal(RSTD[:, T:TC], STD[:, T:TC]))
                stt(m_klat, m_klat, V("kv_norm", j), RSTD[:, T:TC], MUL, MUL).then_inc(mla_lat, 1)
                ph = PLAN["mla_up", l]
                for k in range(4, 8):
                    drain(ph, k, m_kn[:, 2 * (k - 4):2 * (k - 4) + 2, :], pairs)
                dve.wait_ge(rope_ready, 4)
                cos, sin = rope[:, 0, :], rope[:, 1, :]
                for k in range(2):
                    b = wait_filled(dve, ph, 14 + k)
                    tt(m_t2[:, 2 * k, :], ps[:, b, 0:T], sin, MUL)
                    tt(m_t2[:, 2 * k + 1, :], ps[:, b, T:TC], sin, MUL).then_inc(drained[b], 1)
                b = wait_filled(dve, ph, 16)
                tt(m_t1[:, 0, :], ps[:, b, 0:T], sin, MUL).then_inc(drained[b], 1)
                link(tt(m_t1[:, 1, :], m_kpe, cos, MUL))
                wait_drained(dve, ph, 16)
                link(tt(m_t1[:, 2, :], m_t1[:, 0, :], m_t1[:, 1, :], ADD))
                for i in range(2):
                    ts(m_kpm[:, i, :], m_t1[:, 2, :], V("parity", i), None, MUL).then_inc(kpe_ready, 1)
                s, n, _ = ph.piece(2)
                dve.wait_ge(piece_full[s], 16 * n)
                attention(l, mla_scale)

            def stick(l):
                ph = PLAN["sb_in", l]
                for k in range(4, 8):
                    drain(ph, k, s_k[:, 2 * (k - 4):2 * (k - 4) + 2, :], pairs)
                ph = PLAN["sb", l]
                for i in range(SB_H + 3):
                    if i < SB_H:
                        at = 5 * (i // 2) + 2 * (i % 2)
                        b = wait_filled(dve, ph, at)
                        if i >= 2:
                            wait_drained(dve, ph, 5 * (i // 2 - 1) + 2 * (i % 2) + 1)
                        ts(s_z[:, i % 2, :], ps[:, b, 0:384], SB_D ** -0.5, None, MUL).then_inc(drained[b], 1)
                        wait_drained(dve, ph, at)
                        dve.wait_ge(sb_ln, i + 1)
                        stt(s_sp[:, i % 2, :], s_z[:, i % 2, :], 0.0, s_e[:, i % 2, :], ALU.max, ADD).then_inc(sb_soft, 1)
                    if 1 <= i <= SB_H:
                        u = i - 1
                        at = 5 * (u // 2) + 2 * (u % 2) + 1
                        b = wait_filled(dve, ph, at)
                        tt(s_d[:, u % 2, :], s_z[:, u % 2, :], ps[:, b, 0:384], SUB).then_inc(drained[b], 1)
                    if i >= 3 and i % 2 == 1:
                        g = (i - 3) // 2
                        drain(ph, 5 * g + 4, s_o[:, g, :], lambda b: b[:, 0:T])

            def retention(l):
                ph = PLAN["ret_in", l]
                dve.wait_ge(rope_ready, 4)
                cos, sin = rope[:, 2, :], rope[:, 3, :]
                for k in range(8):
                    b = wait_filled(dve, ph, k)
                    if k >= 2:
                        dve.wait_ge(ret_roped, k - 1)
                    for i in range(2):
                        half = ps[:, b, i * T:(i + 1) * T]
                        tt(r_ta[:, k % 2, i, :], half, cos, MUL)
                        last = tt(r_tb[:, k % 2, i, :], half, sin, MUL)
                    last.then_inc(drained[b], 1)
                s, n, _ = ph.piece(24)
                dve.wait_ge(piece_full[s], 16 * n)
                decay = ring[:, s, :]
                ph = PLAN["ret", l]
                for h in range(RET_H):
                    b = wait_filled(dve, ph, 3 * h)
                    tt(r_sc[:, h % 2, :], ps[:, b, 0:384], decay[:, h * 384:(h + 1) * 384], MUL).then_inc(drained[b], 1)
                    wait_drained(dve, ph, 12 + h)
                    link(v.reciprocal(stat[:, h, T:TC], stat[:, h, 0:T]))
                    for c in range(4 * h, 4 * h + 4):
                        stt(r_o[:, c, :], r_o[:, c, :], V("gn_g", c), stat[:, h, T:TC], MUL, MUL).then_inc(ret_normed, 1)

            def ffn(l):
                ph = PLAN["ffn_up", l]
                with dve.Fori(0, ph.turns) as turn:
                    for j in range(8):
                        wait_drained(dve, ph, j, turn)
                        r = pairs(f_r[:, j % 2, :])
                        tt(f_h[:, bass.ds(turn * 16 + 2 * j, 2), :], r, r, MUL).then_inc(hidden_ready, 1)

            def modulate(n):
                l, i = n // 2, n % 2
                dve.wait_ge(*((ln_ready, 8 * n) if n else (x_ready, 8 * 2 * DEPTH)))
                for c in range(DC):
                    shift = 3 * i * DC + c
                    ts(H[:, c, 0:T], X[:, c, 0:T], scale2[:, l, i, c, 0:1], mod2[:, l, shift, 0:1], MUL, ADD).then_inc(hm_dve, 1)

            def layer_norm(m, cols, y):
                l, i = m // 2, m % 2
                for c in range(DC):
                    b = wait_filled(dve, y, c)
                    dve.wait_ge(x_alpha, 8 * m + c + 1)
                    for n in range(cols // T):
                        at, gate = slice(n * T, (n + 1) * T), mod2[:, l, (3 * i + 2) * DC + c, n:n + 1]
                        last = stt(X[:, c, at], ps[:, b, at], gate, X[:, c, at], MUL, ADD)
                    last.then_inc(drained[b], 1)
                ph = PLAN["ln", m]
                wait_drained(dve, ph, 0)
                for c in range(0, DC, 2):
                    tt(X[:, c, 0:cols], X[:, c, 0:cols], MU[:, 0:cols], SUB).then_inc(xc_dve, 1)
                wait_drained(dve, ph, 1)
                link(v.reciprocal(RSTD[:, 0:cols], STD[:, 0:cols]))
                for c in range(DC):
                    stt(X[:, c, 0:cols], X[:, c, 0:cols], V("ln", (4 * l + 2 * i) * DC + c), RSTD[:, 0:cols], MUL, MUL)\
                        .then_inc(ln_scaled, 1)

            def fourier_gqa():
                ph = PLAN["ab_in", 0]

                def head(c):
                    return a_q[:, c, :] if c < GQ_H else a_k[:, c - GQ_H, :]

                for c in range(8):
                    drain(ph, 2 + c, head(c))
                for c in range(8):
                    wait_drained(dve, ph, 12 + c)
                    link(v.reciprocal(stat[:, 2 + c % 2, :], stat[:, c % 2, :]))
                    stt(head(c), head(c), V("qk_gain", c // GQ_H), stat[:, 2 + c % 2, :], MUL, MUL).then_inc(ab_normed, 1)
                for c in range(8):
                    b = wait_filled(dve, ph, 20 + c)
                    if c >= 2:
                        dve.wait_ge(ab_roped, c - 1)
                    tt(a_t[:, c % 2, :], ps[:, b, 0:T], ax_sin, MUL).then_inc(drained[b], 1)
                ph = PLAN["fnet", 0]
                for k in range(4):
                    drain(ph, k, a_ab[:, k, :])
                for cc in range(2):
                    drain(ph, 8 + cc, a_o[:, cc, :])
                dve.wait_ge(zeros_set, 1)
                attention(4, head_scale)

            def neighbours():
                ph = PLAN["na_in", 1]
                for k in range(5, 12, 2):
                    drain(ph, k, n_k[:, k - 4, :])
                for j in range(4):
                    drain(ph, 13 + 2 * j, n_v[:, 2:4, j * 256:(j + 1) * 256], pairs)
                link(v.memset(n_bm[:, :, T:TC], 0.0))
                for j in range(3):
                    s, n, _ = PLAN["att", 5].piece(j)
                    dve.wait_ge(piece_full[s], 16 * n)
                attention(5, head_scale)

            def route(l, nb):
                wait_drained(dve, PLAN["route", l], 0)
                for tb in range(nb):
                    sc, biased, rest, sel = (r[:, tb, :] for r in (e_sc, e_sb, e_rep, e_sel))
                    top, total, inv = route_s[:, 0:8], route_s[:, 8 + tb:9 + tb], route_s[:, 16 + tb:17 + tb]
                    link(tt(biased, sc, V("e_bias", l * EXPERTS, EXPERTS), ADD))
                    link(v.max(top, biased))
                    link(v.match_replace(rest, top, biased, NEG))
                    link(tt(sel, rest, biased, ALU.is_lt))
                    link(stt(e_w[:, tb, :], sc, 1.0, sel, MUL, MUL, accum_out=total))
                    link(v.reciprocal(inv, total))
                    link(ts(wts[:, tb, 0:EXPERTS], e_w[:, tb, :], inv, ROUTE_SCALE, MUL, MUL))
                link(v.memset(wts[:, :, EXPERTS:EXPERTS + 1], 1.0))

            def moe(l):
                nb = 4 - 2 * l
                route(l, nb)
                dve.wait_ge(acc_zeroed, l + 1)

                def gated(ph, k, e, turn=0):
                    n = 2 if l == 0 else 1
                    for i in range(n):
                        wait_drained(dve, ph, k + i, turn)
                        b = wait_filled(dve, ph, k + n + i, turn)
                        at = slice(i * TC, (i + 1) * TC)
                        tt(e_a[:, e % 2, at], e_sg[:, e % 2, at], ps[:, b, :], MUL).then_inc(drained[b], 1)

                def add(ph, k, e, turn=0):
                    for tb in range(nb):
                        for half in range(2):
                            b, n = ph.fill(k + 2 * tb + half, turn)
                            dve.wait_ge(drained[b], n - 1)
                            dve.wait_ge(filled[b], n)
                            acc = e_acc[:, tb, half * 512:(half + 1) * 512]
                            stt(acc, ps[:, b, :], wts[:, tb, e], acc, MUL, ADD).then_inc(drained[b], 1)

                gated(PLAN["moe_head", l], 0, 0)
                ph = PLAN["moe", l]
                per, nu = (12, 4) if l == 0 else (6, 2)
                with dve.Fori(0, ph.turns) as turn:
                    for k in range(8):
                        gated(ph, per * k, k + 1, turn)
                        add(ph, per * k + nu, bass.ds(turn * 8 + k, 1), turn)
                add(PLAN["moe_tail", l], 0, slice(EXPERTS, EXPERTS + 1))

            dve.wait_ge(consts_loaded, 48)
            rope_tables()
            for l in range(DEPTH):
                mods(l)
                pre_norm(2 * l)
                (mla, stick, retention)[l % 3](l)
                post_norm(2 * l, PLAN["mix_out", l])
                pre_norm(2 * l + 1)
                ffn(l)
                post_norm(2 * l + 1, PLAN["ffn_down", l])
            for l in range(DEPTH_2):
                cols = TC if l == 0 else T
                mods2(l)
                modulate(2 * l)
                (fourier_gqa, neighbours)[l]()
                layer_norm(2 * l, cols, PLAN["out2", l])
                modulate(2 * l + 1)
                moe(l)
                layer_norm(2 * l + 1, cols, PLAN["moe_turn", l])

        @block.gpsimd
        def _(pool):
            link = chained(pool, pool_step)
            g = nc.gpsimd
            MUL, ADD, SUB = ALU.mult, ALU.add, ALU.subtract
            g.memset(zeros[:], 0.0).then_inc(zeros_set, 1)

            def post_norm(s):
                if s:
                    pool.wait_ge(x_ready, 8 * s)
                else:
                    pool.wait_ge(x_loaded, 32)
                for c in range(DC):
                    pool.wait_ge(y_scaled, 8 * s + c + 1)
                    g.tensor_tensor(X[:, c, 0:T], X[:, c, 0:T], Y[:, c, :], ADD).then_inc(x_ready, 1)

            def attention(l):
                for i, unit in enumerate(attention_units(l)):
                    U, nk = UNIT0[l] + i, unit["nk"]
                    pool.wait_ge(att_rinv, U + 1)
                    g.tensor_scalar(att_p[:, i % 2, 0:nk], att_p[:, i % 2, 0:nk], att_stat[:, 2, U:U + 1], None, MUL)\
                        .then_inc(att_prob, 1)

            def mla(l):
                ph = PLAN["mla_up", l]
                pool.wait_ge(rope_ready, 4)
                cos = rope[:, 0, :]
                for k in range(2):
                    wait_drained(pool, ph, 14 + k)
                    for c in (2 * k, 2 * k + 1):
                        link(g.tensor_tensor(m_qp[:, c, :], m_qp[:, c, :], cos, MUL))
                    q = m_qp[:, 2 * k:2 * k + 2, :]
                    g.tensor_tensor(q, q, m_t2[:, 2 * k:2 * k + 2, :], ADD).then_inc(mla_rope, 1)
                attention(l)

            def stick(l):
                s, n, _ = PLAN["sb_in", l].piece(12)
                pool.wait_ge(piece_full[s], 16 * n)
                mask, guard = ring[:, s, 2 * P:2 * P + 384], ring[:, s, 2 * P + 384:2 * P + 768]
                for i in range(SB_H + 1):
                    if i < SB_H:
                        pool.wait_ge(sb_soft, i + 1)
                        g.tensor_tensor(s_sp[:, i % 2, :], s_sp[:, i % 2, :], mask, MUL).then_inc(sb_masked, 1)
                    if i >= 1:
                        u = i - 1
                        wait_drained(pool, PLAN["sb", l], 5 * (u // 2) + 2 * (u % 2) + 1)
                        g.tensor_tensor(s_d[:, u % 2, :], s_d[:, u % 2, :], guard, ADD).then_inc(sb_guarded, 1)

            def retention(l):
                ph = PLAN["ret_in", l]
                for k in range(8):
                    wait_drained(pool, ph, k)
                    dst = r_q if k < RET_H else r_k
                    h = k % RET_H
                    g.tensor_tensor(dst[:, 2 * h, :], r_ta[:, k % 2, 0, :], r_tb[:, k % 2, 1, :], SUB)
                    g.tensor_tensor(dst[:, 2 * h + 1, :], r_ta[:, k % 2, 1, :], r_tb[:, k % 2, 0, :], ADD).then_inc(ret_roped, 1)
                for h in range(RET_H):
                    pool.wait_ge(ret_normed, 4 * h + 4)
                    at = slice(4 * h, 4 * h + 4)
                    g.tensor_tensor(r_o[:, at, :], r_o[:, at, :], r_g[:, at, :], MUL).then_inc(ret_gated, 1)

            def modulate(n):
                l, i = n // 2, n % 2
                cols = TC if l == 0 else T
                pool.wait_ge(mod_ready, DEPTH + l + 1)
                pool.wait_ge(*((ln_ready, 8 * n) if n else (x_loaded, 32)))
                if n < 3:
                    for c in range(DC):
                        shift = 3 * i * DC + c
                        g.tensor_scalar(H[:, c, T:TC], X[:, c, T:TC], scale2[:, l, i, c, 1:2], mod2[:, l, shift, 1:2], MUL, ADD)\
                            .then_inc(hm_pool, 1)
                    pool.wait_ge(hm_pool, 8 * n + 8)
                for c in range(DC):
                    pool.wait_ge(hm_dve, 8 * n + c + 1)
                    g.tensor_scalar(X[:, c, 0:cols], X[:, c, 0:cols], DN_ALPHA, None, MUL).then_inc(x_alpha, 1)

            def layer_norm(m, cols):
                wait_drained(pool, PLAN["ln", m], 0)
                for c in range(1, DC, 2):
                    g.tensor_tensor(X[:, c, 0:cols], X[:, c, 0:cols], MU[:, 0:cols], SUB).then_inc(xc_pool, 1)

            def fourier_gqa():
                for c in range(8):
                    wait_drained(pool, PLAN["ab_in", 0], 20 + c)
                    q = a_q[:, c, 0:T] if c < GQ_H else a_k[:, c - GQ_H, 0:T]
                    link(g.tensor_tensor(q, q, ax_cos, MUL))
                    g.tensor_tensor(q, q, a_t[:, c % 2, :], ADD).then_inc(ab_roped, 1)
                attention(4)

            for l in range(DEPTH):
                if l % 3 == 0:
                    mla(l)
                elif l % 3 == 1:
                    stick(l)
                else:
                    retention(l)
                post_norm(2 * l)
                post_norm(2 * l + 1)
            for l in range(DEPTH_2):
                cols = TC if l == 0 else T
                modulate(2 * l)
                if l == 0:
                    fourier_gqa()
                else:
                    attention(5)
                layer_norm(2 * l, cols)
                modulate(2 * l + 1)
                g.memset(e_acc, 0.0).then_inc(acc_zeroed, 1)
                layer_norm(2 * l + 1, cols)


def columns(a):
    return np.asarray(a).reshape(-1, P).T


def chunked(w):
    w = np.asarray(w)
    return w.reshape(-1, P, w.shape[1]).transpose(1, 0, 2)


def by_columns(w, n):
    c = chunked(w)
    return [c[:, :, i:i + n].reshape(P, -1) for i in range(0, c.shape[2], n)]


def shape_constants():
    f64 = np.float64
    k, q = np.arange(P)[:, None], np.arange(P)[None, :]
    rot = np.zeros((P, P))
    for m in range(P):
        rot[(m + 32, m) if m % 64 < 32 else (m - 32, m)] = -1.0 if m % 64 < 32 else 1.0
    t = np.arange(T)
    inv = 10000.0 ** (-(2.0 / 64) * (np.arange(P) % 32))
    ang = (np.where(np.arange(P)[:, None] < 64, t // GRID_W, t % GRID_W).astype(np.float32)
           * inv.astype(np.float32)[:, None]).astype(f64)
    tab = np.concatenate([np.eye(P), np.full((P, P), 1.0 / D), rot, np.cos(ang), np.sin(ang)], 1)
    inv_freq = np.stack([10000.0 ** (-(2.0 * (np.arange(P) % 32)) / MLA_ROPE), 10000.0 ** (-(2.0 * np.arange(P)) / RET_K)], 1)
    parity = np.stack([np.arange(P) < 64, np.arange(P) >= 64], 1)
    causal = np.where(q <= k, 0.0, NEG)
    mla_mask = np.concatenate([causal, np.zeros((P, P)), causal], 1)
    strict = (k < q).astype(f64)
    sb_mask = np.concatenate([strict, np.ones((P, P)), strict], 1)
    sb = np.concatenate([(k >= q).astype(f64), np.ones((P, P)), sb_mask, (sb_mask - 1.0) * -NEG], 1)
    decay = []
    for h in range(RET_H):
        log_gamma = np.log(1.0 - 2.0 ** (-5.0 - h))
        near = np.where(q >= k, np.exp(np.maximum(q - k, 0) * log_gamma), 0.0) * RET_K ** -0.5
        far = np.exp((q + P - k) * log_gamma) * RET_K ** -0.5
        decay += [near, far, near]
    n = np.arange(T)
    tok = 2 * np.pi * np.outer(n, n) / T
    ch = 2 * np.pi * np.outer(np.arange(64), np.arange(64)) / 64
    norm = 1.0 / np.sqrt(T * 64.0)
    two = np.eye(2)
    dft = np.concatenate([chunked(np.cos(tok)).reshape(P, -1), chunked(np.sin(tok)).reshape(P, -1),
                          np.kron(two, np.cos(ch) * norm), np.kron(two, -np.sin(ch) * norm)], 1)
    col = np.arange(GRID_W)
    start = np.clip(col - NA_KW // 2, 0, GRID_W - NA_KW)
    inside = (col[None, :] >= start[:, None]) & (col[None, :] < start[:, None] + NA_KW)
    window = np.where(np.tile(inside, (T // GRID_W, T // GRID_W)), 0.0, NEG)
    row = np.arange(T) // GRID_W
    cc = np.arange(T) % GRID_W
    dr = np.clip(row[None, :] - row[:, None] + 7, 0, 14)
    dc = np.clip(cc[None, :] - cc[:, None] + NA_KW - 1, 0, 2 * NA_KW - 2)
    f = np.float32
    return dict(tab=tab.astype(f), inv_freq=inv_freq.astype(f), parity=parity.astype(f), mla_mask=mla_mask.astype(f),
                sb=sb.astype(f), decay=np.concatenate(decay, 1).astype(f), dft=dft.astype(f),
                window=chunked(window.astype(f)).reshape(P, -1), dr=dr, dc=dc)


def pieces_of(inp, con):
    def experts(l):
        gate, up, down = (inp[n][l] for n in ("moe_w_gate_2", "moe_w_up_2", "moe_w_down_2"))
        gates = list(gate) + [inp["sh_w_gate_2"][l]]
        ups = list(up) + [inp["sh_w_up_2"][l]]
        yield chunked(gates[0]).reshape(P, -1)
        yield chunked(ups[0]).reshape(P, -1)
        for e in range(EXPERTS):
            yield chunked(gates[e + 1]).reshape(P, -1)
            yield chunked(ups[e + 1]).reshape(P, -1)
            yield chunked(down[e]).reshape(P, -1)
        yield chunked(inp["sh_w_down_2"][l]).reshape(P, -1)

    for l in range(DEPTH):
        yield from by_columns(inp["ada_w"][l], 256)
        j = l // 3
        if l % 3 == 0:
            w = inp["mla_w_in"][j]
            yield from by_columns(np.concatenate([w, w[:, 384:448]], 1), 256)
            up = inp["mla_w_q_up"][j].reshape(256, MLA_H, MLA_NOPE + MLA_ROPE)
            yield chunked(up[:, :, 0:MLA_NOPE].reshape(256, -1)).reshape(P, -1)
            up_kv = inp["mla_w_kv_up"][j].reshape(P, MLA_H, 2, MLA_V)
            yield up_kv.transpose(0, 2, 1, 3).reshape(P, -1)
            pe = chunked(up[:, :, MLA_NOPE:].reshape(256, -1)).reshape(P, -1)
            yield np.concatenate([pe, np.zeros((P, P), np.float32), con["mla_mask"]], 1)
            yield from by_columns(inp["mla_w_out"][j], 256)
        elif l % 3 == 1:
            yield from by_columns(inp["sb_w_in"][j], 256)
            yield con["sb"]
            yield from by_columns(inp["sb_w_out"][j], 256)
        else:
            yield from by_columns(inp["ret_w_in"][j], 256)
            yield con["decay"]
            yield from by_columns(inp["ret_w_out"][j], P)
        yield from by_columns(inp["ffn_w1"][l], 256)
        for m in by_columns(inp["ffn_w2"][l], P):
            yield m[:, 0:PIECE]
            yield m[:, PIECE:]
    for l in range(DEPTH_2):
        yield from by_columns(inp["w_mod_2"][l], 256)
        if l == 0:
            yield from by_columns(inp["ab_w_in_2"][0], 256)
            fnet = inp["ab_w_fnet_2"][0]
            blocks = np.zeros((P, 2, P), np.float32)
            for g in range(4):
                blocks[(g % 2) * 64:(g % 2 + 1) * 64, g // 2, (g % 2) * 64:(g % 2 + 1) * 64] = fnet[g]
            yield np.concatenate([con["dft"], blocks.reshape(P, -1)], 1)
            yield from by_columns(inp["ab_w_out_2"][0], 256)
        else:
            yield from by_columns(inp["na_w_in_2"][0], 256)
            bias = inp["na_rpb_2"][0][:, con["dr"], con["dc"]]
            for qb in range(2):
                yield bias[:, qb * P:(qb + 1) * P, :].transpose(1, 0, 2).reshape(P, -1)
            yield con["window"]
            yield from by_columns(inp["na_w_out_2"][0], 256)
        yield chunked(inp["moe_w_router_2"][l]).reshape(P, -1)
        yield from experts(l)


def kernel(**inputs):
    import concourse.bacc as bacc
    from concourse.bass_utils import run_bass_kernel_spmd

    inp = {k: np.asarray(a) for k, a in inputs.items()}
    con = shape_constants()
    stream = np.zeros((STREAM, P, PIECE), np.float32)
    n = 0
    for piece in pieces_of(inp, con):
        stream[n, :, 0:piece.shape[1]] = piece
        n += 1
    assert n == PIECES, (n, PIECES)
    vec = np.zeros((P, NVEC), np.float32)
    conds = np.stack([columns(inp["c"][0]), columns(inp["c_2"][0]), columns(inp["c_ctx_2"])], 2)
    ln = [inp[k][l] for l in range(DEPTH_2) for k in ("ln1_g_2", "ln1_b_2", "ln2_g_2", "ln2_b_2")]
    for name, a in (
        ("ada_b", columns(inp["ada_b"])), ("norm_g", columns(inp["norm_g"])), ("b_mod", columns(inp["b_mod_2"])),
        ("ln", columns(np.stack(ln))), ("q_norm", columns(inp["mla_q_norm"])), ("kv_norm", columns(inp["mla_kv_norm"])),
        ("gn_g", columns(inp["ret_gn_g"])), ("qk_gain", columns(np.stack([inp["ab_q_norm_2"][0], inp["ab_k_norm_2"][0]]))),
        ("conds", conds.reshape(P, -1)), ("e_bias", np.broadcast_to(inp["moe_bias_2"].reshape(1, -1), (P, DEPTH_2 * EXPERTS))),
        ("inv_freq", con["inv_freq"]), ("parity", con["parity"]), ("eps", np.full((P, 1), EPS, np.float32)),
    ):
        vec[:, VEC[name][0]:VEC[name][1]] = a
    arrays = {
        "stream": stream, "vectors": vec, "tables": con["tab"],
        "latent": np.ascontiguousarray(inp["x"][0].reshape(T, DC, P).transpose(2, 1, 0)),
        "context": np.ascontiguousarray(inp["ctx_2"][0].reshape(T, DC, P).transpose(2, 1, 0)),
        "positions": np.ascontiguousarray(np.broadcast_to(inp["positions"][0], (P, T))),
    }
    nc = bacc.Bacc("TRN2", target_bir_lowering=False, num_devices=1)
    args = [nc.dram_tensor(k + "_in", a.shape, mybir.dt.from_np(a.dtype), kind="ExternalInput").ap() for k, a in arrays.items()]
    out = nc.dram_tensor("out", (P, DC, T), F32, kind="ExternalOutput").ap()
    build(nc, *args, out)
    r = run_bass_kernel_spmd(nc, [{k + "_in": a for k, a in arrays.items()}], core_ids=[0])
    got = r.results[0]["out"]
    return np.ascontiguousarray(got.transpose(2, 1, 0).reshape(1, T, D))
```

```python
from contextlib import ExitStack

import numpy as np
import concourse.bass as bass
import concourse.mybir as mybir

P = 128
D = 1024
DC = D // P
T = 256
TC = 512
FF = 4096
DEPTH, DEPTH_2 = 4, 2
MODS = 6 * DC
EPS = 1e-6
NEG = -1e30
MLA_H, MLA_NOPE, MLA_ROPE, MLA_V = 8, 128, 64, 128
SB_H, SB_D = 16, 64
RET_H, RET_K, RET_V = 4, 256, 512
GQ_H, GKV_H, FN = 6, 2, 256
NA_H, NA_KW, GRID_W = 8, 16, 64
EXPERTS, TOP_K, EXP_D, ROUTE_SCALE = 64, 8, 256, 2.5
DN_ALPHA = (2 * DEPTH_2) ** 0.25
BANKS = 8
SLOTS = 8
PIECE = 2048

F32 = mybir.dt.float32
I32 = mybir.dt.int32
BF16 = mybir.dt.bfloat16
ACT = mybir.ActivationFunctionType
ALU = mybir.AluOpType
AX = mybir.AxisListType

VEC = {}
_at = 0
for _name, _n in (("ada_b", DEPTH * MODS), ("norm_g", DEPTH * 4 * DC), ("b_mod", DEPTH_2 * MODS),
                  ("ln", DEPTH_2 * 4 * DC), ("q_norm", 4), ("kv_norm", 2), ("gn_g", 16), ("qk_gain", 2),
                  ("conds", 3 * DC), ("e_bias", DEPTH_2 * EXPERTS), ("inv_freq", 2), ("parity", 2),
                  ("eps", 1), ("slot", 3)):
    VEC[_name] = (_at, _at + _n)
    _at += _n
NVEC = _at
TAB_W = 6 * P + 2 * T


class Phase:

    def __init__(self, banks, pieces, turns=1, fills=None):
        self.banks, self.pieces, self.turns, self.fills = banks, pieces, turns, fills or turns

    def fill(self, k, turn=0):
        b = self.banks[k]
        return b, self.base[b] + self.banks[:k].count(b) + 1 + self.banks.count(b) * turn

    def piece(self, j, turn=0):
        p = self.first + j
        return p % SLOTS, p // SLOTS + 1 + (self.pieces // SLOTS) * turn, p


def attention_banks(units):
    return [b for u in range(units) for b in (u % 2, 2 + u % 2, 4 + u % 2)]


def plan():
    order = {}
    for l in range(DEPTH):
        if l == 0:
            order["mod", 0] = Phase([6, 5] * 3, 0)
        order["norm", 4 * l] = Phase([7], 0)
        if l % 3 == 0:
            order["mla_in", l] = Phase([0, 1, 2, 3], 2)
            if l == 0:
                order["mod_in", l] = Phase([6], 0)
            order["mla_up", l] = Phase([4, 5, 6, 7, 0, 1, 2, 3, 4, 5, 6, 7, 0, 1, 2, 3, 4], 3)
            if l == 0:
                order["mod_up", l] = Phase([6, 7], 0)
            order["att", l] = Phase(attention_banks(2 * MLA_H), 0)
            if l == 0:
                order["mod_att", l] = Phase([6, 7, 6], 0)
            order["mix_out", l] = Phase([0, 1, 2, 3], 4)
        elif l % 3 == 1:
            order["sb_in", l] = Phase([0, 1, 2, 3, 4, 5, 6, 7, 0, 1, 2, 3], 13)
            order["sb", l] = Phase([b for h in range(SB_H) for b in
                                    ([h % 2, 2 + h % 2] + ([4 + h // 2 % 2] if h % 2 else []))], 0)
            order["mix_out", l] = Phase([0, 1, 2, 3], 4)
        else:
            order["ret_in", l] = Phase([0, 1, 2, 3, 4, 5, 6, 7] * 3, 25)
            order["ret", l] = Phase([b for h in range(RET_H) for b in (h % 2, 2, 3)] + [4, 5, 4, 5], 0)
            order["mix_out", l] = Phase([0, 1, 2, 3], 8)
        order["norm", 4 * l + 1] = Phase([7], 0)
        order["norm", 4 * l + 2] = Phase([7], 0)
        mod_banks = [6] if l < DEPTH - 1 else [6, 5]
        extra = [6, 5] if l < DEPTH - 1 else []
        order["ffn_up", l] = Phase([b for i in range(4) for b in [2 * i % 4, 2 * i % 4 + 1] + mod_banks], 8, 2)
        order["ffn_down", l] = Phase([b for k in range(2) for b in [k] + mod_banks + extra], 8, 2)
        order["norm", 4 * l + 3] = Phase([7], 0)
    for l in range(DEPTH_2):
        if l == 0:
            order["ab_in", l] = Phase([0, 1] + [2, 3, 4, 5, 6, 7, 0, 1] + [2, 3] + [4, 5, 6, 7] * 4, 6)
            order["fnet", l] = Phase([0, 1, 2, 3, 4, 5, 6, 7, 0, 1], 1)
            order["att", 4] = Phase(attention_banks(4 * GQ_H), 0)
            order["out2", l] = Phase(list(range(8)), 4)
        else:
            order["na_in", l] = Phase([0, 1, 2, 3] + [4, 5, 6, 7, 0, 1, 2, 3] + [4, 5, 6, 7] * 2, 12)
            order["att", 5] = Phase(attention_banks(2 * NA_H), 3)
            order["out2", l] = Phase(list(range(8)), 4)
        order["ln", 2 * l] = Phase([6, 7], 0)
        order["route", l] = Phase([0], 1)
        nb = (TC, T)[l] // P
        order["moe_head", l] = Phase([1, 6, 7, 1, 6, 7, 1, 6][:2 * nb] + [2, 3, 4, 5] + [0] + [6, 7, 0, 1, 3, 4, 5, 6][:2 * nb], 3)
        order["moe", l] = Phase([0, 1, 2, 3, 4, 6, 7], 3 * EXPERTS, fills=EXPERTS)
        order["moe_turn", l] = Phase(list(range(8)), 0)
        order["ln", 2 * l + 1] = Phase([6, 7], 0)
    base, first = [0] * BANKS, 0
    for ph in order.values():
        ph.base, ph.first = list(base), first
        for b in ph.banks:
            base[b] += ph.fills
        first += ph.pieces * ph.turns
        assert ph.turns == 1 or ph.pieces % SLOTS == 0
    return order, first


def mod_plan():
    stretches = {("start", 0): [("mod", 0)] * 6, ("mla", 0): [("mod", 0)] * 6}
    for l in range(DEPTH):
        nxt = ("mod", l + 1) if l < DEPTH - 1 else ("mod2", 0)
        stretches["up", l] = [nxt] * 4
        stretches["down", l] = [nxt, ("mod2", 1)] * 2 if l < DEPTH - 1 else [nxt] * 2
    piece = step = 0
    done, out = {}, {}
    for key, jobs in stretches.items():
        n_turns = 1 if key[0] in ("start", "mla") else 2
        steps = [8 * (1 if job[0] == "mod" else 2) for job in jobs]
        first = {}
        for job in jobs:
            first[job] = done.get(job, 0)
        blocks = []
        seen = {}
        for job in jobs:
            blocks.append((first[job] + seen.get(job, 0), jobs.count(job)))
            seen[job] = seen.get(job, 0) + 1
        for job in seen:
            done[job] = first[job] + seen[job] * n_turns
        out[key] = dict(jobs=jobs, steps=steps, blocks=blocks, turns=n_turns, piece=piece, step=step)
        piece += 2 * len(jobs) * n_turns
        step += sum(steps) * n_turns
    assert all(n == 12 for n in done.values())
    return out, piece


ROWS_T, SLOT, HIDDEN_T, HIDDEN, OUTPUT = 0, 2, 3, 4, 5
FAR = 2 * TC
TURN = 8


def expert_piece(ph, turn, k, part):
    j = 3 * k + (-1, 0, 4)[part]
    if isinstance(turn, int) and turn * TURN + k == 0 and part < 2:
        j = part
    if isinstance(turn, int) and turn * TURN + k == EXPERTS - 1 and part == 2:
        j -= 2
    p = ph.first + j
    return p % SLOTS, turn * (3 * TURN // SLOTS) + (p // SLOTS + 1), p


def spare_blocks(rows):
    return (rows * TOP_K - 1) // P


MOD_PLAN, MOD_PIECES = mod_plan()
PLAN, PIECES = plan()
STREAM = -(-PIECES // SLOTS) * SLOTS
UNIT0 = {0: 0, 3: 16, 4: 32, 5: 56}
UNITS = 72


def build(nc, stream, mod_stream, vec_d, tab_d, x_d, ctx_d, pos_d, out_d, h2_d, ff_d):
    ctx = ExitStack()
    with ctx:
        def sb(name, shape, dt=F32):
            return ctx.enter_context(nc.sbuf_tensor(name, shape, dt))

        def sem(name):
            return ctx.enter_context(nc.semaphore(name))

        ring = sb("ring", [P, SLOTS, PIECE])
        X = sb("X", [P, DC, TC])
        H = sb("H", [P, DC, TC])
        YS = sb("YS", [P, DC * TC])
        arena = sb("arena", [P, 16384])
        vec = sb("vec", [P, NVEC])
        tab = sb("tab", [P, TAB_W])
        pos = sb("pos", [P, T], I32)
        rope = sb("rope", [P, 4, T])
        zeros = sb("zeros", [P, TC])
        stat = sb("stat", [P, 4, TC])
        mod = sb("mod", [P, DEPTH, MODS])
        gains = sb("gains", [P, DEPTH, 4, DC])
        mod2 = sb("mod2", [P, DEPTH_2, MODS, 2])
        scale2 = sb("scale2", [P, DEPTH_2, 2, DC, 2])
        cond = sb("cond", [P, DC, 3])
        att_stat = sb("att_stat", [P, 3, UNITS])
        route_s = sb("route_s", [P, 32])
        onehot = sb("onehot", [P, 2, 4, P], BF16)
        slot_vals = sb("slot_vals", [P, 4, EXPERTS * 6], BF16)
        slot_rec = sb("slot_rec", [P, TURN, 2])
        slot_row = sb("slot_row", [P, TURN], I32)
        spare_int = sb("spare_int", [P, 5], I32)
        ps = ctx.enter_context(nc.psum_tensor("ps", [P, BANKS, TC], F32))

        def V(name, i=0, n=1):
            a = VEC[name][0] + i
            return vec[:, a:a + n]

        ident, ones_d, rot = tab[:, 0:P], tab[:, P:2 * P], tab[:, 2 * P:3 * P]
        ax_cos, ax_sin = tab[:, 3 * P:3 * P + T], tab[:, 3 * P + T:3 * P + 2 * T]
        tri, ones, count1 = (tab[:, i * P + 2 * T:(i + 1) * P + 2 * T] for i in range(3, 6))
        Y = YS[:, 0:DC * T].rearrange("p (c t) -> p c t", c=DC)
        SQ = YS[:, DC * T:2 * DC * T].rearrange("p (c t) -> p c t", c=DC)
        SQ2 = YS[:, :].rearrange("p (c t) -> p c t", c=DC)
        MU, STD, RSTD = stat[:, 0, :], stat[:, 1, :], stat[:, 2, :]

        def region(at, *shape):
            n = int(np.prod(shape))
            v = arena[:, at:at + n]
            if len(shape) == 2:
                v = v.rearrange("p (a b) -> p a b", a=shape[0])
            elif len(shape) == 3:
                v = v.rearrange("p (a b c) -> p a b c", a=shape[0], b=shape[1])
            return v

        piece_full = [sem(f"piece_full{s}") for s in range(SLOTS)]
        piece_used = [sem(f"piece_used{s}") for s in range(SLOTS)]
        filled = [sem(f"filled{b}") for b in range(BANKS)]
        drained = [sem(f"drained{b}") for b in range(BANKS)]
        consts_loaded = sem("consts_loaded")
        x_loaded = sem("x_loaded")
        ctx_loaded = sem("ctx_loaded")
        zeros_set = sem("zeros_set")
        cond_ready = sem("cond_ready")
        rope_reduced = sem("rope_reduced")
        rope_ready = sem("rope_ready")
        dve_step = sem("dve_step")
        act_step = sem("act_step")
        pool_step = sem("pool_step")
        mod_ready = sem("mod_ready")
        mod_first_full = [sem(f"mod_first_full{s}") for s in range(6)]
        mod_mla_full = [sem(f"mod_mla_full{s}") for s in range(2)]
        mod_full = [sem(f"mod_full{s}") for s in range(2)]
        mod_step = sem("mod_step")
        mod_added = sem("mod_added")
        sq_dve = sem("sq_dve")
        sq_act = sem("sq_act")
        h_scaled = sem("h_scaled")
        h_ready = sem("h_ready")
        y_scaled = sem("y_scaled")
        x_ready = sem("x_ready")
        x_added = sem("x_added")
        hidden_ready = sem("hidden_ready")
        mla_sq = sem("mla_sq")
        mla_lat = sem("mla_lat")
        mla_rope = sem("mla_rope")
        kpe_ready = sem("kpe_ready")
        att_exp = sem("att_exp")
        att_rinv = sem("att_rinv")
        att_prob = sem("att_prob")
        sb_neg = sem("sb_neg")
        sb_ln = sem("sb_ln")
        sb_soft = sem("sb_soft")
        sb_masked = sem("sb_masked")
        sb_guarded = sem("sb_guarded")
        sb_prob = sem("sb_prob")
        ret_part = sem("ret_part")
        ret_roped = sem("ret_roped")
        ret_sq = sem("ret_sq")
        ret_normed = sem("ret_normed")
        ret_gated = sem("ret_gated")
        hm_dve = sem("hm_dve")
        hm_pool = sem("hm_pool")
        x_alpha = sem("x_alpha")
        xc_dve = sem("xc_dve")
        xc_pool = sem("xc_pool")
        ln_sq = sem("ln_sq")
        ln_scaled = sem("ln_scaled")
        ln_ready = sem("ln_ready")
        ab_sq = sem("ab_sq")
        ab_normed = sem("ab_normed")
        ab_roped = sem("ab_roped")
        routed = sem("routed")
        slot_consts = sem("slot_consts")
        h2_stored = sem("h2_stored")
        ff_set = sem("ff_set")
        onehot_ready = sem("onehot_ready")
        slot_part = sem("slot_part")
        gathered = [sem(f"gathered{i}") for i in range(2)]
        rows_due = sem("rows_due")
        sum_due = sem("sum_due")
        expert_silu = sem("expert_silu")
        scattered = sem("scattered")
        ff_loaded = sem("ff_loaded")
        spares_counted = sem("spares_counted")
        spare = {n: [sem(f"spare_{n}{l}") for l in range(DEPTH_2)] for n in (
            "step", "picked", "weights", "onehot", "slots", "recorded", "rows", "rows_t", "x_t", "hidden", "silu", "gated",
            "hidden_t", "h_t", "output", "scaled", "added")}
        stored = sem("stored")

        def wait_filled(eng, ph, k, turn=0):
            b, n = ph.fill(k, turn)
            eng.wait_ge(filled[b], n)
            return b

        def wait_drained(eng, ph, k, turn=0):
            b, n = ph.fill(k, turn)
            eng.wait_ge(drained[b], n)

        def chained(eng, done):
            count = [0]

            def link(ins):
                count[0] += 1
                ins.then_inc(done, 1)
                eng.wait_ge(done, count[0])
            return link

        m_qlat, m_klat, m_kpe = region(0, 2, T), region(512, T), region(768, T)
        m_qn, m_qp, m_kn = region(1024, 8, T), region(3072, 4, T), region(4096, 8, T)
        m_v, m_kpm, m_o = region(6144, 2, D), region(8192, 2, T), region(8704, 8, T)
        m_t1, m_t2, m_sq = region(10752, 4, T), region(11776, 4, T), region(10752, 3, T)
        att_p, att_pt = region(12800, 4, TC), region(14848, 2, TC)
        att_s = {l: region(10752, 4, TC) for l in (0, 3, 4)}
        att_s[5] = YS[:, 2 * TC:6 * TC].rearrange("p (i t) -> p i t", i=4)

        s_q, s_k, s_v, s_o = region(0, 8, T), region(2048, 8, T), region(4096, 2, D), region(6144, 8, T)
        s_e, s_z, s_sp, s_d = (region(8192 + 1536 * i, 4, 384) for i in range(4))

        r_q, r_k, r_v = region(0, 8, T), region(2048, 8, T), region(4096, 2, 2 * D)
        r_g, r_o = region(8192, 16, T), region(12288, 16, T)
        r_ta = YS[:, 0:1024].rearrange("p (i c t) -> p i c t", i=2, c=2)
        r_tb = YS[:, 1024:2048].rearrange("p (i c t) -> p i c t", i=2, c=2)
        r_sc = YS[:, 2048:2816].rearrange("p (i t) -> p i t", i=2)
        r_sq = [YS[:, n:n + 1024].rearrange("p (c t) -> p c t", c=4) for n in (2816, 0)]

        a_f, a_q, a_k, a_v = region(0, 4, FN), region(1024, 6, TC), region(4096, 2, TC), region(5120, 4, FN)
        a_o, a_t = region(6144, 8, TC), region(10240, 2, T)
        a_ab, a_fr = region(12800, 4, 2 * T), region(14848, 2, TC)

        n_q, n_k, n_v = region(0, 8, T), region(2048, 8, TC), region(6144, 4, D)
        n_o = region(10240, 8, T)
        n_bm = YS[:, 0:2 * TC].rearrange("p (i t) -> p i t", i=2)

        f_h, f_r = region(0, 32, T), region(8192, 2, TC)
        mod_w, mod_first, mod_mla = region(9216, 2, 4, TC), region(0, 6, 4, TC), YS[:, :].rearrange("p (h c n) -> p h c n", h=2, c=4)
        mod_acc, mod_acc_mla = region(13312, 2, 2, TC), [stat[:, 0, :], stat[:, 3, :]]
        mod_sum = route_s[:, 0:8].rearrange("p (n t) -> p n t", n=2)
        e_acc, sh_g, sh_h = region(0, 4, D), region(4096, 2, TC), region(5120, 2, TC)
        e_sc, e_sb, e_rep, e_sel, e_w, wts, rank = (region(6144 + 256 * i, 4, EXPERTS) for i in range(7))
        e_x, e_xt, e_g, e_h = region(7936, 2, D), region(9984, 2, DC, P), region(12032, 2, EXP_D), region(12544, 2, EXP_D)
        e_ht, e_y = region(13056, 2, P), region(13312, 2, D)
        sp_w, sp_hot = region(0, 3, PIECE), region(15360, 4, P)
        sp_tokens, sp_blocks, sp_sum0, sp_sum1, sp_mask, sp_rest, sp_ones = (region(15872 + EXPERTS * i, EXPERTS) for i in range(7))
        sp_col = region(16320, 64)
        h2_rows = YS[:, :].rearrange("p (a n) -> p a n", a=4)

        mla_scale = float((MLA_NOPE + MLA_ROPE) ** -0.5)
        head_scale = float(P ** -0.5)

        def slot(ph, j, turn=0):
            return ring[:, ph.piece(j, turn)[0], :]

        def attention_units(l):
            units = []
            if l in (0, 3):
                mask = slot(PLAN["mla_up", l], 2)[:, 1152:1536]
                for h in range(MLA_H):
                    for qb in range(2):
                        nk, at = (P, 0) if qb == 0 else (T, P)
                        qs = slice(qb * P, qb * P + P)
                        units.append(dict(
                            score=[(m_qn[:, h, qs], m_kn[:, h, 0:nk]), (m_qp[:, h // 2, qs], m_kpm[:, h % 2, 0:nk])],
                            mask=mask[:, at:at + nk], nk=nk, bias=None,
                            v=[m_v[:, kb, h * P:(h + 1) * P] for kb in range(nk // P)], o=m_o[:, h, qs]))
            elif l == 4:
                for qb in range(4):
                    for h in range(GQ_H):
                        k0 = 0 if qb < 2 else T
                        g = h // (GQ_H // GKV_H)
                        qs = slice(qb * P, qb * P + P)
                        units.append(dict(
                            score=[(a_q[:, h, qs], a_k[:, g, k0:TC])], mask=zeros[:, k0:TC], nk=TC - k0, bias=None,
                            v=[a_v[:, kb, g * P:(g + 1) * P] for kb in range(k0 // P, 4)], o=a_o[:, 2 + h, qs]))
            else:
                for h in range(NA_H):
                    for qb in range(2):
                        qs = slice(qb * P, qb * P + P)
                        ph = PLAN["att", 5]
                        units.append(dict(
                            score=[(n_q[:, h, qs], n_k[:, h, :])], mask=None, nk=TC,
                            bias=(slot(ph, qb)[:, h * T:(h + 1) * T], slot(ph, 2)[:, qb * T:(qb + 1) * T]),
                            v=[n_v[:, kb, h * P:(h + 1) * P] for kb in range(4)], o=n_o[:, h, qs]))
            return units

        def turns(eng, ph, body, peel):
            if peel:
                body(0)
            with eng.Fori(1 if peel else 0, ph.turns) as turn:
                body(turn)

        def expert(turn, k):
            return turn * TURN + k

        def lacks(turn, k):
            return isinstance(turn, int) and turn * TURN + k >= EXPERTS

        def wait_past(eng, signal, n):
            if not isinstance(n, int) or n > 0:
                eng.wait_ge(signal, n)

        def expert_turns(eng, l, step):
            if l == 0:
                for k in range(TURN):
                    step(0, k)
            with eng.Fori(1 if l == 0 else 0, EXPERTS // TURN - 1) as turn:
                for k in range(TURN):
                    step(turn, k)
            for k in range(TURN):
                step(EXPERTS // TURN - 1, k)

        def spare_turns(eng, l, body):
            eng.wait_ge(spares_counted, l + 1)
            most = spare_blocks((TC, T)[l])
            n = eng.value_load(spare_int[0:1, 4:5], min_val=0, max_val=most)
            with eng.Fori(0, most) as i:
                with eng.If(i < n):
                    body(i)

        def mod_piece_at(key, i, half, turn):
            before = MOD_PLAN[key]["piece"] // 2
            if key[0] == "start":
                n = 2 * i + half
                return mod_first[:, n % 6, :, :], mod_first_full[n % 6], 16 * (n // 6 + 1)
            if key[0] == "mla":
                return mod_mla[:, half, :, :], mod_mla_full[half], 16 * (i + 1)
            n = turn * len(MOD_PLAN[key]["jobs"]) + (before - MOD_PLAN["up", 0]["piece"] // 2 + i + 1)
            return mod_w[:, half, :, :], mod_full[half], n * 16

        def mod_acc_of(key, i, n):
            return mod_acc_mla[i % 2] if key[0] == "mla" else mod_acc[:, i % 2, n, :]

        def mod_steps(key, i, turn):
            m = MOD_PLAN[key]
            return turn * sum(m["steps"]) + (m["step"] + sum(m["steps"][:i]))

        def mod_adds(key, i, turn):
            m = MOD_PLAN[key]
            return turn * (sum(m["steps"]) // 8) + (m["step"] + sum(m["steps"][:i])) // 8

        def mod_conds(key, i):
            return [0] if MOD_PLAN[key]["jobs"][i][0] == "mod" else [1, 2]

        block = ctx.enter_context(nc.Block())

        @block.sync
        def _(sp):
            def first(s):
                sp.dma_start(ring[:, s, :], stream[s]).then_inc(piece_full[s], 16)

            def mods(key, i, half):
                out, full, _ = mod_piece_at(key, i, half, 0)
                sp.dma_start(out, mod_stream[MOD_PLAN[key]["piece"] + 2 * i + half].rearrange("p (c n) -> p c n", c=4)).then_inc(full, 16)

            for n in range(12):
                if n >= 6:
                    sp.wait_ge(mod_step, 4 * (n - 5))
                mods(("start", 0), n // 2, n % 2)
                if n == 8:
                    first(0)
            for s in range(1, SLOTS):
                first(s)
            wait_filled(sp, PLAN["norm", 0], 0)
            for n in range(12):
                if n >= 2:
                    sp.wait_ge(mod_step, 48 + 4 * (n - 1))
                mods(("mla", 0), n // 2, n % 2)
            sp.dma_start(X[:, :, T:TC], ctx_d).then_inc(ctx_loaded, 16)
            with sp.Fori(1, STREAM // SLOTS) as i:
                for s in range(SLOTS):
                    sp.wait_ge(piece_used[s], i)
                    sp.dma_start(ring[:, s, :], stream[bass.ds(i * SLOTS + s, 1)].rearrange("a p n -> p (a n)"))\
                        .then_inc(piece_full[s], 16)
            sp.wait_ge(ln_ready, 4 * DC)
            sp.dma_start(out_d, X[:, :, 0:T]).then_inc(stored, 16)
            sp.wait_ge(stored, 16)
            for s in range(SLOTS):
                sp.wait_ge(piece_full[s], 16 * (STREAM // SLOTS))

        @block.tensor
        def _(pe):
            mm = nc.tensor.matmul

            def take(ph, j, turn=0):
                s, n, p = ph.piece(j, turn)
                pe.wait_ge(piece_full[s], n * 16)
                return ring[:, s, :], None if p == 0 and isinstance(turn, int) and turn == 0 else piece_used[(p - 1) % SLOTS]

            def bank(ph, k, turn=0):
                b, n = ph.fill(k, turn)
                if not isinstance(n, int) or n > 1:
                    pe.wait_ge(drained[b], n - 1)
                return ps[:, b, :], filled[b]

            def products(out, pairs, filled_sem=None, used=None):
                for i, (lhs, rhs) in enumerate(pairs):
                    m = mm(out, lhs, rhs, start=(i == 0), stop=(i == len(pairs) - 1))
                    if i == 0 and used is not None:
                        m.then_inc(used, 1)
                if filled_sem is not None:
                    m.then_inc(filled_sem, 1)

            def mod_columns(ph, k, key, i, turn):
                pe.wait_ge(mod_step, mod_steps(key, i, turn) + MOD_PLAN[key]["steps"][i])
                for n in range(len(mod_conds(key, i))):
                    out, full = bank(ph, k + n, turn)
                    for q in range(4):
                        m = nc.tensor.transpose(out[:, q * P:(q + 1) * P], mod_acc_of(key, i, n)[:, q * P:(q + 1) * P], ident)
                    m.then_inc(full, 1)

            def first_mods():
                for i in range(6):
                    mod_columns(PLAN["mod", 0], i, ("start", 0), i, 0)

            def mean_square(n):
                ph = PLAN["norm", n]
                out, full = bank(ph, 0)
                for i, k in enumerate((0, 1, 2, 3) if n % 2 == 0 else (0, 2, 1, 3)):
                    pe.wait_ge((sq_act, sq_dve)[k // 2 if n % 2 == 0 else (k + 1) % 2], 2 * n + (k % 2 if n % 2 == 0 else k // 2) + 1)
                    for c in (2 * k, 2 * k + 1):
                        m = mm(out[:, 0:T], ones_d, SQ[:, c, :], start=(i == 0 and c == 2 * k), stop=(i == 3 and c == 2 * k + 1))
                m.then_inc(full, 1)

            def pair(ph, k, j, rhs, off=0, width=256, waits=None):
                w, used = take(ph, j)
                out, full = bank(ph, k)
                for i in range(2):
                    for c, r in enumerate(rhs):
                        if waits and i == 0:
                            waits(c)
                        m = mm(out[:, i * T:(i + 1) * T], w[:, off + c * width + i * P:off + c * width + i * P + P], r,
                               start=(c == 0), stop=(c == len(rhs) - 1))
                        if i == c == 0 and used is not None and off == 0:
                            m.then_inc(used, 1)
                m.then_inc(full, 1)

            def token_major(ph, k, j, blocks):
                w, used = take(ph, j)
                out, full = bank(ph, k)
                for i, tb in enumerate(blocks):
                    products(out[:, i * 256:(i + 1) * 256],
                             [(H[:, c, tb * P:(tb + 1) * P], w[:, c * 256:(c + 1) * 256]) for c in range(DC)],
                             full if i == 1 else None, used if i == 0 and blocks[0] == 0 else None)

            def wait_h(s):
                return lambda c: pe.wait_ge(h_ready, 8 * s + c + 1)

            h_lat = [H[:, c, 0:T] for c in range(DC)]

            def attention(l, beside=None):
                ph, units, u0 = PLAN["att", l], attention_units(l), UNIT0[l]
                for i in range(len(units) + 3):
                    if beside:
                        beside(i)
                    if i < len(units):
                        out, full = bank(ph, 3 * i)
                        products(out[:, 0:units[i]["nk"]], units[i]["score"], full)
                    if 2 <= i < len(units) + 2:
                        u = i - 2
                        out, full = bank(ph, 3 * u + 1)
                        pe.wait_ge(att_prob, u0 + u + 1)
                        for kb in range(units[u]["nk"] // P):
                            m = nc.tensor.transpose(out[:, kb * P:(kb + 1) * P], att_p[:, u % 4, kb * P:(kb + 1) * P], ident)
                        m.then_inc(full, 1)
                    if i >= 3:
                        u = i - 3
                        out, full = bank(ph, 3 * u + 2)
                        wait_drained(pe, ph, 3 * u + 1)
                        products(out[:, 0:P], [(v, att_pt[:, u % 2, kb * P:(kb + 1) * P])
                                               for kb, v in enumerate(units[u]["v"])], full)

            def mla(l):
                ph = PLAN["mla_in", l]
                for k in range(2):
                    pair(ph, k, k, h_lat, waits=wait_h(2 * l))
                j = l // 3
                if l == 0:
                    mod_columns(PLAN["mod_in", 0], 0, ("mla", 0), 0, 0)
                out, full = bank(ph, 2)
                pe.wait_ge(mla_sq, 2 * j + 1)
                products(out[:, 0:T], [(ones_d, m_sq[:, c, :]) for c in range(2)], full)
                out, full = bank(ph, 3)
                pe.wait_ge(mla_sq, 2 * j + 2)
                mm(out[:, 0:T], ones_d, m_sq[:, 2, :], start=True, stop=True).then_inc(full, 1)
                ph = PLAN["mla_up", l]
                pe.wait_ge(mla_lat, 3 * j + 2)
                qlat = [m_qlat[:, c, :] for c in range(2)]
                for k in range(4):
                    w, used = take(ph, 0)
                    out, full = bank(ph, k)
                    for i in range(2):
                        n = (2 * k + i) * P
                        products(out[:, i * T:(i + 1) * T], [(w[:, c * D + n:c * D + n + P], qlat[c]) for c in range(2)],
                                 full if i else None, used if k == i == 0 else None)
                w, used = take(ph, 1)
                pe.wait_ge(mla_lat, 3 * j + 3)
                for k in range(4):
                    out, full = bank(ph, 4 + k)
                    for i in range(2):
                        m = mm(out[:, i * T:(i + 1) * T], w[:, (2 * k + i) * P:(2 * k + i + 1) * P], m_klat, start=True, stop=True)
                        if k == i == 0:
                            m.then_inc(used, 1)
                    m.then_inc(full, 1)
                for k in range(4):
                    out, full = bank(ph, 8 + k)
                    tb, half = k // 2, k % 2
                    mm(out, m_klat[:, tb * P:(tb + 1) * P], w[:, D + half * 512:D + (half + 1) * 512], start=True, stop=True)\
                        .then_inc(full, 1)
                w, used = take(ph, 2)
                for k in range(2):
                    out, full = bank(ph, 12 + k)
                    for i in range(2):
                        n = (2 * k + i) * P
                        products(out[:, i * T:(i + 1) * T], [(w[:, c * 512 + n:c * 512 + n + P], qlat[c]) for c in range(2)],
                                 full if i else None, used if k == i == 0 else None)
                for k in range(2):
                    wait_drained(pe, ph, 12 + k)
                    out, full = bank(ph, 14 + k)
                    for i in range(2):
                        m = mm(out[:, i * T:(i + 1) * T], rot, m_qp[:, 2 * k + i, :], start=True, stop=True)
                    m.then_inc(full, 1)
                out, full = bank(ph, 16)
                mm(out[:, 0:T], rot, m_kpe, start=True, stop=True).then_inc(full, 1)
                for k in range(12):
                    wait_drained(pe, ph, k)
                pe.wait_ge(mla_rope, 2 * j + 2)
                pe.wait_ge(kpe_ready, 2 * j + 2)
                if l == 0:
                    for i in range(2):
                        mod_columns(PLAN["mod_up", 0], i, ("mla", 0), 1 + i, 0)

                def beside(i):
                    if i % 5 == 4 and i < 15:
                        mod_columns(PLAN["mod_att", 0], i // 5, ("mla", 0), 3 + i // 5, 0)
                attention(l, beside if l == 0 else None)
                ph = PLAN["mix_out", l]
                for k in range(2 * MLA_H):
                    wait_drained(pe, PLAN["att", l], 3 * k + 2)
                for k in range(4):
                    pair(ph, k, k, [m_o[:, h, :] for h in range(MLA_H)])

            def stick(l):
                ph = PLAN["sb_in", l]
                for k in range(8):
                    pair(ph, k, k, h_lat, waits=wait_h(2 * l))
                for k in range(4):
                    token_major(ph, 8 + k, 8 + k, (0, 1))
                w, used = take(ph, 12)
                tri, ones = w[:, 0:P], w[:, P:2 * P]
                ph = PLAN["sb", l]
                for k in range(12):
                    wait_drained(pe, PLAN["sb_in", l], k)

                def at(h):
                    return 5 * (h // 2) + 2 * (h % 2)

                for i in range(SB_H + 4):
                    if i < SB_H:
                        rows, g = slice((i % 2) * SB_D, (i % 2 + 1) * SB_D), i // 2
                        out, full = bank(ph, at(i))
                        mm(out[:, 0:T], s_k[rows, g, 0:P], s_q[rows, g, :], start=True, stop=True)
                        mm(out[:, T:384], s_k[rows, g, P:T], s_q[rows, g, P:T], start=True, stop=True).then_inc(full, 1)
                    if 2 <= i < SB_H + 2:
                        u = i - 2
                        out, full = bank(ph, at(u) + 1)
                        pe.wait_ge(sb_masked, u + 1)
                        m = mm(out[:, 0:384], tri, s_sp[:, u % 4, :], start=True, stop=False)
                        if u == 0:
                            m.then_inc(used, 1)
                        mm(out[:, P:T], ones, s_sp[:, u % 4, T:384], start=False, stop=True).then_inc(full, 1)
                    if i >= 4:
                        u = i - 4
                        rows = slice((u % 2) * SB_D, (u % 2 + 1) * SB_D)
                        if u % 2 == 0:
                            o_out, o_full = bank(ph, at(u) + 4)
                        pe.wait_ge(sb_prob, u + 1)
                        hv = slice(u * SB_D, (u + 1) * SB_D)
                        mm(o_out[rows, 0:T], s_v[:, 0, hv], s_d[:, u % 4, 0:T], start=True, stop=False)
                        m = mm(o_out[rows, P:T], s_v[:, 1, hv], s_d[:, u % 4, T:384], start=False, stop=True)
                        if u % 2:
                            m.then_inc(o_full, 1)
                for g in range(8):
                    wait_drained(pe, ph, 5 * g + 4)
                ph = PLAN["mix_out", l]
                for k in range(4):
                    pair(ph, k, k, [s_o[:, c, :] for c in range(8)])

            def retention(l):
                ph = PLAN["ret_in", l]
                for k in range(8):
                    pair(ph, k, k, h_lat, waits=wait_h(2 * l))
                for k in range(8):
                    token_major(ph, 8 + k, 8 + k, (0, 1))
                for k in range(8):
                    pair(ph, 16 + k, 16 + k, h_lat)
                for k in range(8, 16):
                    wait_drained(pe, ph, k)
                ph = PLAN["ret", l]
                pe.wait_ge(ret_roped, 2 * RET_H)

                def scores(h):
                    out, full = bank(ph, 3 * h)
                    products(out[:, 0:T], [(r_k[:, 2 * h + c, 0:P], r_q[:, 2 * h + c, :]) for c in range(2)], None,
                             piece_used[PLAN["ret_in", l].piece(23)[0]] if h == 0 else None)
                    products(out[:, T:384], [(r_k[:, 2 * h + c, P:T], r_q[:, 2 * h + c, P:T]) for c in range(2)], full)

                def mean_squares(h):
                    pe.wait_ge(ret_sq, h + 1)
                    out, full = bank(ph, 12 + h)
                    products(out[:, 0:T], [(ones_d, r_sq[h % 2][:, c, :]) for c in range(4)], full)

                scores(0)
                for h in range(RET_H):
                    if h + 1 < RET_H:
                        scores(h + 1)
                    wait_drained(pe, ph, 3 * h)
                    for half in range(2):
                        out, full = bank(ph, 3 * h + 1 + half)
                        for i in range(2):
                            n = h * RET_V + (2 * half + i) * P
                            mm(out[:, i * T:(i + 1) * T], r_v[:, 0, n:n + P], r_sc[:, h % 2, 0:T], start=True, stop=False)
                            m = mm(out[:, i * T + P:(i + 1) * T], r_v[:, 1, n:n + P], r_sc[:, h % 2, T:384],
                                   start=False, stop=True)
                        m.then_inc(full, 1)
                    if h >= 1:
                        mean_squares(h - 1)
                mean_squares(RET_H - 1)
                pe.wait_ge(ret_gated, RET_H)
                ph = PLAN["mix_out", l]
                for k in range(4):
                    out, full = bank(ph, k)
                    for i in range(2):
                        w, used = take(ph, 2 * k + i)
                        products(out[:, i * T:(i + 1) * T], [(w[:, c * P:(c + 1) * P], r_o[:, c, :]) for c in range(16)],
                                 full if i else None, used)

            def ffn(l):
                ph = PLAN["ffn_up", l]
                nm = len(mod_conds(("up", l), 0))
                with pe.Fori(0, ph.turns) as turn:
                    for j in range(8):
                        w, used = take(ph, j, turn)
                        out, full = bank(ph, j + nm * (j // 2), turn)
                        for i in range(2):
                            for c in range(DC):
                                if i == j == 0:
                                    pe.wait_ge(h_ready, 8 * (2 * l + 1) + c + 1)
                                m = mm(out[:, i * T:(i + 1) * T], w[:, c * 256 + i * P:c * 256 + i * P + P], h_lat[c],
                                       start=(c == 0), stop=(c == DC - 1))
                                if i == c == 0:
                                    m.then_inc(used, 1)
                        m.then_inc(full, 1)
                        if j % 2:
                            mod_columns(ph, (2 + nm) * (j // 2) + 2, ("up", l), j // 2, turn)
                ph = PLAN["ffn_down", l]
                pe.wait_ge(hidden_ready, 16 * (l + 1))
                per, jobs = len(ph.banks) // 2, len(MOD_PLAN["down", l]["jobs"]) // 2
                with pe.Fori(0, ph.turns) as turn:
                    for k in range(2):
                        out, full = bank(ph, per * k, turn)
                        for i in range(2):
                            for half in range(2):
                                w, used = take(ph, 4 * k + 2 * i + half, turn)
                                for c in range(16):
                                    m = mm(out[:, i * T:(i + 1) * T], w[:, c * P:(c + 1) * P], f_h[:, 16 * half + c, :],
                                           start=(half == c == 0), stop=(half == 1 and c == 15))
                                    if c == 0:
                                        m.then_inc(used, 1)
                        m.then_inc(full, 1)
                        at = per * k + 1
                        for i in range(jobs):
                            mod_columns(ph, at, ("down", l), jobs * k + i, turn)
                            at += len(mod_conds(("down", l), jobs * k + i))

            def wait_hm(n):
                pe.wait_ge(hm_dve, 8 * n + 8)
                pe.wait_ge(hm_pool, 8 * min(n, 2) + 8)

            h_all = [H[:, c, :] for c in range(DC)]

            def chunks512(ph, k0, j0, pieces, rhs, cols):
                for j in range(pieces):
                    w, used = take(ph, j0 + j)
                    for i in range(2):
                        out, full = bank(ph, k0 + 2 * j + i)
                        products(out[:, 0:cols], [(w[:, c * 256 + i * P:c * 256 + i * P + P], r) for c, r in enumerate(rhs)],
                                 full, None if i else used)

            def fourier_gqa():
                ph = PLAN["ab_in", 0]
                wait_hm(0)
                for k in range(2):
                    token_major(ph, k, 0, (2 * k, 2 * k + 1))
                chunks512(ph, 2, 1, 4, h_all, TC)
                for k in range(2):
                    token_major(ph, 10 + k, 5, (2 * k, 2 * k + 1))
                for c in range(8):
                    out, full = bank(ph, 12 + c)
                    pe.wait_ge(ab_sq, c + 1)
                    mm(out, ones_d, SQ2[:, c, :], start=True, stop=True).then_inc(full, 1)
                for c in range(8):
                    out, full = bank(ph, 20 + c)
                    pe.wait_ge(ab_normed, c + 1)
                    src = a_q[:, c, 0:T] if c < GQ_H else a_k[:, c - GQ_H, 0:T]
                    mm(out[:, 0:T], rot, src, start=True, stop=True).then_inc(full, 1)
                ph2 = PLAN["fnet", 0]
                w, used = take(ph2, 0)
                for k in range(2):
                    wait_drained(pe, ph, k)
                for k in range(4):
                    tb, cc = 2 * (k // 2), k % 2
                    out, full = bank(ph2, k)
                    for i in range(2):
                        products(out[:, i * T:(i + 1) * T],
                                 [(a_f[:, tb + c, cc * P:(cc + 1) * P], w[:, (2 * i + c) * T:(2 * i + c + 1) * T]) for c in range(2)],
                                 full if i else None, used if i == k == 0 else None)
                for k in range(4):
                    wait_drained(pe, ph2, k)
                    out, full = bank(ph2, 4 + k)
                    products(out[:, 0:T], [(w[:, 1024 + i * P:1024 + (i + 1) * P], a_ab[:, k, i * T:(i + 1) * T]) for i in range(2)], full)
                for k in range(4):
                    wait_drained(pe, ph2, 4 + k)
                for cc in range(2):
                    out, full = bank(ph2, 8 + cc)
                    mm(out, w[:, 1280 + cc * P:1280 + (cc + 1) * P], a_fr[:, cc, :], start=True, stop=True).then_inc(full, 1)
                pe.wait_ge(ab_roped, 8)
                for k in range(2):
                    wait_drained(pe, ph, 10 + k)
                attention(4)
                for k in range(2):
                    wait_drained(pe, ph2, 8 + k)
                for k in range(4 * GQ_H):
                    wait_drained(pe, PLAN["att", 4], 3 * k + 2)
                chunks512(PLAN["out2", 0], 0, 0, 4, [a_o[:, c, :] for c in range(8)], TC)

            def neighbours():
                ph = PLAN["na_in", 1]
                wait_hm(2)
                for k in range(4):
                    pair(ph, k, k, h_lat)
                chunks512(ph, 4, 4, 4, h_all, TC)
                for j in range(4):
                    for half in range(2):
                        token_major(ph, 12 + 2 * j + half, 8 + j, (2 * half, 2 * half + 1))
                for k in range(20):
                    wait_drained(pe, ph, k)
                attention(5)
                for k in range(2 * NA_H):
                    wait_drained(pe, PLAN["att", 5], 3 * k + 2)
                ph, po = PLAN["att", 5], PLAN["out2", 1]
                done = [piece_used[ph.piece(j)[0]] for j in (0, 1)] + [piece_used[(ph.piece(0)[2] - 1) % SLOTS]]
                for j in range(4):
                    w, used = take(po, j)
                    for i in range(2):
                        out, full = bank(po, 2 * j + i)
                        for c in range(DC):
                            m = mm(out[:, 0:T], w[:, c * 256 + i * P:c * 256 + i * P + P], n_o[:, c, :], start=(c == 0), stop=(c == DC - 1))
                            if i == 0 and c == 0:
                                m.then_inc(used, 1)
                            elif i == j == 0 and c <= 3:
                                m.then_inc(done[c - 1], 1)
                        m.then_inc(full, 1)

            def layer_norm(m, cols, y, ks):
                ph = PLAN["ln", m]
                out, full = bank(ph, 0)
                for c in range(DC):
                    wait_drained(pe, y, ks[c])
                    i = mm(out[:, 0:cols], ones_d, X[:, c, 0:cols], start=(c == 0), stop=(c == DC - 1))
                i.then_inc(full, 1)
                out, full = bank(ph, 1)
                for c in range(DC):
                    pe.wait_ge(ln_sq, 8 * m + c + 1)
                    i = mm(out[:, 0:cols], ones_d, SQ2[:, c, 0:cols], start=(c == 0), stop=(c == DC - 1))
                i.then_inc(full, 1)

            def moe(l):
                nb = 4 - 2 * l
                cols = nb * P
                n = 2 * l + 1
                wait_hm(n)
                ph = PLAN["route", l]
                w, used = take(ph, 0)
                out, full = bank(ph, 0)
                for tb in range(nb):
                    products(out[:, tb * EXPERTS:(tb + 1) * EXPERTS],
                             [(H[:, c, tb * P:(tb + 1) * P], w[:, c * EXPERTS:(c + 1) * EXPERTS]) for c in range(DC)],
                             full if tb == nb - 1 else None, used if tb == 0 else None)
                head = PLAN["moe_head", l]
                for i in range(2 * nb):
                    out, full = bank(head, i)
                    for c in range(4):
                        m = nc.tensor.transpose(out[:, c * P:(c + 1) * P],
                                                H[:, 4 * (i % 2) + c, (i // 2) * P:(i // 2 + 1) * P], ident)
                    m.then_inc(full, 1)
                for part in range(2):
                    w, used = take(head, part)
                    for q in range(4):
                        b, _ = head.fill(2 * nb + q)
                        if part == 0:
                            bank(head, 2 * nb + q)
                        for c in range(4):
                            m = mm(ps[:, b, 0:cols], w[:, c * TC + q * P:c * TC + (q + 1) * P], H[:, 4 * part + c, 0:cols],
                                   start=(part == c == 0), stop=(part == 1 and c == 3))
                            if q == c == 0:
                                m.then_inc(used, 1)
                        if part == 1:
                            m.then_inc(filled[b], 1)
                    if part == 0:
                        pe.wait_ge(routed, l + 1)
                        out, full = bank(head, 2 * nb + 4)
                        for d in range(nb):
                            mm(out[:, d * EXPERTS:nb * EXPERTS], ones if d else tri,
                               e_sel[:, 0:nb - d, :].rearrange("p a e -> p (a e)"), start=(d == 0), stop=(d == nb - 1))
                        products(out[:, nb * EXPERTS:(nb + 1) * EXPERTS], [(ones, e_sel[:, tb, :]) for tb in range(nb)], full)
                ph = PLAN["moe", l]

                def slots(turn, k):
                    if lacks(turn, k):
                        return
                    e = expert(turn, k)
                    pe.wait_ge(onehot_ready, e + (EXPERTS * l + 1))
                    out, full = bank(ph, SLOT, e)
                    products(out[:, 0:6], [(onehot[:, k % 2, tb, :], slot_vals[:, tb, bass.ds(e * 6, 6)]) for tb in range(nb)], full)

                def rows_turned(turn, k):
                    if lacks(turn, k):
                        return
                    pe.wait_ge(gathered[k % 2], turn * (8 * TURN) + 16 * (EXPERTS // 2 * l + k // 2 + 1))
                    for half in range(2):
                        out, full = bank(ph, ROWS_T + half, expert(turn, k))
                        for c in range(4):
                            at = (4 * half + c) * P
                            m = nc.tensor.transpose(out[:, c * P:(c + 1) * P], e_x[:, k % 2, at:at + P], ident)
                        m.then_inc(full, 1)

                def take_expert(turn, k, part):
                    s, n, p = expert_piece(ph, turn, k, part)
                    pe.wait_ge(piece_full[s], n * 16)
                    return ring[:, s, :], piece_used[(p - 1) % SLOTS]

                def gate_up(turn, k):
                    if lacks(turn, k):
                        return
                    e = expert(turn, k)
                    for half in range(2):
                        wait_drained(pe, ph, ROWS_T + half, e)
                    out, full = bank(ph, HIDDEN, e)
                    for part in range(2):
                        w, used = take_expert(turn, k, part)
                        for c in range(4):
                            m = mm(out, e_xt[:, k % 2, 4 * part + c, :], w[:, c * TC:(c + 1) * TC],
                                   start=(part == c == 0), stop=(part == 1 and c == 3))
                            if c == 0:
                                m.then_inc(used, 1)
                    m.then_inc(full, 1)

                def hidden_turned(turn, k):
                    e = expert(turn, k)
                    wait_drained(pe, ph, HIDDEN, e)
                    out, full = bank(ph, HIDDEN_T, e)
                    for c in range(2):
                        m = nc.tensor.transpose(out[:, c * P:(c + 1) * P], e_h[:, k % 2, c * P:(c + 1) * P], ident)
                    m.then_inc(full, 1)

                def down(turn, k):
                    e = expert(turn, k)
                    w, used = take_expert(turn, k, 2)
                    wait_drained(pe, ph, HIDDEN_T, e)
                    for half in range(2):
                        out, full = bank(ph, OUTPUT + half, e)
                        products(out, [(e_ht[:, c, :], w[:, c * D + half * 512:c * D + (half + 1) * 512]) for c in range(2)],
                                 full, None if half else used)

                for k in range(4):
                    slots(0, k)
                w, used = take(head, 2)
                for q in range(2):
                    wait_drained(pe, head, 2 * nb + 2 + q)
                for i in range(2 * nb):
                    out, full = bank(head, 2 * nb + 5 + i)
                    tb, at = i // 2, (i % 2) * 512
                    products(out, [(sh_h[:, c, tb * P:(tb + 1) * P], w[:, c * D + at:c * D + at + 512]) for c in range(2)],
                             full, None if i else used)
                rows_turned(0, 0)
                rows_turned(0, 1)
                gate_up(0, 0)

                def step(turn, k):
                    rows_turned(turn, k + 2)
                    slots(turn, k + 4)
                    hidden_turned(turn, k)
                    gate_up(turn, k + 1)
                    down(turn, k)
                expert_turns(pe, l, step)

                def spare_block(i):
                    pe.wait_ge(spare["onehot"][l], i + 1)
                    vals = sp_col[:, 16:24].rearrange("p (a b) -> p a b", a=4)
                    products(ps[:, 2, 0:2], [(sp_hot[:, tb, :], vals[:, tb, :]) for tb in range(nb)], spare["slots"][l])
                    pe.wait_ge(spare["rows"][l], i * 16 + 16)
                    for c in range(DC):
                        m = nc.tensor.transpose(ps[:, c // 4, (c % 4) * P:(c % 4 + 1) * P], e_x[:, 0, c * P:(c + 1) * P], ident)
                    m.then_inc(spare["rows_t"][l], 1)
                    pe.wait_ge(spare["x_t"][l], i * 2 + 2)
                    pe.wait_ge(spare["weights"][l], i * 48 + 48)
                    products(ps[:, 4, :], [(e_xt[:, 0, c, :], sp_w[:, c // 4, (c % 4) * TC:(c % 4 + 1) * TC]) for c in range(DC)],
                             spare["hidden"][l])
                    pe.wait_ge(spare["gated"][l], i + 1)
                    for c in range(2):
                        m = nc.tensor.transpose(ps[:, 3, c * P:(c + 1) * P], e_h[:, 0, c * P:(c + 1) * P], ident)
                    m.then_inc(spare["hidden_t"][l], 1)
                    pe.wait_ge(spare["h_t"][l], i + 1)
                    for half in range(2):
                        products(ps[:, 6 + half, :],
                                 [(e_ht[:, c, :], sp_w[:, 2, c * D + half * 512:c * D + (half + 1) * 512]) for c in range(2)],
                                 spare["output"][l] if half else None)
                spare_turns(pe, l, spare_block)
                ph = PLAN["moe_turn", l]
                pe.wait_ge(ff_loaded, 16 * (l + 1))
                for c in range(DC):
                    out, full = bank(ph, c)
                    for tb in range(nb):
                        m = nc.tensor.transpose(out[:, tb * P:(tb + 1) * P], e_acc[:, tb, c * P:(c + 1) * P], ident)
                    m.then_inc(full, 1)

            pe.wait_ge(consts_loaded, 48)
            pe.wait_ge(cond_ready, 2)
            first_mods()
            for l in range(DEPTH):
                mean_square(4 * l)
                (mla, stick, retention)[l % 3](l)
                mean_square(4 * l + 1)
                mean_square(4 * l + 2)
                ffn(l)
                mean_square(4 * l + 3)
            for l in range(DEPTH_2):
                (fourier_gqa, neighbours)[l]()
                layer_norm(2 * l, TC if l == 0 else T, PLAN["out2", l], list(range(8)))
                moe(l)
                layer_norm(2 * l + 1, TC if l == 0 else T, PLAN["moe_turn", l], list(range(8)))

        @block.scalar
        def _(act):
            link = chained(act, act_step)
            fn = nc.scalar.activation
            act.dma_start(vec[:], vec_d).then_inc(consts_loaded, 16)
            act.dma_start(tab[:], tab_d).then_inc(consts_loaded, 16)
            act.dma_start(pos[:], pos_d).then_inc(consts_loaded, 16)
            act.dma_start(X[:, :, 0:T], x_d).then_inc(x_loaded, 16)
            eps = V("eps")

            def drain(ph, k, out, in_, func=ACT.Copy, turn=0, **kw):
                b, _ = ph.fill(k, turn)
                wait_filled(act, ph, k, turn)
                return fn(out, in_(ps[:, b, :]), func, **kw).then_inc(drained[b], 1)

            def whole(b):
                return b

            def left(b):
                return b[:, 0:T]

            def pairs(b):
                return b.rearrange("p (a t) -> p a t", a=2)

            def pre_norm(s):
                for k in (0, 1):
                    act.wait_ge(*((x_ready, 4 * s + 2 * k - 2) if s else (x_loaded, 16)))
                    fn(SQ[:, 2 * k:2 * k + 2, :], X[:, 2 * k:2 * k + 2, 0:T], ACT.Square).then_inc(sq_act, 1)
                drain(PLAN["norm", 2 * s], 0, STD[:, 0:T], left, ACT.Sqrt, bias=eps)
                l = s // 2
                act.wait_ge(mod_ready, l + 2 if s else 1)
                for c in range(DC):
                    act.wait_ge(h_scaled, 8 * s + c + 1)
                    shift = (s % 2) * 3 * DC + c
                    fn(H[:, c, 0:T], H[:, c, 0:T], ACT.Identity, bias=mod[:, l, shift:shift + 1]).then_inc(h_ready, 1)

            def post_norm(s, ph):
                def one(k, at, turn):
                    b = wait_filled(act, ph, k, turn)
                    fn(SQ[:, at, :], pairs(ps[:, b, :]), ACT.Square).then_inc(sq_act, 1)
                    drain(ph, k, Y[:, at, :], pairs, turn=turn)
                if ph.turns == 1:
                    for k in (1, 3):
                        one(k, slice(2 * k, 2 * k + 2), 0)
                else:
                    with act.Fori(0, ph.turns) as turn:
                        one(len(ph.banks) // 2, bass.ds(turn * 4 + 2, 2), turn)
                drain(PLAN["norm", 2 * s + 1], 0, STD[:, 0:T], left, ACT.Sqrt, bias=eps)

            def attention(l):
                ph, units, u0 = PLAN["att", l], attention_units(l), UNIT0[l]
                for i in range(len(units) + 2):
                    if i < len(units):
                        U, nk = u0 + i, units[i]["nk"]
                        wait_drained(act, ph, 3 * i)
                        fn(att_p[:, i % 4, 0:nk], att_s[l][:, i % 4, 0:nk], ACT.Exp, scale=-1.0, bias=att_stat[:, 0, U:U + 1],
                           accum_out=att_stat[:, 1, U:U + 1]).then_inc(att_exp, 1)
                    if i >= 2:
                        u = i - 2
                        if u >= 2:
                            wait_filled(act, ph, 3 * (u - 2) + 2)
                        nk = units[u]["nk"]
                        drain(ph, 3 * u + 1, att_pt[:, u % 2, 0:nk], lambda b: b[:, 0:nk])

            def mla(l):
                ph, j = PLAN["mla_in", l], l // 3
                wait_drained(act, ph, 0)
                fn(m_sq[:, 0:2, :], m_qlat, ACT.Square).then_inc(mla_sq, 1)
                wait_drained(act, ph, 1)
                fn(m_sq[:, 2, :], m_klat, ACT.Square).then_inc(mla_sq, 1)
                drain(ph, 2, STD[:, 0:T], left, ACT.Sqrt, scale=D / 256.0, bias=eps)
                drain(ph, 3, STD[:, T:TC], left, ACT.Sqrt, scale=D / 128.0, bias=eps)
                ph = PLAN["mla_up", l]
                for k in range(0, 4):
                    drain(ph, k, m_qn[:, 2 * k:2 * k + 2, :], pairs)
                for k in range(8, 12):
                    tb, half = (k - 8) // 2, k % 2
                    drain(ph, k, m_v[:, tb, half * 512:(half + 1) * 512], whole)
                for k in range(12, 14):
                    drain(ph, k, m_qp[:, 2 * (k - 12):2 * (k - 12) + 2, :], pairs)
                attention(l)

            def stick(l):
                ph = PLAN["sb_in", l]
                for k in range(0, 4):
                    drain(ph, k, s_q[:, 2 * k:2 * k + 2, :], pairs)
                for k in range(8, 12):
                    drain(ph, k, s_v[:, :, (k - 8) * 256:(k - 7) * 256], pairs)
                ph = PLAN["sb", l]
                for i in range(SB_H + 3):
                    if i < SB_H:
                        act.wait_ge(sb_neg, i + 1)
                        e = s_e[:, i % 4, :]
                        link(fn(e, e, ACT.Exp))
                        fn(e, e, ACT.Ln, bias=1.0).then_inc(sb_ln, 1)
                    if i >= 3:
                        u = i - 3
                        act.wait_ge(sb_guarded, u + 1)
                        fn(s_d[:, u % 4, :], s_d[:, u % 4, :], ACT.Exp).then_inc(sb_prob, 1)

            def sines(w):
                act.wait_ge(rope_reduced, 2 * w + 2)
                for n in (2 * w, 2 * w + 1):
                    fn(rope[:, n, :], rope[:, n, :], ACT.Sin).then_inc(rope_ready, 1)

            def retention(l):
                sines(1)
                ph = PLAN["ret_in", l]
                for k in range(8, 16):
                    drain(ph, k, r_v[:, :, (k - 8) * 256:(k - 7) * 256], pairs)
                for k in range(16, 24):
                    drain(ph, k, r_g[:, 2 * (k - 16):2 * (k - 16) + 2, :], pairs, ACT.Silu)
                ph = PLAN["ret", l]

                def deviation(h):
                    drain(ph, 12 + h, stat[:, h, 0:T], left, ACT.Sqrt, scale=D / float(RET_V), bias=eps)

                for h in range(RET_H):
                    for half in range(2):
                        at = slice(4 * h + 2 * half, 4 * h + 2 * half + 2)
                        drain(ph, 3 * h + 1 + half, r_o[:, at, :], pairs)
                    for half in range(2):
                        wait_drained(act, ph, 3 * h + 1 + half)
                    fn(r_sq[h % 2], r_o[:, 4 * h:4 * h + 4, :], ACT.Square).then_inc(ret_sq, 1)
                    if h >= 1:
                        deviation(h - 1)
                deviation(RET_H - 1)

            def ffn(l):
                ph = PLAN["ffn_up", l]

                def body(turn):
                    for j in range(8):
                        k = j + len(mod_conds(("up", l), 0)) * (j // 2)
                        b = wait_filled(act, ph, k, turn)
                        n = turn * 8 + (16 * l + j - 1)
                        if not isinstance(n, int) or n > 0:
                            act.wait_ge(hidden_ready, n)
                        fn(f_r[:, j % 2, :], ps[:, b, :], ACT.Relu).then_inc(drained[b], 1)
                turns(act, ph, body, l == 0)

            def layer_norm(m, cols):
                ph, l = PLAN["ln", m], m // 2
                drain(ph, 0, MU[:, 0:cols], lambda b: b[:, 0:cols])
                for c in range(DC):
                    act.wait_ge(xc_dve if c % 2 == 0 else xc_pool, 4 * m + c // 2 + 1)
                    fn(SQ2[:, c, 0:cols], X[:, c, 0:cols], ACT.Square).then_inc(ln_sq, 1)
                drain(ph, 1, STD[:, 0:cols], lambda b: b[:, 0:cols], ACT.Sqrt, bias=eps)
                for c in range(DC):
                    act.wait_ge(ln_scaled, 8 * m + c + 1)
                    fn(X[:, c, 0:cols], X[:, c, 0:cols], ACT.Identity, bias=V("ln", (4 * l + 2 * (m % 2) + 1) * DC + c))\
                        .then_inc(ln_ready, 1)

            def fourier_gqa():
                ph = PLAN["ab_in", 0]
                for k in range(2):
                    drain(ph, k, a_f[:, 2 * k:2 * k + 2, :], pairs)
                for c in range(8):
                    wait_drained(act, ph, 2 + c)
                    src = a_q[:, c, :] if c < GQ_H else a_k[:, c - GQ_H, :]
                    fn(SQ2[:, c, :], src, ACT.Square).then_inc(ab_sq, 1)
                for k in range(2):
                    drain(ph, 10 + k, a_v[:, 2 * k:2 * k + 2, :], pairs)
                for c in range(8):
                    if c >= 2:
                        act.wait_ge(ab_normed, c - 1)
                    drain(ph, 12 + c, stat[:, c % 2, :], whole, ACT.Sqrt, scale=D / float(P), bias=eps)
                ph = PLAN["fnet", 0]
                for k in range(4):
                    tok, cc = k // 2, k % 2
                    drain(ph, 4 + k, a_fr[:, cc, tok * T:(tok + 1) * T], left)
                attention(4)

            def neighbours():
                ph = PLAN["na_in", 1]
                for k in range(4):
                    drain(ph, k, n_q[:, 2 * k:2 * k + 2, :], pairs)
                for k in range(4, 12, 2):
                    drain(ph, k, n_k[:, k - 4, :], whole)
                for j in range(4):
                    drain(ph, 12 + 2 * j, n_v[:, 0:2, j * 256:(j + 1) * 256], pairs)
                attention(5)

            def moe(l):
                nb = 4 - 2 * l
                cols = nb * P
                b = wait_filled(act, PLAN["route", l], 0)
                fn(e_sc[:, 0:nb, :], ps[:, b, 0:nb * EXPERTS].rearrange("p (a e) -> p a e", a=nb), ACT.Sigmoid)\
                    .then_inc(drained[b], 1)

                head, ph = PLAN["moe_head", l], PLAN["moe", l]
                for i in range(2 * nb):
                    drain(head, i, h2_rows[:, i // 2, (i % 2) * 512:(i % 2 + 1) * 512], whole)
                for i in range(2):
                    drain(head, 2 * nb + i, sh_g[:, i, 0:cols], lambda b: b[:, 0:cols], ACT.Silu)
                for i in range(2 * nb):
                    drain(head, 2 * nb + 5 + i, e_acc[:, i // 2, (i % 2) * 512:(i % 2 + 1) * 512], whole)

                def rows_turned(turn, k):
                    if not lacks(turn, k):
                        drain(ph, ROWS_T, e_xt[:, k % 2, 0:4, :], lambda b: b.rearrange("p (c t) -> p c t", c=4),
                              turn=expert(turn, k))

                def silu(turn, k):
                    if not lacks(turn, k):
                        b = wait_filled(act, ph, HIDDEN, expert(turn, k))
                        fn(e_g[:, k % 2, :], ps[:, b, 0:EXP_D], ACT.Silu).then_inc(expert_silu, 1)

                rows_turned(0, 0)
                rows_turned(0, 1)
                silu(0, 0)

                def step(turn, k):
                    e = expert(turn, k)
                    rows_turned(turn, k + 2)
                    drain(ph, HIDDEN_T, e_ht, lambda b: b[:, 0:EXP_D].rearrange("p (c t) -> p c t", c=2), turn=e)
                    silu(turn, k + 1)
                    wait_drained(act, ph, SLOT, e)
                    wait_past(act, scattered, turn * (16 * TURN) + 16 * (EXPERTS * l + k - 1))
                    drain(ph, OUTPUT, e_y[:, k % 2, 0:512], whole, turn=e, scale=slot_rec[:, k, 1:2])
                expert_turns(act, l, step)

                def spare_block(i):
                    act.wait_ge(spare["rows_t"][l], i + 1)
                    fn(e_xt[:, 0, 0:4, :], ps[:, 0, :].rearrange("p (c t) -> p c t", c=4), ACT.Copy).then_inc(spare["x_t"][l], 1)
                    act.wait_ge(spare["hidden"][l], i + 1)
                    fn(e_g[:, 0, :], ps[:, 4, 0:EXP_D], ACT.Silu).then_inc(spare["silu"][l], 1)
                    act.wait_ge(spare["hidden_t"][l], i + 1)
                    fn(e_ht, ps[:, 3, 0:EXP_D].rearrange("p (c t) -> p c t", c=2), ACT.Copy).then_inc(spare["h_t"][l], 1)
                    act.wait_ge(spare["output"][l], i + 1)
                    fn(e_y[:, 0, 0:512], ps[:, 6, :], ACT.Copy, scale=sp_col[:, 1:2]).then_inc(spare["scaled"][l], 1)
                spare_turns(act, l, spare_block)

            act.wait_ge(consts_loaded, 48)
            conds = V("conds", 0, 3 * DC).rearrange("p (c n) -> p c n", n=3)
            fn(cond[:, :, 0:1], conds[:, :, 0:1], ACT.Silu).then_inc(cond_ready, 1)
            fn(cond[:, :, 1:3], conds[:, :, 1:3], ACT.Silu).then_inc(cond_ready, 1)
            sines(0)
            for l in range(DEPTH):
                pre_norm(2 * l)
                (mla, stick, retention)[l % 3](l)
                post_norm(2 * l, PLAN["mix_out", l])
                pre_norm(2 * l + 1)
                ffn(l)
                post_norm(2 * l + 1, PLAN["ffn_down", l])
            for l in range(DEPTH_2):
                (fourier_gqa, neighbours)[l]()
                layer_norm(2 * l, TC if l == 0 else T)
                moe(l)
                layer_norm(2 * l + 1, TC if l == 0 else T)

        @block.vector
        def _(dve):
            link = chained(dve, dve_step)
            v = nc.vector
            tt, ts, stt = v.tensor_tensor, v.tensor_scalar, v.scalar_tensor_tensor
            MUL, ADD, SUB = ALU.mult, ALU.add, ALU.subtract

            def pairs(b):
                return b.rearrange("p (a t) -> p a t", a=2)

            def drain(ph, k, out, shape=None, turn=0):
                b = wait_filled(dve, ph, k, turn)
                src = ps[:, b, :] if shape is None else shape(ps[:, b, :])
                v.tensor_copy(out, src).then_inc(drained[b], 1)

            def rope_tables(w):
                f, turns_, ang = (Y[:, c, :] for c in range(3))
                c1, c2 = 6.28125, 0.0019350051879882812
                c3 = 2 * np.pi - c1 - c2
                big = 1.5 * 2 ** 23
                link(v.tensor_copy(f, pos[:]))
                link(ts(ang, f, V("inv_freq", w), None, MUL))
                for i, quarter in enumerate((0.25, 0.0)):
                    r = rope[:, 2 * w + i, :]
                    link(ts(turns_, ang, float(1 / (2 * np.pi)), quarter, MUL, ADD))
                    link(ts(turns_, turns_, big, None, ADD))
                    link(ts(turns_, turns_, big, None, SUB))
                    link(stt(r, turns_, -c1, ang, MUL, ADD))
                    link(stt(r, turns_, -c2, r, MUL, ADD))
                    link(stt(r, turns_, -float(c3), r, MUL, ADD))
                    link(ts(r, r, float(quarter * 2 * np.pi), 3.1415925, ADD, ALU.min))
                    ts(r, r, -3.1415925, None, ALU.max).then_inc(rope_reduced, 1)

            def mod_piece(key, i, half, turn):
                weights, full, n = mod_piece_at(key, i, half, turn)
                dve.wait_ge(full, n)
                conds = mod_conds(key, i)
                step = mod_steps(key, i, turn) + half * 4 * len(conds)
                for c in range(4):
                    for n, col in enumerate(conds):
                        acc, w, x = mod_acc_of(key, i, n), weights[:, c, :], cond[:, 4 * half + c, col:col + 1]
                        if half == c == 0:
                            ins = ts(acc, w, x, None, MUL)
                        else:
                            dve.wait_ge(mod_step, step + (c - 1) * len(conds) + n + 1)
                            ins = stt(acc, w, x, acc, MUL, ADD)
                        ins.then_inc(mod_step, 1)

            def mod_block(ph, k, key, i, turn):
                table, l = MOD_PLAN[key]["jobs"][i]
                block0, per_turn = MOD_PLAN[key]["blocks"][i]
                at = (turn * per_turn + block0) * 4
                at = slice(at, at + 4) if isinstance(at, int) else bass.ds(at, 4)
                before = mod_adds(key, i, turn)
                if not isinstance(before, int) or before > 0:
                    dve.wait_ge(mod_added, before)
                for n in range(len(mod_conds(key, i))):
                    b = wait_filled(dve, ph, k + n, turn)
                    v.tensor_reduce(mod_sum[:, n, :], ps[:, b, :].rearrange("p (a t) -> p a t", a=4), AX.X, ADD)\
                        .then_inc(drained[b], 1)
                for n in range(len(mod_conds(key, i))):
                    wait_drained(dve, ph, k + n, turn)
                    if table == "mod":
                        out, bias = mod[:, l, at], V("ada_b", l * MODS, MODS)[:, at]
                    else:
                        out, bias = mod2[:, l, at, n], V("b_mod", l * MODS, MODS)[:, at]
                    tt(out, mod_sum[:, n, :], bias, ADD).then_inc(mod_added, 1)

            def first_mods():
                dve.wait_ge(cond_ready, 2)
                for i in range(6):
                    for half in range(2):
                        mod_piece(("start", 0), i, half, 0)
                    if i:
                        mod_block(PLAN["mod", 0], i - 1, ("start", 0), i - 1, 0)
                mod_block(PLAN["mod", 0], 5, ("start", 0), 5, 0)

            def added(l):
                return 12 * (l + 1) + 8 * l if l < DEPTH else 12 * DEPTH + 24 * 2

            def mods(l, parts=(0, 1)):
                dve.wait_ge(mod_added, added(l) if 1 in parts else 6)

                def part(i):
                    return mod[:, l, i * DC:(i + 1) * DC]

                for i in parts:
                    g = V("norm_g", (4 * l + 2 * i) * DC, 2 * DC)
                    stt(gains[:, l, 2 * i, :], part(3 * i + 1), 1.0, g[:, 0:DC], ADD, MUL)
                    last = tt(gains[:, l, 2 * i + 1, :], part(3 * i + 2), g[:, DC:2 * DC], MUL)
                last.then_inc(mod_ready, 1)
                dve.wait_ge(mod_ready, l + 2 if 1 in parts else 1)

            def mods2(l):
                dve.wait_ge(mod_added, added(DEPTH))
                for i in range(2):
                    last = ts(scale2[:, l, i, :, :], mod2[:, l, (3 * i + 1) * DC:(3 * i + 2) * DC, :], 1.0, None, ADD)
                last.then_inc(mod_ready, 1)
                dve.wait_ge(mod_ready, DEPTH + l + 2)

            def reciprocal_deviation(n):
                wait_drained(dve, PLAN["norm", n], 0)
                link(v.reciprocal(RSTD[:, 0:T], STD[:, 0:T]))

            def pre_norm(s):
                for k in (2, 3):
                    dve.wait_ge(*((x_added, 4 * s + 2 * k - 6) if s else (x_loaded, 16)))
                    x = X[:, 2 * k:2 * k + 2, 0:T]
                    tt(SQ[:, 2 * k:2 * k + 2, :], x, x, MUL).then_inc(sq_dve, 1)
                reciprocal_deviation(2 * s)
                for c in range(DC):
                    stt(H[:, c, 0:T], X[:, c, 0:T], gains[:, s // 2, 2 * (s % 2), c:c + 1], RSTD[:, 0:T], MUL, MUL)\
                        .then_inc(h_scaled, 1)

            def post_norm(s, ph):
                def one(k, at, turn):
                    drain(ph, k, Y[:, at, :], pairs, turn)
                    wait_drained(dve, ph, k, turn)
                    tt(SQ[:, at, :], Y[:, at, :], Y[:, at, :], MUL).then_inc(sq_dve, 1)
                if ph.turns == 1:
                    for k in (0, 2):
                        one(k, slice(2 * k, 2 * k + 2), 0)
                else:
                    l = s // 2
                    per, jobs = len(ph.banks) // 2, len(MOD_PLAN["down", l]["jobs"]) // 2
                    with dve.Fori(0, ph.turns) as turn:
                        for k in range(2):
                            at = per * k + 1
                            for i in range(jobs * k, jobs * k + jobs):
                                for half in range(2):
                                    mod_piece(("down", l), i, half, turn)
                            if k == 0:
                                one(0, bass.ds(turn * 4, 2), turn)
                            for i in range(jobs * k, jobs * k + jobs):
                                mod_block(ph, at, ("down", l), i, turn)
                                at += len(mod_conds(("down", l), i))
                reciprocal_deviation(2 * s + 1)
                for c in range(DC):
                    stt(Y[:, c, :], Y[:, c, :], gains[:, s // 2, 2 * (s % 2) + 1, c:c + 1], RSTD[:, 0:T], MUL, MUL)\
                        .then_inc(y_scaled, 1)
                for c in range(4, DC):
                    dve.wait_ge(y_scaled, 8 * s + c + 1)
                    tt(X[:, c, 0:T], X[:, c, 0:T], Y[:, c, :], ADD).then_inc(x_added, 1)

            def attention(l, scale, beside=None):
                ph, units, u0 = PLAN["att", l], attention_units(l), UNIT0[l]
                for i in range(len(units) + 4):
                    if beside:
                        beside(i)
                    if i < len(units):
                        unit, U = units[i], u0 + i
                        nk, mask = unit["nk"], unit["mask"]
                        if unit["bias"] is not None:
                            bias, window = unit["bias"]
                            mask = n_bm[:, i % 2, :]
                            link(stt(mask[:, 0:T], bias, 1.0 / scale, window, MUL, ADD))
                        b = wait_filled(dve, ph, 3 * i)
                        if i >= 4:
                            dve.wait_ge(att_exp, U - 3)
                        v.tensor_tensor_reduce(out=att_s[l][:, i % 4, 0:nk], in0=ps[:, b, 0:nk], in1=mask, scale=-scale,
                                               scalar=3e38, op0=ADD, op1=ALU.min,
                                               accum_out=att_stat[:, 0, U:U + 1]).then_inc(drained[b], 1)
                    if 1 <= i <= len(units):
                        U = u0 + i - 1
                        dve.wait_ge(att_exp, U + 1)
                        v.reciprocal(att_stat[:, 2, U:U + 1], att_stat[:, 1, U:U + 1]).then_inc(att_rinv, 1)
                    if i >= 4:
                        drain(ph, 3 * (i - 4) + 2, units[i - 4]["o"], lambda b: b[:, 0:P])

            def mla(l):
                ph, j = PLAN["mla_in", l], l // 3

                def mod_pair(i):
                    for half in range(2):
                        mod_piece(("mla", 0), i, half, 0)
                if l == 0:
                    mod_pair(0)
                drain(ph, 0, m_qlat, pairs)
                drain(ph, 1, region(512, 2, T), pairs)
                wait_drained(dve, ph, 2)
                link(v.reciprocal(RSTD[:, 0:T], STD[:, 0:T]))
                for c in range(2):
                    stt(m_qlat[:, c, :], m_qlat[:, c, :], V("q_norm", 2 * j + c), RSTD[:, 0:T], MUL, MUL).then_inc(mla_lat, 1)
                wait_drained(dve, ph, 3)
                link(v.reciprocal(RSTD[:, T:TC], STD[:, T:TC]))
                stt(m_klat, m_klat, V("kv_norm", j), RSTD[:, T:TC], MUL, MUL).then_inc(mla_lat, 1)
                ph = PLAN["mla_up", l]
                if l == 0:
                    mod_block(PLAN["mod_in", 0], 0, ("mla", 0), 0, 0)
                    mod_pair(1)
                for k in range(4, 8):
                    drain(ph, k, m_kn[:, 2 * (k - 4):2 * (k - 4) + 2, :], pairs)
                if l == 0:
                    mod_pair(2)
                dve.wait_ge(rope_ready, 2)
                cos, sin = rope[:, 0, :], rope[:, 1, :]
                for k in range(2):
                    b = wait_filled(dve, ph, 14 + k)
                    tt(m_t2[:, 2 * k, :], ps[:, b, 0:T], sin, MUL)
                    tt(m_t2[:, 2 * k + 1, :], ps[:, b, T:TC], sin, MUL).then_inc(drained[b], 1)
                b = wait_filled(dve, ph, 16)
                tt(m_t1[:, 0, :], ps[:, b, 0:T], sin, MUL).then_inc(drained[b], 1)
                link(tt(m_t1[:, 1, :], m_kpe, cos, MUL))
                wait_drained(dve, ph, 16)
                link(tt(m_t1[:, 2, :], m_t1[:, 0, :], m_t1[:, 1, :], ADD))
                for i in range(2):
                    ts(m_kpm[:, i, :], m_t1[:, 2, :], V("parity", i), None, MUL).then_inc(kpe_ready, 1)
                s, n, _ = ph.piece(2)
                dve.wait_ge(piece_full[s], 16 * n)
                if l == 0:
                    for i in range(2):
                        mod_block(PLAN["mod_up", 0], i, ("mla", 0), 1 + i, 0)

                def beside(i):
                    if i < 15 and i % 5 in (0, 2):
                        mod_piece(("mla", 0), 3 + i // 5, i % 5 // 2, 0)
                    if i >= 5 and i % 5 == 1:
                        mod_block(PLAN["mod_att", 0], i // 5 - 1, ("mla", 0), 2 + i // 5, 0)
                attention(l, mla_scale, beside if l == 0 else None)
                if l == 0:
                    mods(0, (1,))

            def stick(l):
                ph = PLAN["sb_in", l]
                for k in range(4, 8):
                    drain(ph, k, s_k[:, 2 * (k - 4):2 * (k - 4) + 2, :], pairs)
                ph = PLAN["sb", l]
                def at(h):
                    return 5 * (h // 2) + 2 * (h % 2)

                for i in range(SB_H + 5):
                    if i < SB_H:
                        b = wait_filled(dve, ph, at(i))
                        if i >= 4:
                            wait_drained(dve, ph, at(i - 4) + 1)
                        ts(s_z[:, i % 4, :], ps[:, b, 0:384], SB_D ** -0.5, None, MUL).then_inc(drained[b], 1)
                        if i >= 4:
                            dve.wait_ge(sb_soft, i - 3)
                        wait_drained(dve, ph, at(i))
                        stt(s_e[:, i % 4, :], s_z[:, i % 4, :], -1.0, s_z[:, i % 4, :], MUL, ALU.min).then_inc(sb_neg, 1)
                    if 1 <= i <= SB_H:
                        u = i - 1
                        dve.wait_ge(sb_ln, u + 1)
                        stt(s_sp[:, u % 4, :], s_z[:, u % 4, :], 0.0, s_e[:, u % 4, :], ALU.max, ADD).then_inc(sb_soft, 1)
                    if 2 <= i < SB_H + 2:
                        u = i - 2
                        b = wait_filled(dve, ph, at(u) + 1)
                        tt(s_d[:, u % 4, :], s_z[:, u % 4, :], ps[:, b, 0:384], SUB).then_inc(drained[b], 1)
                    if i >= 6 and i % 2 == 0:
                        g = (i - 6) // 2
                        drain(ph, 5 * g + 4, s_o[:, g, :], lambda b: b[:, 0:T])

            def retention(l):
                rope_tables(1)
                ph = PLAN["ret_in", l]
                dve.wait_ge(rope_ready, 4)
                cos, sin = rope[:, 2, :], rope[:, 3, :]
                for k in range(8):
                    b = wait_filled(dve, ph, k)
                    if k >= 2:
                        dve.wait_ge(ret_roped, k - 1)
                    for i in range(2):
                        half = ps[:, b, i * T:(i + 1) * T]
                        tt(r_ta[:, k % 2, i, :], half, cos, MUL)
                        last = tt(r_tb[:, k % 2, i, :], half, sin, MUL)
                    last.then_inc(drained[b], 1)
                s, n, _ = ph.piece(24)
                dve.wait_ge(piece_full[s], 16 * n)
                decay = ring[:, s, :]
                ph = PLAN["ret", l]
                for h in range(RET_H):
                    b = wait_filled(dve, ph, 3 * h)
                    tt(r_sc[:, h % 2, :], ps[:, b, 0:384], decay[:, h * 384:(h + 1) * 384], MUL).then_inc(drained[b], 1)
                for h in range(RET_H):
                    wait_drained(dve, ph, 12 + h)
                    link(v.reciprocal(stat[:, h, T:TC], stat[:, h, 0:T]))
                    for c in range(4 * h, 4 * h + 4):
                        stt(r_o[:, c, :], r_o[:, c, :], V("gn_g", c), stat[:, h, T:TC], MUL, MUL).then_inc(ret_normed, 1)

            def ffn(l):
                ph = PLAN["ffn_up", l]
                with dve.Fori(0, ph.turns) as turn:
                    for j in range(8):
                        mod_piece(("up", l), j // 2, j % 2, turn)
                        nm = len(mod_conds(("up", l), 0))
                        wait_drained(dve, ph, j + nm * (j // 2), turn)
                        r = pairs(f_r[:, j % 2, :])
                        tt(f_h[:, bass.ds(turn * 16 + 2 * j, 2), :], r, r, MUL).then_inc(hidden_ready, 1)
                        if j % 2:
                            mod_block(ph, (2 + nm) * (j // 2) + 2, ("up", l), j // 2, turn)

            def modulate(n):
                l, i = n // 2, n % 2
                if n:
                    dve.wait_ge(ln_ready, 8 * n)
                else:
                    dve.wait_ge(x_ready, 4 * 2 * DEPTH)
                    dve.wait_ge(x_added, 4 * 2 * DEPTH)
                for c in range(DC):
                    shift = 3 * i * DC + c
                    ts(H[:, c, 0:T], X[:, c, 0:T], scale2[:, l, i, c, 0:1], mod2[:, l, shift, 0:1], MUL, ADD).then_inc(hm_dve, 1)

            def layer_norm(m, cols, y):
                l, i = m // 2, m % 2
                for c in range(DC):
                    b = wait_filled(dve, y, c)
                    dve.wait_ge(x_alpha, 8 * m + c + 1)
                    for n in range(cols // T):
                        at, gate = slice(n * T, (n + 1) * T), mod2[:, l, (3 * i + 2) * DC + c, n:n + 1]
                        last = stt(X[:, c, at], ps[:, b, at], gate, X[:, c, at], MUL, ADD)
                    last.then_inc(drained[b], 1)
                ph = PLAN["ln", m]
                wait_drained(dve, ph, 0)
                for c in range(0, DC, 2):
                    tt(X[:, c, 0:cols], X[:, c, 0:cols], MU[:, 0:cols], SUB).then_inc(xc_dve, 1)
                wait_drained(dve, ph, 1)
                link(v.reciprocal(RSTD[:, 0:cols], STD[:, 0:cols]))
                for c in range(DC):
                    stt(X[:, c, 0:cols], X[:, c, 0:cols], V("ln", (4 * l + 2 * i) * DC + c), RSTD[:, 0:cols], MUL, MUL)\
                        .then_inc(ln_scaled, 1)

            def fourier_gqa():
                ph = PLAN["ab_in", 0]

                def head(c):
                    return a_q[:, c, :] if c < GQ_H else a_k[:, c - GQ_H, :]

                for c in range(8):
                    drain(ph, 2 + c, head(c))
                for c in range(8):
                    wait_drained(dve, ph, 12 + c)
                    link(v.reciprocal(stat[:, 2 + c % 2, :], stat[:, c % 2, :]))
                    stt(head(c), head(c), V("qk_gain", c // GQ_H), stat[:, 2 + c % 2, :], MUL, MUL).then_inc(ab_normed, 1)
                for c in range(8):
                    b = wait_filled(dve, ph, 20 + c)
                    if c >= 2:
                        dve.wait_ge(ab_roped, c - 1)
                    tt(a_t[:, c % 2, :], ps[:, b, 0:T], ax_sin, MUL).then_inc(drained[b], 1)
                ph = PLAN["fnet", 0]
                for k in range(4):
                    drain(ph, k, a_ab[:, k, :])
                for cc in range(2):
                    drain(ph, 8 + cc, a_o[:, cc, :])
                dve.wait_ge(zeros_set, 1)
                attention(4, head_scale)

            def neighbours():
                ph = PLAN["na_in", 1]
                for k in range(5, 12, 2):
                    drain(ph, k, n_k[:, k - 4, :])
                for j in range(4):
                    drain(ph, 13 + 2 * j, n_v[:, 2:4, j * 256:(j + 1) * 256], pairs)
                link(v.memset(n_bm[:, :, T:TC], 0.0))
                for j in range(3):
                    s, n, _ = PLAN["att", 5].piece(j)
                    dve.wait_ge(piece_full[s], 16 * n)
                attention(5, head_scale)

            def route(l, nb):
                wait_drained(dve, PLAN["route", l], 0)
                for tb in range(nb):
                    sc, biased, rest, sel = (r[:, tb, :] for r in (e_sc, e_sb, e_rep, e_sel))
                    top, total, inv = route_s[:, 0:8], route_s[:, 8 + tb:9 + tb], route_s[:, 16 + tb:17 + tb]
                    link(tt(biased, sc, V("e_bias", l * EXPERTS, EXPERTS), ADD))
                    link(v.max(top, biased))
                    link(v.match_replace(rest, top, biased, NEG))
                    link(tt(sel, rest, biased, ALU.is_lt))
                    link(stt(e_w[:, tb, :], sc, 1.0, sel, MUL, MUL, accum_out=total))
                    link(v.reciprocal(inv, total))
                    last = ts(wts[:, tb, :], e_w[:, tb, :], inv, ROUTE_SCALE, MUL, MUL)
                last.then_inc(routed, 1)
                dve.wait_ge(routed, l + 1)

            def weight_parts(nb):
                vals = slot_vals[:, :, :].rearrange("p a (e v) -> p a e v", v=6)
                rest, part = e_rep[:, 0:nb, :], e_w[:, 0:nb, :]
                w = wts[:, 0:nb, :]
                for i in range(3):
                    link(v.tensor_copy(vals[:, 0:nb, :, 3 + i], w))
                    if i < 2:
                        link(v.tensor_copy(part, vals[:, 0:nb, :, 3 + i]))
                        link(tt(rest, w, part, SUB))
                        w = rest

            def count_spares(l, nb):
                link(ts(sp_blocks, sp_tokens, float(P), None, ALU.is_gt))
                for b in range(2, nb):
                    link(stt(sp_blocks, sp_tokens, float(b * P), sp_blocks, ALU.is_gt, ADD))
                old, new, by = sp_blocks, sp_sum1, 1
                while by < EXPERTS:
                    v.tensor_copy(new[:, 0:by], old[:, 0:by])
                    link(tt(new[:, by:], old[:, by:], old[:, 0:EXPERTS - by], ADD))
                    old, new, by = new, (sp_sum0 if new is sp_sum1 else sp_sum1), 2 * by
                assert old is sp_sum0
                v.memset(sp_ones, 1.0)
                v.tensor_copy(spare_int[:, 4:5], old[:, EXPERTS - 1:EXPERTS]).then_inc(spares_counted, 1)
                vals = sp_col[:, 16:24].rearrange("p (a b) -> p a b", a=4)
                for tb in range(nb):
                    link(ts(vals[:, tb, 0:1], V("slot", 0), float(tb * P - FAR), None, ADD))

            def moe(l):
                nb = 4 - 2 * l
                cols = nb * P
                route(l, nb)
                head, ph = PLAN["moe_head", l], PLAN["moe", l]
                dve.wait_ge(slot_consts, l + 1)
                weight_parts(nb)
                b = wait_filled(dve, head, 2 * nb + 4)
                stt(rank[:, 0:nb, :], ps[:, b, 0:nb * EXPERTS].rearrange("p (a e) -> p a e", a=nb), 1.0, e_sel[:, 0:nb, :], ADD, MUL)
                v.tensor_copy(sp_tokens, ps[:, b, nb * EXPERTS:(nb + 1) * EXPERTS]).then_inc(drained[b], 1)
                wait_drained(dve, head, 2 * nb + 4)

                def one_hot(turn, k):
                    if lacks(turn, k):
                        return
                    e = expert(turn, k)
                    if not isinstance(e, int) or e >= 2:
                        wait_filled(dve, ph, SLOT, e - 2)
                    for tb in range(nb):
                        last = ts(onehot[:, k % 2, tb, :], count1, rank[:, tb, bass.ds(e, 1)], None, ALU.is_equal)
                    last.then_inc(onehot_ready, 1)

                def records(turn, k):
                    if lacks(turn, k):
                        return
                    e = expert(turn, k)
                    b = wait_filled(dve, ph, SLOT, e)
                    k8 = slice(k % TURN, k % TURN + 1)
                    wait_past(dve, scattered, turn * (16 * TURN) + 16 * (EXPERTS * l + k - 7))
                    v.tensor_reduce(slot_rec[:, k % TURN, :], ps[:, b, 0:6].rearrange("p (a n) -> p a n", a=2), AX.X, ADD)\
                        .then_inc(slot_part, 1)
                    dve.wait_ge(slot_part, e + (EXPERTS * l + 1))
                    stt(slot_row[:, k8], slot_rec[:, k % TURN, 0:1], float(FAR), V("slot", 1 + l), ADD, ALU.min).then_inc(drained[b], 1)

                def rows_turned(turn, k):
                    if not lacks(turn, k):
                        e = expert(turn, k)
                        b = wait_filled(dve, ph, ROWS_T + 1, e)
                        v.tensor_copy(e_xt[:, k % 2, 4:8, :], ps[:, b, :].rearrange("p (c t) -> p c t", c=4)).then_inc(drained[b], 1)

                def gated(turn, k):
                    if lacks(turn, k):
                        return
                    e = expert(turn, k)
                    dve.wait_ge(expert_silu, e + (EXPERTS * l + 1))
                    b = wait_filled(dve, ph, HIDDEN, e)
                    tt(e_h[:, k % 2, :], e_g[:, k % 2, :], ps[:, b, EXP_D:2 * EXP_D], MUL).then_inc(drained[b], 1)

                one_hot(0, 0)
                one_hot(0, 1)
                for i in range(2):
                    wait_drained(dve, head, 2 * nb + i)
                    b = wait_filled(dve, head, 2 * nb + 2 + i)
                    tt(sh_h[:, i, 0:cols], sh_g[:, i, 0:cols], ps[:, b, 0:cols], MUL).then_inc(drained[b], 1)
                for k in range(4):
                    records(0, k)
                    if k < 3:
                        one_hot(0, k + 2)
                count_spares(l, nb)
                rows_turned(0, 0)
                rows_turned(0, 1)
                gated(0, 0)

                def step(turn, k):
                    e = expert(turn, k)
                    rows_turned(turn, k + 2)
                    records(turn, k + 4)
                    one_hot(turn, k + 5)
                    gated(turn, k + 1)
                    b = wait_filled(dve, ph, OUTPUT + 1, e)
                    wait_drained(dve, ph, SLOT, e)
                    wait_past(dve, scattered, turn * (16 * TURN) + 16 * (EXPERTS * l + k - 1))
                    ts(e_y[:, k % 2, 512:D], ps[:, b, :], slot_rec[:, k, 1:2], None, MUL).then_inc(drained[b], 1)
                expert_turns(dve, l, step)

                def spare_block(i):
                    count = [0]

                    def then(ins):
                        count[0] += 1
                        ins.then_inc(spare["step"][l], 1)
                        dve.wait_ge(spare["step"][l], i * steps + count[0])

                    steps = 10 + 3 * nb
                    first = PLAN["moe", l].first
                    at_e, before, shift = (sp_col[:, n:n + 1] for n in (2, 3, 4))
                    record, places, pieces_ = sp_col[:, 0:2], sp_col[:, 8:8 + nb], sp_col[:, 12:15]
                    vals = sp_col[:, 16:24].rearrange("p (a b) -> p a b", a=4)
                    this = count1[:, bass.ds(i, 1)]
                    then(stt(sp_mask, sp_sum0, this, sp_ones, ALU.is_lt, MUL, accum_out=at_e))
                    then(stt(sp_rest, sp_sum0, this, sp_blocks, ALU.is_lt, MUL, accum_out=before))
                    ts(pieces_[:, 0:1], at_e, 3.0, -1.0, MUL, ADD)
                    ts(pieces_[:, 1:2], at_e, 3.0, 1.0, MUL, ALU.max)
                    then(ts(pieces_[:, 2:3], at_e, 3.0, 4.0, MUL, ADD))
                    then(ts(pieces_, pieces_, 0.0, float(3 * EXPERTS - 1), ALU.max, ALU.min))
                    then(ts(pieces_, pieces_, float(P), float(first * P), MUL, ADD))
                    ts(spare_int[:, 0:3], pieces_, V("slot", 0), None, ADD).then_inc(spare["picked"][l], 1)
                    then(tt(shift, before, this, SUB))
                    then(ts(shift, shift, float(P), None, MUL))
                    then(ts(at_e, at_e, 1.0, None, ADD))
                    then(ts(sp_mask, count1[:, 0:EXPERTS], at_e, None, ALU.is_equal))
                    for tb in range(nb):
                        then(stt(sp_rest, rank[:, tb, :], 1.0, sp_mask, MUL, MUL, accum_out=places[:, tb:tb + 1]))
                        then(stt(sp_rest, wts[:, tb, :], 1.0, sp_mask, MUL, MUL, accum_out=vals[:, tb, 1:2]))
                    then(ts(places, places, shift, None, ADD))
                    for tb in range(nb):
                        last = ts(sp_hot[:, tb, :], count1, places[:, tb:tb + 1], None, ALU.is_equal)
                        if tb < nb - 1:
                            then(last)
                    last.then_inc(spare["onehot"][l], 1)
                    dve.wait_ge(spare["slots"][l], i + 1)
                    dve.wait_ge(spare["added"][l], i * 16)
                    then(v.tensor_copy(record, ps[:, 2, 0:2]))
                    assert count[0] == steps, (count[0], steps)
                    stt(spare_int[:, 3:4], record[:, 0:1], float(FAR), V("slot", 1 + l), ADD, ALU.min).then_inc(spare["recorded"][l], 1)
                    dve.wait_ge(spare["rows_t"][l], i + 1)
                    v.tensor_copy(e_xt[:, 0, 4:8, :], ps[:, 1, :].rearrange("p (c t) -> p c t", c=4)).then_inc(spare["x_t"][l], 1)
                    dve.wait_ge(spare["silu"][l], i + 1)
                    tt(e_h[:, 0, :], e_g[:, 0, :], ps[:, 4, EXP_D:2 * EXP_D], MUL).then_inc(spare["gated"][l], 1)
                    dve.wait_ge(spare["output"][l], i + 1)
                    dve.wait_ge(spare["scaled"][l], i * 2 + 1)
                    ts(e_y[:, 0, 512:D], ps[:, 7, :], record[:, 1:2], None, MUL).then_inc(spare["scaled"][l], 1)
                spare_turns(dve, l, spare_block)

            dve.wait_ge(consts_loaded, 48)
            rope_tables(0)
            first_mods()
            for l in range(DEPTH):
                mods(l, (0, 1) if l else (0,))
                pre_norm(2 * l)
                (mla, stick, retention)[l % 3](l)
                post_norm(2 * l, PLAN["mix_out", l])
                pre_norm(2 * l + 1)
                ffn(l)
                post_norm(2 * l + 1, PLAN["ffn_down", l])
            for l in range(DEPTH_2):
                cols = TC if l == 0 else T
                mods2(l)
                modulate(2 * l)
                (fourier_gqa, neighbours)[l]()
                layer_norm(2 * l, cols, PLAN["out2", l])
                modulate(2 * l + 1)
                moe(l)
                layer_norm(2 * l + 1, cols, PLAN["moe_turn", l])

        @block.gpsimd
        def _(pool):
            link = chained(pool, pool_step)
            g = nc.gpsimd
            MUL, ADD, SUB = ALU.mult, ALU.add, ALU.subtract
            g.memset(zeros[:], 0.0).then_inc(zeros_set, 1)

            def post_norm(s):
                pool.wait_ge(*((x_ready, 4 * s) if s else (x_loaded, 16)))
                for c in range(4):
                    pool.wait_ge(y_scaled, 8 * s + c + 1)
                    g.tensor_tensor(X[:, c, 0:T], X[:, c, 0:T], Y[:, c, :], ADD).then_inc(x_ready, 1)

            def mod_loads(key):
                m = MOD_PLAN[key]

                def body(turn):
                    for i in range(len(m["jobs"])):
                        for half in range(2):
                            n = mod_steps(key, i, turn) + (half * m["steps"][i] // 2 - 4)
                            if not isinstance(n, int) or n > 0:
                                pool.wait_ge(mod_step, n)
                            p = turn * (2 * len(m["jobs"])) + (m["piece"] + 2 * i + half)
                            src = mod_stream[p] if isinstance(p, int) else mod_stream[bass.ds(p, 1)].rearrange("a p n -> p (a n)")
                            pool.dma_start(mod_w[:, half, :, :], src.rearrange("p (c n) -> p c n", c=4)).then_inc(mod_full[half], 16)
                with pool.Fori(0, m["turns"]) as turn:
                    body(turn)

            def attention(l):
                for i, unit in enumerate(attention_units(l)):
                    U, nk = UNIT0[l] + i, unit["nk"]
                    pool.wait_ge(att_rinv, U + 1)
                    g.tensor_scalar(att_p[:, i % 4, 0:nk], att_p[:, i % 4, 0:nk], att_stat[:, 2, U:U + 1], None, MUL)\
                        .then_inc(att_prob, 1)

            def mla(l):
                ph = PLAN["mla_up", l]
                pool.wait_ge(rope_ready, 2)
                cos = rope[:, 0, :]
                for k in range(2):
                    wait_drained(pool, ph, 14 + k)
                    for c in (2 * k, 2 * k + 1):
                        link(g.tensor_tensor(m_qp[:, c, :], m_qp[:, c, :], cos, MUL))
                    q = m_qp[:, 2 * k:2 * k + 2, :]
                    g.tensor_tensor(q, q, m_t2[:, 2 * k:2 * k + 2, :], ADD).then_inc(mla_rope, 1)
                attention(l)

            def stick(l):
                s, n, _ = PLAN["sb_in", l].piece(12)
                pool.wait_ge(piece_full[s], 16 * n)
                mask, guard = ring[:, s, 2 * P:2 * P + 384], ring[:, s, 2 * P + 384:2 * P + 768]
                for i in range(SB_H + 2):
                    if i < SB_H:
                        pool.wait_ge(sb_soft, i + 1)
                        g.tensor_tensor(s_sp[:, i % 4, :], s_sp[:, i % 4, :], mask, MUL).then_inc(sb_masked, 1)
                    if i >= 2:
                        u = i - 2
                        wait_drained(pool, PLAN["sb", l], 5 * (u // 2) + 2 * (u % 2) + 1)
                        g.tensor_tensor(s_d[:, u % 4, :], s_d[:, u % 4, :], guard, ADD).then_inc(sb_guarded, 1)

            def retention(l):
                ph = PLAN["ret_in", l]
                for k in range(8):
                    wait_drained(pool, ph, k)
                    dst = r_q if k < RET_H else r_k
                    h = k % RET_H
                    g.tensor_tensor(dst[:, 2 * h, :], r_ta[:, k % 2, 0, :], r_tb[:, k % 2, 1, :], SUB)
                    g.tensor_tensor(dst[:, 2 * h + 1, :], r_ta[:, k % 2, 1, :], r_tb[:, k % 2, 0, :], ADD).then_inc(ret_roped, 1)
                for h in range(RET_H):
                    pool.wait_ge(ret_normed, 4 * h + 4)
                    at = slice(4 * h, 4 * h + 4)
                    g.tensor_tensor(r_o[:, at, :], r_o[:, at, :], r_g[:, at, :], MUL).then_inc(ret_gated, 1)

            def modulate(n):
                l, i = n // 2, n % 2
                cols = TC if l == 0 else T
                pool.wait_ge(mod_ready, DEPTH + l + 2)
                pool.wait_ge(*((ln_ready, 8 * n) if n else (ctx_loaded, 16)))
                if n < 3:
                    for c in range(DC):
                        shift = 3 * i * DC + c
                        g.tensor_scalar(H[:, c, T:TC], X[:, c, T:TC], scale2[:, l, i, c, 1:2], mod2[:, l, shift, 1:2], MUL, ADD)\
                            .then_inc(hm_pool, 1)
                    pool.wait_ge(hm_pool, 8 * n + 8)
                for c in range(DC):
                    pool.wait_ge(hm_dve, 8 * n + c + 1)
                    g.tensor_scalar(X[:, c, 0:cols], X[:, c, 0:cols], DN_ALPHA, None, MUL).then_inc(x_alpha, 1)

            def layer_norm(m, cols):
                wait_drained(pool, PLAN["ln", m], 0)
                for c in range(1, DC, 2):
                    g.tensor_tensor(X[:, c, 0:cols], X[:, c, 0:cols], MU[:, 0:cols], SUB).then_inc(xc_pool, 1)

            def fourier_gqa():
                for c in range(8):
                    wait_drained(pool, PLAN["ab_in", 0], 20 + c)
                    q = a_q[:, c, 0:T] if c < GQ_H else a_k[:, c - GQ_H, 0:T]
                    link(g.tensor_tensor(q, q, ax_cos, MUL))
                    g.tensor_tensor(q, q, a_t[:, c % 2, :], ADD).then_inc(ab_roped, 1)
                attention(4)

            def moe(l):
                nb = 4 - 2 * l
                cols = nb * P
                head, ph = PLAN["moe_head", l], PLAN["moe", l]
                h2, ff = h2_d[l], ff_d[l]
                vals = slot_vals[:, :, :].rearrange("p a (e v) -> p a e v", v=6)
                link(g.memset(vals[:, 0:nb, :, 0], 1.0))
                link(g.tensor_scalar(vals[:, 0:nb, :, 0], vals[:, 0:nb, :, 0], V("slot", 0), None, MUL))
                for tb in range(nb):
                    link(g.memset(vals[:, tb, :, 1], float(tb * P - FAR)))
                g.memset(vals[:, 0:nb, :, 2], 0.0).then_inc(slot_consts, 1)
                for half in range(2):
                    pool.dma_start(h2[cols:cols + P, half * 512:(half + 1) * 512], zeros[:, 0:512]).then_inc(h2_stored, 16)
                    pool.dma_start(ff[cols:cols + P, half * 512:(half + 1) * 512], zeros[:, 0:512]).then_inc(ff_set, 16)
                for i in range(2 * nb):
                    wait_drained(pool, head, i)
                pool.dma_start(h2[0:cols].rearrange("(a p) n -> p a n", p=P), h2_rows[:, 0:nb, :]).then_inc(h2_stored, 16)
                pool.wait_ge(h2_stored, 48 * (l + 1))

                def gather(turn, k):
                    if lacks(turn, k):
                        return
                    e = expert(turn, k)
                    wait_drained(pool, ph, SLOT, e)
                    if not isinstance(e, int) or e >= 2:
                        wait_filled(pool, ph, ROWS_T + 1, e - 2)
                    k8 = slice(k % TURN, k % TURN + 1)
                    pool.sem_inc(rows_due, 1)
                    pool.indirect_dma_start(e_x[:, k % 2, :], None, h2, bass.IndirectOffsetOnAxis(slot_row[:, k8], 0))\
                        .then_inc(gathered[k % 2], 16)

                gather(0, 0)
                gather(0, 1)
                for i in range(2 * nb):
                    wait_drained(pool, head, 2 * nb + 5 + i)
                pool.dma_start(ff[0:cols].rearrange("(a p) n -> p a n", p=P), e_acc[:, 0:nb, :]).then_inc(ff_set, 16)
                gather(0, 2)
                gather(0, 3)
                pool.wait_ge(ff_set, 48 * (l + 1))

                def step(turn, k):
                    e = expert(turn, k)
                    gather(turn, k + 4)
                    for half in range(2):
                        wait_drained(pool, ph, OUTPUT + half, e)
                    wait_past(pool, scattered, turn * (16 * TURN) + 16 * (EXPERTS * l + k))
                    pool.sem_inc(sum_due, 1)
                    pool.indirect_dma_start(ff, bass.IndirectOffsetOnAxis(slot_row[:, k:k + 1], 0), e_y[:, k % 2, :], None,
                                            compute_op=ADD).then_inc(scattered, 16)
                expert_turns(pool, l, step)
                pool.wait_ge(scattered, 16 * EXPERTS * (l + 1))

                def spare_block(i):
                    pool.wait_ge(spare["picked"][l], i + 1)
                    pool.sem_inc(rows_due, 1)
                    for n in range(3):
                        pool.indirect_dma_start(sp_w[:, n, :], None, stream.rearrange("s p n -> (s p) n"),
                                                bass.IndirectOffsetOnAxis(spare_int[:, n:n + 1], 0)).then_inc(spare["weights"][l], 16)
                    pool.wait_ge(spare["recorded"][l], i + 1)
                    pool.sem_inc(rows_due, 1)
                    pool.indirect_dma_start(e_x[:, 0, :], None, h2, bass.IndirectOffsetOnAxis(spare_int[:, 3:4], 0))\
                        .then_inc(spare["rows"][l], 16)
                    pool.wait_ge(spare["scaled"][l], i * 2 + 2)
                    pool.sem_inc(sum_due, 1)
                    pool.indirect_dma_start(ff, bass.IndirectOffsetOnAxis(spare_int[:, 3:4], 0), e_y[:, 0, :], None,
                                            compute_op=ADD).then_inc(spare["added"][l], 16)
                    pool.wait_ge(spare["added"][l], i * 16 + 16)
                spare_turns(pool, l, spare_block)
                pool.dma_start(e_acc[:, 0:nb, :], ff[0:cols].rearrange("(a p) n -> p a n", p=P)).then_inc(ff_loaded, 16)

            for l in range(DEPTH):
                if l % 3 == 0:
                    mla(l)
                elif l % 3 == 1:
                    stick(l)
                else:
                    retention(l)
                post_norm(2 * l)
                mod_loads(("up", l))
                mod_loads(("down", l))
                post_norm(2 * l + 1)
            for l in range(DEPTH_2):
                cols = TC if l == 0 else T
                modulate(2 * l)
                if l == 0:
                    fourier_gqa()
                else:
                    attention(5)
                layer_norm(2 * l, cols)
                modulate(2 * l + 1)
                moe(l)
                layer_norm(2 * l + 1, cols)


def columns(a):
    return np.asarray(a).reshape(-1, P).T


def chunked(w):
    w = np.asarray(w)
    return w.reshape(-1, P, w.shape[1]).transpose(1, 0, 2)


def by_columns(w, n):
    c = chunked(w)
    return [c[:, :, i:i + n].reshape(P, -1) for i in range(0, c.shape[2], n)]


def shape_constants():
    f64 = np.float64
    k, q = np.arange(P)[:, None], np.arange(P)[None, :]
    rot = np.zeros((P, P))
    for m in range(P):
        rot[(m + 32, m) if m % 64 < 32 else (m - 32, m)] = -1.0 if m % 64 < 32 else 1.0
    t = np.arange(T)
    inv = 10000.0 ** (-(2.0 / 64) * (np.arange(P) % 32))
    ang = (np.where(np.arange(P)[:, None] < 64, t // GRID_W, t % GRID_W).astype(np.float32)
           * inv.astype(np.float32)[:, None]).astype(f64)
    before = (k < q).astype(f64)
    tab = np.concatenate([np.eye(P), np.full((P, P), 1.0 / D), rot, np.cos(ang), np.sin(ang), before, np.ones((P, P)),
                          np.broadcast_to(1.0 + q, (P, P))], 1)
    p = np.arange(P)
    slot = np.stack([p, TC + p, T + p], 1)
    inv_freq = np.stack([10000.0 ** (-(2.0 * (np.arange(P) % 32)) / MLA_ROPE), 10000.0 ** (-(2.0 * np.arange(P)) / RET_K)], 1)
    parity = np.stack([np.arange(P) < 64, np.arange(P) >= 64], 1)
    causal = np.where(q <= k, 0.0, NEG)
    mla_mask = np.concatenate([causal, np.zeros((P, P)), causal], 1)
    strict = (k < q).astype(f64)
    sb_mask = np.concatenate([strict, np.ones((P, P)), strict], 1)
    sb = np.concatenate([(k >= q).astype(f64), np.ones((P, P)), sb_mask, (sb_mask - 1.0) * -NEG], 1)
    decay = []
    for h in range(RET_H):
        log_gamma = np.log(1.0 - 2.0 ** (-5.0 - h))
        near = np.where(q >= k, np.exp(np.maximum(q - k, 0) * log_gamma), 0.0) * RET_K ** -0.5
        far = np.exp((q + P - k) * log_gamma) * RET_K ** -0.5
        decay += [near, far, near]
    n = np.arange(T)
    tok = 2 * np.pi * np.outer(n, n) / T
    ch = 2 * np.pi * np.outer(np.arange(64), np.arange(64)) / 64
    norm = 1.0 / np.sqrt(T * 64.0)
    two = np.eye(2)
    dft = np.concatenate([chunked(np.cos(tok)).reshape(P, -1), chunked(np.sin(tok)).reshape(P, -1),
                          np.kron(two, np.cos(ch) * norm), np.kron(two, -np.sin(ch) * norm)], 1)
    col = np.arange(GRID_W)
    start = np.clip(col - NA_KW // 2, 0, GRID_W - NA_KW)
    inside = (col[None, :] >= start[:, None]) & (col[None, :] < start[:, None] + NA_KW)
    window = np.where(np.tile(inside, (T // GRID_W, T // GRID_W)), 0.0, NEG)
    row = np.arange(T) // GRID_W
    cc = np.arange(T) % GRID_W
    dr = np.clip(row[None, :] - row[:, None] + 7, 0, 14)
    dc = np.clip(cc[None, :] - cc[:, None] + NA_KW - 1, 0, 2 * NA_KW - 2)
    f = np.float32
    return dict(tab=tab.astype(f), slot=slot.astype(f), inv_freq=inv_freq.astype(f), parity=parity.astype(f), mla_mask=mla_mask.astype(f),
                sb=sb.astype(f), decay=np.concatenate(decay, 1).astype(f), dft=dft.astype(f),
                window=chunked(window.astype(f)).reshape(P, -1), dr=dr, dc=dc)


def pieces_of(inp, con):
    def experts(l):
        gate, up, down = (inp[n][l] for n in ("moe_w_gate_2", "moe_w_up_2", "moe_w_down_2"))

        def gate_up(g, u):
            both = np.concatenate([chunked(g), chunked(u)], 2)
            yield both[:, 0:4].reshape(P, -1)
            yield both[:, 4:8].reshape(P, -1)
        yield from gate_up(inp["sh_w_gate_2"][l], inp["sh_w_up_2"][l])
        yield chunked(inp["sh_w_down_2"][l]).reshape(P, -1)
        yield from gate_up(gate[0], up[0])
        for e in range(EXPERTS):
            if e < EXPERTS - 1:
                yield from gate_up(gate[e + 1], up[e + 1])
            yield chunked(down[e]).reshape(P, -1)

    for l in range(DEPTH):
        j = l // 3
        if l % 3 == 0:
            w = inp["mla_w_in"][j]
            yield from by_columns(np.concatenate([w, w[:, 384:448]], 1), 256)
            up = inp["mla_w_q_up"][j].reshape(256, MLA_H, MLA_NOPE + MLA_ROPE)
            yield chunked(up[:, :, 0:MLA_NOPE].reshape(256, -1)).reshape(P, -1)
            up_kv = inp["mla_w_kv_up"][j].reshape(P, MLA_H, 2, MLA_V)
            yield up_kv.transpose(0, 2, 1, 3).reshape(P, -1)
            pe = chunked(up[:, :, MLA_NOPE:].reshape(256, -1)).reshape(P, -1)
            yield np.concatenate([pe, np.zeros((P, P), np.float32), con["mla_mask"]], 1)
            yield from by_columns(inp["mla_w_out"][j], 256)
        elif l % 3 == 1:
            yield from by_columns(inp["sb_w_in"][j], 256)
            yield con["sb"]
            yield from by_columns(inp["sb_w_out"][j], 256)
        else:
            yield from by_columns(inp["ret_w_in"][j], 256)
            yield con["decay"]
            yield from by_columns(inp["ret_w_out"][j], P)
        yield from by_columns(inp["ffn_w1"][l], 256)
        for m in by_columns(inp["ffn_w2"][l], P):
            yield m[:, 0:PIECE]
            yield m[:, PIECE:]
    for l in range(DEPTH_2):
        if l == 0:
            yield from by_columns(inp["ab_w_in_2"][0], 256)
            fnet = inp["ab_w_fnet_2"][0]
            blocks = np.zeros((P, 2, P), np.float32)
            for g in range(4):
                blocks[(g % 2) * 64:(g % 2 + 1) * 64, g // 2, (g % 2) * 64:(g % 2 + 1) * 64] = fnet[g]
            yield np.concatenate([con["dft"], blocks.reshape(P, -1)], 1)
            yield from by_columns(inp["ab_w_out_2"][0], 256)
        else:
            yield from by_columns(inp["na_w_in_2"][0], 256)
            bias = inp["na_rpb_2"][0][:, con["dr"], con["dc"]]
            for qb in range(2):
                yield bias[:, qb * P:(qb + 1) * P, :].transpose(1, 0, 2).reshape(P, -1)
            yield con["window"]
            yield from by_columns(inp["na_w_out_2"][0], 256)
        yield chunked(inp["moe_w_router_2"][l]).reshape(P, -1)
        yield from experts(l)


def mod_pieces_of(inp):
    tables = {"mod": inp["ada_w"], "mod2": inp["w_mod_2"]}
    for m in MOD_PLAN.values():
        for turn in range(m["turns"]):
            for (table, l), (first, per_turn) in zip(m["jobs"], m["blocks"]):
                at = (first + turn * per_turn) * TC
                block = chunked(tables[table][l][:, at:at + TC])
                yield block[:, 0:4].reshape(P, -1)
                yield block[:, 4:8].reshape(P, -1)


def kernel(**inputs):
    import concourse.bacc as bacc
    from concourse.bass_utils import run_bass_kernel_spmd

    inp = {k: np.asarray(a) for k, a in inputs.items()}
    con = shape_constants()
    stream = np.zeros((STREAM, P, PIECE), np.float32)
    n = 0
    for piece in pieces_of(inp, con):
        stream[n, :, 0:piece.shape[1]] = piece
        n += 1
    assert n == PIECES, (n, PIECES)
    mod_stream = np.stack(list(mod_pieces_of(inp)))
    assert len(mod_stream) == MOD_PIECES
    vec = np.zeros((P, NVEC), np.float32)
    conds = np.stack([columns(inp["c"][0]), columns(inp["c_2"][0]), columns(inp["c_ctx_2"])], 2)
    ln = [inp[k][l] for l in range(DEPTH_2) for k in ("ln1_g_2", "ln1_b_2", "ln2_g_2", "ln2_b_2")]
    for name, a in (
        ("ada_b", columns(inp["ada_b"])), ("norm_g", columns(inp["norm_g"])), ("b_mod", columns(inp["b_mod_2"])),
        ("ln", columns(np.stack(ln))), ("q_norm", columns(inp["mla_q_norm"])), ("kv_norm", columns(inp["mla_kv_norm"])),
        ("gn_g", columns(inp["ret_gn_g"])), ("qk_gain", columns(np.stack([inp["ab_q_norm_2"][0], inp["ab_k_norm_2"][0]]))),
        ("conds", conds.reshape(P, -1)), ("e_bias", np.broadcast_to(inp["moe_bias_2"].reshape(1, -1), (P, DEPTH_2 * EXPERTS))),
        ("inv_freq", con["inv_freq"]), ("parity", con["parity"]), ("eps", np.full((P, 1), EPS, np.float32)),
        ("slot", con["slot"]),
    ):
        vec[:, VEC[name][0]:VEC[name][1]] = a
    arrays = {
        "stream": stream, "mod_stream": mod_stream, "vectors": vec, "tables": con["tab"],
        "latent": np.ascontiguousarray(inp["x"][0].reshape(T, DC, P).transpose(2, 1, 0)),
        "context": np.ascontiguousarray(inp["ctx_2"][0].reshape(T, DC, P).transpose(2, 1, 0)),
        "positions": np.ascontiguousarray(np.broadcast_to(inp["positions"][0], (P, T))),
    }
    nc = bacc.Bacc("TRN2", target_bir_lowering=False, num_devices=1)
    args = [nc.dram_tensor(k + "_in", a.shape, mybir.dt.from_np(a.dtype), kind="ExternalInput").ap() for k, a in arrays.items()]
    out = nc.dram_tensor("out", (P, DC, T), F32, kind="ExternalOutput").ap()
    by_tokens = [[nc.dram_tensor(f"{n}{l}", (rows + P, D), F32).ap() for l, rows in enumerate((TC, T))] for n in ("moe_in", "moe_out")]
    build(nc, *args, out, *by_tokens)
    r = run_bass_kernel_spmd(nc, [{k + "_in": a for k, a in arrays.items()}], core_ids=[0])
    got = r.results[0]["out"]
    return np.ascontiguousarray(got.transpose(2, 1, 0).reshape(1, T, D))
```
